# Optimizing a Trainium2 kernel written in Bass

```python
import jax
import jax.numpy as jnp
from jax import lax
import numpy as np

D_MODEL = 1024
BATCH = 1
SEQ = 512
DEPTH = 2

CTX_LEN = 256
GRID_W = 64
Q_BLOCK = 128
RET_CHUNK = 128
ROPE_BASE = 10000.0
NORM_EPS = 1e-6
N_MOD = 6

RET_HEADS = 4
RET_DK = 128
RET_DV = 256
RET_DECAY_START = 5.0
RET_BWD_OFFSET = 0.5

MLA_HEADS = 8
MLA_Q_RANK = 256
MLA_KV_RANK = 256
MLA_NOPE = 64
MLA_ROPE = 32
MLA_V = 128

GQA_HEADS = 8
GQA_KV_HEADS = 2
GQA_HD = 128

FFN_HIDDEN = ((8 * D_MODEL + 3 * 256 - 1) // (3 * 256)) * 256

RET_W = RET_HEADS * RET_DV
MLA_W = MLA_HEADS * MLA_V
GQA_W = GQA_HEADS * GQA_HD
N_BRANCH = 3

IN_SIZES = (
    RET_HEADS * RET_DK,
    RET_HEADS * RET_DK,
    RET_W,
    RET_W,
    MLA_Q_RANK,
    MLA_KV_RANK,
    MLA_ROPE,
    GQA_W,
    GQA_KV_HEADS * GQA_HD,
    GQA_KV_HEADS * GQA_HD,
    N_BRANCH * D_MODEL,
)
IN_DIM = sum(IN_SIZES)

kernel_name = 'hybrid_ret_mla_gqa_dit_trunk'

def rms_norm(x, g=None):
    xf = x.astype(jnp.float32)
    y = xf * lax.rsqrt(jnp.mean(xf * xf, axis=-1, keepdims=True) + NORM_EPS)
    if g is not None:
        y = y * g.astype(jnp.float32)
    return y.astype(x.dtype)

def modulate(x, shift, scale):
    return x * (1 + scale) + shift

def axis_angles(pos, dim):
    half = dim // 2
    inv_freq = ROPE_BASE ** (-jnp.arange(half, dtype=jnp.float32) / half)
    ang = pos.astype(jnp.float32)[:, None] * inv_freq[None, :]
    return jnp.cos(ang), jnp.sin(ang)

def rope_tables(rows, cols, dim):
    cr, sr = axis_angles(rows, dim // 2)
    cc, sc = axis_angles(cols, dim // 2)
    return (cr, sr, cc, sc)

def rotate_half(x, cos, sin):
    x1, x2 = jnp.split(x, 2, axis=-1)
    cos = cos[:, None, :]
    sin = sin[:, None, :]
    return jnp.concatenate([x1 * cos - x2 * sin, x2 * cos + x1 * sin], axis=-1)

def rope_2d(x, tabs):
    if tabs is None:
        return x
    cr, sr, cc, sc = tabs
    xr, xc = jnp.split(x.astype(jnp.float32), 2, axis=-1)
    out = jnp.concatenate([rotate_half(xr, cr, sr), rotate_half(xc, cc, sc)], axis=-1)
    return out.astype(x.dtype)

def retention_log_decay(offset):
    h = jnp.arange(RET_HEADS, dtype=jnp.float32)
    return jnp.log1p(-jnp.exp2(-(RET_DECAY_START + offset) - h))

def retention_scan(q, k, v, log_gamma, state0):
    B, T, H, dk = q.shape
    dv = v.shape[-1]
    C = RET_CHUNK
    n = T // C
    qc = q.astype(jnp.float32).reshape(B, n, C, H, dk)
    kc = k.astype(jnp.float32).reshape(B, n, C, H, dk)
    vc = v.astype(jnp.float32).reshape(B, n, C, H, dv)
    pos = jnp.arange(C, dtype=jnp.float32)
    diff = pos[:, None] - pos[None, :]
    lower = diff >= 0
    decay = jnp.where(lower[None],
                      jnp.exp(log_gamma[:, None, None] * jnp.where(lower, diff, 0.0)[None]),
                      0.0)
    scores = jnp.einsum('bnihd,bnjhd->bnhij', qc, kc) * decay
    inner = jnp.einsum('bnhij,bnjhe->bnihe', scores, vc)
    zeta = jnp.exp(log_gamma[:, None] * (C - 1 - pos)[None, :])
    upd = jnp.einsum('bnjhd,bnjhe,hj->nbhde', kc, vc, zeta)
    chunk_decay = jnp.exp(log_gamma * C)[None, :, None, None]

    def step(s, u):
        return chunk_decay * s + u, s

    s_final, s_prev = lax.scan(step, state0, upd)
    xi = jnp.exp(log_gamma[:, None] * (pos + 1)[None, :])
    cross = jnp.einsum('bnihd,nbhde,hi->bnihe', qc, s_prev, xi)
    return (inner + cross).reshape(B, T, H, dv), s_final

def retention_readout(y, g):
    B, T = y.shape[:2]
    y = rms_norm(y).reshape(B, T, RET_W)
    return (jax.nn.silu(g.astype(jnp.float32)) * y).astype(g.dtype)

def retention_branch(fl, fc, need_ctx):
    lg_f = retention_log_decay(0.0)
    lg_b = retention_log_decay(RET_BWD_OFFSET)
    B = fl['ret_q'].shape[0]
    zero = jnp.zeros((B, RET_HEADS, RET_DK, RET_DV), jnp.float32)
    rev = lambda a: a[:, ::-1]
    qc, kc, vc = fc['ret_q'], fc['ret_k'], fc['ret_v']
    q, k, v = fl['ret_q'], fl['ret_k'], fl['ret_v']
    yc_f, s_f = retention_scan(qc, kc, vc, lg_f, zero)
    yc_b, s_b = retention_scan(rev(qc), rev(kc), rev(vc), lg_b, zero)
    y_f, _ = retention_scan(q, k, v, lg_f, s_f)
    y_b, _ = retention_scan(rev(q), rev(k), rev(v), lg_b, s_b)
    y = retention_readout(y_f + rev(y_b), fl['ret_g'])
    yc = retention_readout(yc_f + rev(yc_b), fc['ret_g']) if need_ctx else None
    return y, yc

def mixer_features(p, g_mla_q, g_mla_kv, w_mla_qb, w_mla_kvb, g_gqa_q, g_gqa_k,
                   tabs_ret, tabs_mla, tabs_gqa):
    B, T, _ = p.shape
    split_at = np.cumsum(IN_SIZES)[:-1].tolist()
    (rq, rk, rv, rg, cq, ckv, kr, gq, gk, gv, gates) = jnp.split(p, split_at, axis=-1)
    f = {}
    f['ret_q'] = rope_2d(rq.reshape(B, T, RET_HEADS, RET_DK), tabs_ret)
    f['ret_k'] = rope_2d(rk.reshape(B, T, RET_HEADS, RET_DK), tabs_ret) * (RET_DK ** -0.5)
    f['ret_v'] = rv.reshape(B, T, RET_HEADS, RET_DV)
    f['ret_g'] = rg
    qh = (rms_norm(cq, g_mla_q) @ w_mla_qb).reshape(B, T, MLA_HEADS, MLA_NOPE + MLA_ROPE)
    q_nope, q_pe = jnp.split(qh, [MLA_NOPE], axis=-1)
    kvh = (rms_norm(ckv, g_mla_kv) @ w_mla_kvb).reshape(B, T, MLA_HEADS, MLA_NOPE + MLA_V)
    k_nope, f['mla_v'] = jnp.split(kvh, [MLA_NOPE], axis=-1)
    k_pe = jnp.broadcast_to(rope_2d(kr[:, :, None, :], tabs_mla), (B, T, MLA_HEADS, MLA_ROPE))
    f['mla_q'] = jnp.concatenate([q_nope, rope_2d(q_pe, tabs_mla)], axis=-1)
    f['mla_k'] = jnp.concatenate([k_nope, k_pe], axis=-1)
    f['gqa_q'] = rope_2d(rms_norm(gq.reshape(B, T, GQA_HEADS, GQA_HD), g_gqa_q), tabs_gqa)
    f['gqa_k'] = rope_2d(rms_norm(gk.reshape(B, T, GQA_KV_HEADS, GQA_HD), g_gqa_k), tabs_gqa)
    f['gqa_v'] = gv.reshape(B, T, GQA_KV_HEADS, GQA_HD)
    f['gates'] = gates.reshape(B, T, N_BRANCH, D_MODEL)
    return f

def block_attention(q, k, v, scale):
    B, L, Hk, G, d = q.shape
    e = v.shape[-1]
    nb = L // Q_BLOCK
    kf = k.astype(jnp.float32)
    vf = v.astype(jnp.float32)
    qb = jnp.moveaxis(q.reshape(B, nb, Q_BLOCK, Hk, G, d), 1, 0)

    def one_block(qblk):
        s = jnp.einsum('bqhgd,bshd->bhgqs', qblk.astype(jnp.float32), kf) * scale
        pr = jax.nn.softmax(s, axis=-1)
        return jnp.einsum('bhgqs,bshe->bqhge', pr, vf).astype(q.dtype)

    o = lax.map(one_block, qb)
    return jnp.moveaxis(o, 0, 1).reshape(B, L, Hk * G * e)

def merge_branches(y_ret, y_mla, y_gqa, gates, w_ret_o, w_mla_o, w_gqa_o, w_out):
    gs = jax.nn.sigmoid(gates)
    z = (gs[:, :, 0] * (y_ret @ w_ret_o)
         + gs[:, :, 1] * (y_mla @ w_mla_o)
         + gs[:, :, 2] * (y_gqa @ w_gqa_o))
    return z @ w_out

def token_mixer(h, hc, w_in, g_mla_q, g_mla_kv, w_mla_qb, w_mla_kvb, g_gqa_q, g_gqa_k,
                w_ret_o, w_mla_o, w_gqa_o, w_out, tabs_ret, tabs_mla, tabs_gqa, need_ctx):
    B, L = h.shape[:2]
    Cn = hc.shape[1]
    G = GQA_HEADS // GQA_KV_HEADS
    mla_scale = (MLA_NOPE + MLA_ROPE) ** -0.5
    gqa_scale = GQA_HD ** -0.5
    fl = mixer_features(h @ w_in, g_mla_q, g_mla_kv, w_mla_qb, w_mla_kvb, g_gqa_q, g_gqa_k,
                        tabs_ret, tabs_mla, tabs_gqa)
    fc = mixer_features(hc @ w_in, g_mla_q, g_mla_kv, w_mla_qb, w_mla_kvb, g_gqa_q, g_gqa_k,
                        None, None, None)
    y_ret, yc_ret = retention_branch(fl, fc, need_ctx)
    mla_k = jnp.concatenate([fc['mla_k'], fl['mla_k']], axis=1)
    mla_v = jnp.concatenate([fc['mla_v'], fl['mla_v']], axis=1)
    y_mla = block_attention(fl['mla_q'][:, :, :, None, :], mla_k, mla_v, mla_scale)
    gqa_k = jnp.concatenate([fc['gqa_k'], fl['gqa_k']], axis=1)
    gqa_v = jnp.concatenate([fc['gqa_v'], fl['gqa_v']], axis=1)
    y_gqa = block_attention(fl['gqa_q'].reshape(B, L, GQA_KV_HEADS, G, GQA_HD),
                            gqa_k, gqa_v, gqa_scale)
    y = merge_branches(y_ret, y_mla, y_gqa, fl['gates'], w_ret_o, w_mla_o, w_gqa_o, w_out)
    if not need_ctx:
        return y, None
    yc_mla = block_attention(fc['mla_q'][:, :, :, None, :], fc['mla_k'], fc['mla_v'], mla_scale)
    yc_gqa = block_attention(fc['gqa_q'].reshape(B, Cn, GQA_KV_HEADS, G, GQA_HD),
                             fc['gqa_k'], fc['gqa_v'], gqa_scale)
    yc = merge_branches(yc_ret, yc_mla, yc_gqa, fc['gates'], w_ret_o, w_mla_o, w_gqa_o, w_out)
    return y, yc

def swiglu(h, w_ffn_in, w_ffn_out):
    a, b = jnp.split(h @ w_ffn_in, 2, axis=-1)
    return (jax.nn.silu(a) * b) @ w_ffn_out

def setup_inputs(seed: int = 0) -> dict:
    key = jax.random.key(seed)
    ks = jax.random.split(key, 22)
    f32 = jnp.float32
    D = D_MODEL

    def normal(k, shape, s=1.0):
        return jax.random.normal(k, shape, f32) * s

    def dense(k, shape, fan_in, gain=1.0):
        return jax.random.normal(k, shape, f32) * (gain * fan_in ** -0.5)

    def norm_gain(k, shape):
        return 1.0 + 0.02 * jax.random.normal(k, shape, f32)

    return {
        'x': normal(ks[0], (BATCH, SEQ, D)),
        'c': normal(ks[1], (BATCH, D)),
        'ctx': normal(ks[2], (BATCH, CTX_LEN, D)),
        'c_ctx': normal(ks[3], (D,)),
        'w_mod': dense(ks[4], (DEPTH, D, N_MOD * D), D, 0.5),
        'b_mod': normal(ks[5], (DEPTH, N_MOD * D), 0.02),
        'g_mix': norm_gain(ks[6], (DEPTH, D)),
        'w_in': dense(ks[7], (DEPTH, D, IN_DIM), D),
        'g_mla_q': norm_gain(ks[8], (DEPTH, MLA_Q_RANK)),
        'g_mla_kv': norm_gain(ks[9], (DEPTH, MLA_KV_RANK)),
        'w_mla_qb': dense(ks[10], (DEPTH, MLA_Q_RANK, MLA_HEADS * (MLA_NOPE + MLA_ROPE)), MLA_Q_RANK),
        'w_mla_kvb': dense(ks[11], (DEPTH, MLA_KV_RANK, MLA_HEADS * (MLA_NOPE + MLA_V)), MLA_KV_RANK),
        'g_gqa_q': norm_gain(ks[12], (DEPTH, GQA_HD)),
        'g_gqa_k': norm_gain(ks[13], (DEPTH, GQA_HD)),
        'w_ret_o': dense(ks[14], (DEPTH, RET_W, D), RET_W),
        'w_mla_o': dense(ks[15], (DEPTH, MLA_W, D), MLA_W),
        'w_gqa_o': dense(ks[16], (DEPTH, GQA_W, D), GQA_W),
        'w_out': dense(ks[17], (DEPTH, D, D), D),
        'g_ffn': norm_gain(ks[18], (DEPTH, D)),
        'w_ffn_in': dense(ks[19], (DEPTH, D, 2 * FFN_HIDDEN), D),
        'w_ffn_out': dense(ks[20], (DEPTH, FFN_HIDDEN, D), FFN_HIDDEN),
        'g_final': norm_gain(ks[21], (D,)),
    }

def reference(x, c, ctx, c_ctx, w_mod, b_mod, g_mix, w_in, g_mla_q, g_mla_kv, w_mla_qb,
              w_mla_kvb, g_gqa_q, g_gqa_k, w_ret_o, w_mla_o, w_gqa_o, w_out, g_ffn,
              w_ffn_in, w_ffn_out, g_final):
    B, L, D = x.shape
    ROWS = L // GRID_W
    rows = jnp.repeat(jnp.arange(ROWS, dtype=jnp.int32), GRID_W)
    cols = jnp.arange(ROWS * GRID_W, dtype=jnp.int32) % GRID_W
    tabs_ret = rope_tables(rows, cols, RET_DK)
    tabs_mla = rope_tables(rows, cols, MLA_ROPE)
    tabs_gqa = rope_tables(rows, cols, GQA_HD)
    sc = jax.nn.silu(c)
    scc = jax.nn.silu(c_ctx)
    xc = ctx
    for l in range(DEPTH):
        need_ctx = l < DEPTH - 1
        mod = (sc @ w_mod[l] + b_mod[l]).reshape(B, 1, N_MOD, D)
        modc = (scc @ w_mod[l] + b_mod[l]).reshape(1, 1, N_MOD, D)
        h = modulate(rms_norm(x, g_mix[l]), mod[:, :, 0], mod[:, :, 1])
        hc = modulate(rms_norm(xc, g_mix[l]), modc[:, :, 0], modc[:, :, 1])
        y, yc = token_mixer(h, hc, w_in[l], g_mla_q[l], g_mla_kv[l], w_mla_qb[l], w_mla_kvb[l],
                            g_gqa_q[l], g_gqa_k[l], w_ret_o[l], w_mla_o[l], w_gqa_o[l], w_out[l],
                            tabs_ret, tabs_mla, tabs_gqa, need_ctx)
        x = x + mod[:, :, 2] * y
        h2 = modulate(rms_norm(x, g_ffn[l]), mod[:, :, 3], mod[:, :, 4])
        x = x + mod[:, :, 5] * swiglu(h2, w_ffn_in[l], w_ffn_out[l])
        if need_ctx:
            xc = xc + modc[:, :, 2] * yc
            hc2 = modulate(rms_norm(xc, g_ffn[l]), modc[:, :, 3], modc[:, :, 4])
            xc = xc + modc[:, :, 5] * swiglu(hc2, w_ffn_in[l], w_ffn_out[l])
    return rms_norm(x, g_final)


_drawn_inputs = setup_inputs


def setup_inputs(seed=0):
    import zlib

    import numpy as np

    out = dict(_drawn_inputs(seed))
    spreads = {}
    factors = {'g_mix': 8.0,
     'g_mla_q': 8.0,
     'g_mla_kv': 8.0,
     'w_mla_qb': 2.944,
     'g_gqa_q': 8.0,
     'g_gqa_k': 8.0,
     'g_ffn': 6.684,
     'g_final': 2.743}
    for name, (base, spread) in spreads.items():
        noise = np.random.default_rng([zlib.crc32(name.encode()), seed]).standard_normal(out[name].shape)
        drawn = base * np.exp(spread * noise) if base else spread * noise
        out[name] = jnp.asarray(drawn.astype(out[name].dtype))
    for name, factor in factors.items():
        out[name] = (out[name] * factor).astype(out[name].dtype)
    return out
```

```python
from contextlib import ExitStack

import numpy as np

import concourse.bass as bass
from concourse import mybir

F32 = mybir.dt.float32
F32R = mybir.dt.float32r
ALU = mybir.AluOpType
ACT = mybir.ActivationFunctionType
AX = mybir.AxisListType

P = 128
D = 1024
LAT = 512
CTX = 256
TOK = LAT + CTX
DEPTH = 2
KT = D // P
GRID_W = 64
ROPE_BASE = 10000.0
EPS = 1e-6

RET_HEADS, RET_DK, RET_DV = 4, 128, 256
MLA_HEADS, MLA_RANK, MLA_NOPE, MLA_ROPE, MLA_V = 8, 256, 64, 32, 128
MLA_QK = MLA_NOPE + MLA_ROPE
RKT = MLA_RANK // P
GQA_HEADS, GQA_KV, GQA_HD = 8, 2, 128
FFN = 2816
FT = FFN // P
GROUPS = [(0, 8), (8, 8), (16, 6)]
N_MOD = 6
CH = KT * P

O_RQ = 0
O_RK = O_RQ + RET_HEADS * RET_DK
O_RV = O_RK + RET_HEADS * RET_DK
O_RG = O_RV + RET_HEADS * RET_DV
O_CQ = O_RG + RET_HEADS * RET_DV
O_CKV = O_CQ + MLA_RANK
O_KR = O_CKV + MLA_RANK
O_GQ = O_KR + MLA_ROPE
O_GK = O_GQ + GQA_HEADS * GQA_HD
O_GV = O_GK + GQA_KV * GQA_HD
O_GATE = O_GV + GQA_KV * GQA_HD

G_LAYER = 2 * KT + 2 * RKT + 2
G_FINAL = DEPTH * G_LAYER
NGAIN = G_FINAL + KT

DEC1 = LAT + 3 * P
DEC2 = LAT + P
DEC = DEC1 + DEC2


def add(a, b, times=1):
    out = dict(a)
    for name, n in b.items():
        out[name] = out.get(name, 0) + n * times
    return out


PLAIN = {"e_hi": 1}
ROPED = {"v_perm": 1, "v_c": 1, "v_s": 1, "v_full": 1, "v_hi": 1, "v_lo": 1}
NORMED = {"v_stat": 1, "v_std": 1, "v_rstd": 1, "v_norm": 1}


def attention(nq):
    return {"s_ready": nq, "s_max": nq, "s_nm": nq, "s_exp": nq, "s_rinv": nq, "s_pn": nq,
            "t_ready": nq, "t_hi": nq, "t_lo": nq, "y_ready": nq // 2, "y_hi": nq // 2, "y_lo": nq // 2}


def total(*parts):
    out = {}
    for part in parts:
        out = add(out, part)
    return out


def plan():
    phases, now = [], {"f_lo": 2}

    def phase(kind, layer, turns, per, once=(), **args):
        nonlocal now
        once = dict(once)
        phases.append(dict(kind=kind, layer=layer, turns=turns, per=per, base=dict(now), once=once, **args))
        now = add(add(now, once), per, turns)

    for layer in range(DEPTH):
        full = layer < DEPTH - 1
        nt = TOK if full else LAT
        nq = nt // P
        units = 8 if full else 6
        norm = {"sq": KT, "sq_used": KT, "n_std": 1, "n_rstd": 1, "n_t1": KT, "n_hi": KT, "n_full": KT, "n_lo": KT}
        phase("mod", layer, N_MOD * KT // 2, {"chunk": 2}, {"mod": 3})
        phase("norm", layer, 0, {}, norm, nt=TOK, first=True)
        phase("mla_in", layer, 0, {}, total(
            {"chunk": 6, "free0": 3, "free1": 2, "v_stat": 2, "v_std": 2, "v_rstd": 2,
             "v_norm": 4, "v_hi": 4, "v_lo": 4, "tab": 1}, ROPED))
        phase("mla", layer, MLA_HEADS, total(
            {"chunk": 2, "free0": 2, "free1": 1, "k_ready": 1}, PLAIN, PLAIN, ROPED, attention(nq)), nt=nt)
        merge = {"chunk": 4, "free0": 2, "free1": 2, "mg_add": 2}
        phase("merge", layer, KT // 2, add(merge, {"mg_add": -2}), nt=nt, branch=1, first=True)
        for kv in range(GQA_KV):
            phase("gqa_kv", layer, 0, {}, total({"chunk": 2, "free0": 1, "free1": 1, "tab": 1 - kv},
                                                PLAIN, ROPED, NORMED), kv=kv)
            phase("gqa", layer, GQA_HEADS // GQA_KV // 2, total(
                {"chunk": 2, "free0": 2}, ROPED, ROPED, NORMED, NORMED, attention(nq), attention(nq)),
                nt=nt, kv=kv)
        phase("merge", layer, KT // 2, merge, nt=nt, branch=2, first=False)
        phase("ret", layer, RET_HEADS, total(
            {"chunk": 6, "free0": 4, "free1": 4, "dec": 1, "rs_ready": units, "rs_sd": units,
             "rs_hi": units, "rs_lo": units, "rs_used": units, "v_stat": 1, "v_std": 1, "v_rstd": 1,
             "v_norm": 2, "v_full": 2, "v_hi": 2, "v_lo": 2}, ROPED, ROPED, PLAIN, PLAIN), nt=nt)
        phase("merge", layer, KT // 2, merge, nt=nt, branch=0, first=False)
        phase("z", layer, 0, {}, {"z_hi": KT, "z_lo": KT}, nt=nt)
        phase("out", layer, KT // 2, {"chunk": 2, "free0": 1, "free1": 1},
              nt=nt, kt=KT, mod=2)
        phase("norm", layer, 0, {}, norm, nt=nt, first=False)
        for g, (t0, n) in enumerate(GROUPS):
            phase("ffn", layer, n // 2, {"chunk": 4, "free0": 2, "free1": 2, "f_hi": 2, "f_lo": 2},
                  nt=nt)
            phase("out", layer, KT // 2, {"chunk": 2, "free0": 1, "free1": 1},
                  nt=nt, kt=n, mod=5, group=g)
    phase("final", DEPTH - 1, 0, {}, {}, nt=LAT)
    return phases, now


PHASES, TOTALS = plan()
NCHUNK = TOTALS["chunk"]


class At:

    def __init__(self, ph, i=0, end=False):
        self.base, self.per, self.i = ph["base"], ph["per"], i
        if end:
            self.base, self.i = add(add(ph["base"], ph["once"]), ph["per"], ph["turns"]), 0

    def v(self, name, k=0):
        per = self.per.get(name, 0)
        at = self.base.get(name, 0) + k
        return at + self.i * per if per else at

    def slot(self, k):
        return (self.base.get("chunk", 0) + k) % 2

    def half(self, k):
        return (self.base.get("chunk", 0) + k) // 2 + 1 + self.i * (self.per.get("chunk", 0) // 2)


def ranges(nt):
    return [(0, LAT)] + ([(LAT, nt)] if nt > LAT else [])


def build(nc, a):
    ctx = ExitStack()
    with ctx:
        def sb(name, shape, dt=F32):
            return ctx.enter_context(nc.sbuf_tensor(name, shape, dt))

        sems = {}

        def sem(name):
            if name not in sems:
                sems[name] = ctx.enter_context(nc.semaphore(name))
            return sems[name]

        at = (nc.sbuf_base + 31) // 32 * 32
        arena = sb("arena", [P, KT * TOK + 8])
        xz = nc.alloc_sbuf_tensor_at("xz", [P, KT, TOK], F32, offset=at)
        ranks = nc.alloc_sbuf_tensor_at("ranks", [P, 2, 2, RKT, TOK], F32R, offset=at)
        hh, hl = sb("hh", [P, KT, TOK], F32R), sb("hl", [P, KT, TOK], F32R)
        yh, yl = sb("yh", [P, KT, TOK], F32R), sb("yl", [P, KT, TOK], F32R)
        raw = sb("raw", [P, 2, CH])
        wh, wl = sb("wh", [P, 2, CH], F32R), sb("wl", [P, 2, CH], F32R)
        kh, kl = sb("kh", [P, TOK], F32R), sb("kl", [P, TOK], F32R)
        qh, ql = sb("qh", [P, TOK], F32R), sb("ql", [P, TOK], F32R)
        vh, vl = sb("vh", [P, 2, TOK], F32R), sb("vl", [P, 2, TOK], F32R)
        tmp = sb("tmp", [P, 3, TOK])
        prob = sb("prob", [P, 3, TOK])
        pth, ptl = sb("pth", [P, 6, 2 * P], F32R), sb("ptl", [P, 6, 2 * P], F32R)
        rope = sb("rope", [P, 2, LAT])
        dec = sb("dec", [P, DEC])
        perm = sb("perm", [P, 2, P])
        ident, ones = sb("ident", [P, P]), sb("ones", [P, P])
        eps = sb("eps", [P, 1])
        gains = sb("gains", [P, NGAIN])
        bmod = sb("bmod", [P, DEPTH, N_MOD * KT])
        cvec, csil = sb("cvec", [P, KT, 2]), sb("csil", [P, KT, 2])
        ch, cl = sb("ch", [P, KT, 2], F32R), sb("cl", [P, KT, 2], F32R)
        mods = sb("mods", [P, N_MOD * KT, 2])
        gm = sb("gm", [P, 2, KT, 2])
        mx, nm = sb("mx", [P, 6]), sb("nm", [P, 6])
        mark = sb("mark", [P, 2])
        rs, ri = sb("rs", [P, 6]), sb("ri", [P, 6])
        ps = ctx.enter_context(nc.psum_tensor("ps", [P, 8 * LAT], F32))
        BANK = LAT

        def pair(slot):
            return ps[:, 2 * BANK * slot:2 * BANK * slot + TOK]

        AUX = 2
        pth_f = pth[:, :, :].rearrange("p a b -> p (a b)")
        ptl_f = ptl[:, :, :].rearrange("p a b -> p (a b)")
        xspill = nc.dram_tensor("xspill", (D, TOK), F32, kind="Internal").ap()

        block = ctx.enter_context(nc.Block())

        @block.sync
        def _(sp):
            for s in range(2):
                sp.dma_start(raw[:, s, :], a["stream"][s]).then_inc(sem(f"raw_in{s}"), 16)
            with sp.Fori(1, NCHUNK // 2) as i:
                for s in range(2):
                    sp.wait_ge(sem("w_lo"), 2 * i + (s - 1))
                    src = a["stream"][bass.ds(2 * i + s, 1)].rearrange("a p n -> (a p) n")
                    sp.dma_start(raw[:, s, :], src).then_inc(sem(f"raw_in{s}"), 16)
            sp.wait_ge(sem("out_done"), 16 * KT)

        @block.scalar
        def _(act):
            def split(at, k):
                s = at.slot(k)
                act.wait_ge(sem(f"raw_in{s}"), at.half(k) * 16)
                used = at.v("chunk", k - 1)
                if not isinstance(used, int) or used > 0:
                    act.wait_ge(sem("product"), used)
                act.activation(wh[:, s, :], raw[:, s, :], ACT.Copy).then_inc(sem("w_hi"), 1)

            def plain(at, kc, slot, dst, rows=P, nt=TOK):
                act.wait_ge(sem("product"), at.v("chunk", kc + 1))
                act.activation(dst[0:rows, 0:nt], pair(slot)[0:rows, 0:nt], ACT.Copy).then_inc(sem("e_hi"), 1)

            def std(at, k, nt, n, rows=P):
                act.wait_ge(sem("v_stat"), at.v("v_stat", k + 1))
                act.activation(tmp[0:rows, 2, 0:nt], pair(AUX)[0:rows, 0:nt], ACT.Sqrt, bias=eps[0:rows, :],
                               scale=1.0 / n).then_inc(sem("v_std"), 1)

            def roped(at, kc, kv, kf, slot, dst, rows, r0, nt, scale=1.0, kn=None):
                act.wait_ge(sem("product"), at.v("chunk", kc + 1))
                act.wait_ge(sem("v_lo"), at.v("v_lo", kv))
                if kn is None:
                    act.activation(tmp[0:rows, 0, 0:nt], pair(slot)[0:rows, 0:nt], ACT.Copy,
                                   scale=scale).then_inc(sem(f"free{slot}"), 1)
                else:
                    act.activation(tmp[0:rows, 0, 0:nt], pair(slot)[0:rows, 0:nt], ACT.Copy)
                    act.activation(tmp[0:rows, 1, 0:nt], pair(slot)[0:rows, 0:nt],
                                   ACT.Square).then_inc(sem(f"free{slot}"), 1)
                    std(at, kn, nt, GQA_HD)
                act.wait_ge(sem("v_full"), at.v("v_full", kf + 1))
                act.activation(dst[r0:rows, 0:nt], tmp[r0:rows, 0, 0:nt], ACT.Copy).then_inc(sem("v_hi"), 1)

            def attend(at, ka, nt, rows, scale, head):
                nq, a0, b0 = nt // P, ka * (nt // P), ka * (nt // P) // 2
                for n in range(nq + 2):
                    if n < nq:
                        w = TOK if n < 4 else CTX
                        act.wait_ge(sem("s_nm"), at.v("s_nm", a0 + n + 1))
                        if n >= 3:
                            act.wait_ge(sem("t_ready"), at.v("t_ready", a0 + n - 2))
                        act.activation(prob[:, n % 3, 0:w], ps[:, (4 + 2 * (n % 2)) * BANK:(4 + 2 * (n % 2)) * BANK + w], ACT.Exp,
                                       bias=nm[:, n:n + 1], scale=scale,
                                       accum_out=rs[:, n:n + 1]).then_inc(sem("s_exp"), 1)
                    m = n - 2
                    if 0 <= m < nq:
                        st = 6 if m < 4 else 2
                        act.wait_ge(sem("t_ready"), at.v("t_ready", a0 + m + 1))
                        if m % 2 == 0 and m >= 2:
                            act.wait_ge(sem("y_ready"), at.v("y_ready", b0 + m // 2))
                        act.activation(pth[:, 0:st, (m % 2) * P:(m % 2) * P + P],
                                       pair(1)[:, 0:st * P].rearrange("p (s q) -> p s q", q=P),
                                       ACT.Copy).then_inc(sem("t_hi"), 1)
                    b = n // 2 - 2
                    if n % 2 == 0 and b >= 0:
                        y_hi(at, b0, b, head)
                y_hi(at, b0, nq // 2 - 1, head)

            def y_hi(at, b0, b, head):
                act.wait_ge(sem("y_ready"), at.v("y_ready", b0 + b + 1))
                act.activation(yh[:, bass.ds(head, 1), 2 * P * b:2 * P * (b + 1)], pair(0)[:, 2 * P * b:2 * P * (b + 1)],
                               ACT.Copy).then_inc(sem("y_hi"), 1)

            def load_x(src):
                for t in range(KT):
                    act.dma_start(xz[:, t, :], src[t * P:(t + 1) * P, :]).then_inc(sem("x_in"), 16)

            act.dma_start(cvec[:, :, :], a["cvec"]).then_inc(sem("c_in"), 16)
            for dst, name in ((gains[:, :], "gains"), (bmod[:, :, :], "bmod"), (perm[:, :, :], "perm"),
                              (ident[:, :], "ident")):
                act.dma_start(dst, a[name]).then_inc(sem("const_in"), 16)
            load_x(a["xT"])
            act.wait_ge(sem("c_in"), 16)
            act.activation(csil[:, :, :], cvec[:, :, :], ACT.Silu).then_inc(sem("c_silu"), 1)
            act.wait_ge(sem("c_silu"), 1)
            act.activation(ch[:, :, :], csil[:, :, :], ACT.Copy).then_inc(sem("c_hi"), 1)
            act.wait_ge(sem("const_in"), 64)
            act.wait_ge(sem("eps_set"), 1)
            split(At(PHASES[0]), 0)
            x_loads = 1

            for ph in PHASES:
                kind, layer, at, end = ph["kind"], ph["layer"], At(ph), At(ph, end=True)
                nt, turns = ph.get("nt"), ph["turns"]
                if kind == "mod":
                    for k in range(2):
                        split(At(ph, 0), k + 1)
                    with act.Fori(1, turns) as i:
                        for k in range(2):
                            split(At(ph, i), k + 1)

                elif kind == "norm":
                    if layer == 0 and ph["first"]:
                        act.wait_ge(sem("x_in"), 16 * KT)
                    elif at.v("free0"):
                        act.wait_ge(sem("free0"), at.v("free0"))
                        act.wait_ge(sem("free1"), at.v("free1"))
                        if ph["first"]:
                            for t in range(KT):
                                act.dma_start(xspill[t * P:(t + 1) * P, :], xz[:, t, :]).then_inc(sem("x_out"), 16)
                    for t in range(KT):
                        if t >= 2:
                            act.wait_ge(sem("sq_used"), at.v("sq_used", t - 1))
                        act.activation(tmp[:, t % 2, 0:nt], xz[:, t, 0:nt], ACT.Square).then_inc(sem("sq"), 1)
                    act.wait_ge(sem("sq_used"), at.v("sq_used", KT))
                    act.activation(tmp[:, 2, 0:nt], pair(AUX)[:, 0:nt], ACT.Sqrt, bias=eps[:, :],
                                   scale=1.0 / D).then_inc(sem("n_std"), 1)
                    gi = 0 if ph["first"] else 1
                    act.wait_ge(sem("mod"), 3 * (layer + 1))
                    for t in range(KT):
                        act.wait_ge(sem("n_t1"), at.v("n_t1", t + 1))
                        for u, (r0, r1) in enumerate(ranges(nt)):
                            ins = act.activation(hh[:, t, r0:r1], tmp[:, t % 2, r0:r1], ACT.Identity,
                                                 bias=mods[:, 3 * gi * KT + t, u:u + 1],
                                                 scale=gm[:, gi, t, u:u + 1])
                        ins.then_inc(sem("n_hi"), 1)

                elif kind == "mla_in":
                    if layer:
                        act.wait_ge(sem("x_out"), 16 * KT)
                    act.dma_start(rope[:, :, :], a["rope"][1]).then_inc(sem("tab_in"), 16)
                    for j, (nt_j, which) in enumerate(((TOK if layer < DEPTH - 1 else LAT, 0), (TOK, 1))):
                        for k in range(RKT):
                            split(at, 2 * j + k + 1)
                            act.wait_ge(sem("product"), at.v("chunk", 2 * j + k + 1))
                            if j:
                                act.wait_ge(sem("v_lo"), at.v("v_lo", 2))
                            elif k == 0:
                                act.wait_ge(sem("n_lo"), at.v("n_lo"))
                            act.activation(tmp[:, k, 0:nt_j], pair(k)[:, 0:nt_j], ACT.Copy)
                            act.activation(prob[:, k, 0:nt_j], pair(k)[:, 0:nt_j],
                                           ACT.Square).then_inc(sem(f"free{k}"), 1)
                        std(at, j, nt_j, MLA_RANK)
                        for k in range(RKT):
                            act.wait_ge(sem("v_norm"), at.v("v_norm", 2 * j + k + 1))
                            act.activation(ranks[:, which, 0, k, 0:nt_j], tmp[:, k, 0:nt_j],
                                           ACT.Copy).then_inc(sem("v_hi"), 1)
                    split(at, 5)
                    split(at, 6)
                    roped(at, 5, 4, 0, 0, kh, MLA_QK, MLA_NOPE, TOK)

                elif kind == "mla":
                    with act.Fori(0, turns) as i:
                        t = At(ph, i)
                        split(t, 1)
                        act.wait_ge(sem("k_ready"), t.v("k_ready", 1))
                        act.activation(kh[0:MLA_NOPE, :], pair(0)[0:MLA_NOPE, :], ACT.Copy).then_inc(sem("e_hi"), 1)
                        plain(t, 0, 1, vh[:, 0, :])
                        split(t, 2)
                        roped(t, 1, 0, 0, 0, qh, MLA_QK, 0, nt)
                        attend(t, 0, nt, MLA_QK, MLA_QK ** -0.5, i)

                elif kind == "gqa_kv":
                    if ph["kv"] == 0:
                        act.wait_ge(sem("free1"), at.v("free1"))
                        act.dma_start(rope[:, :, :], a["rope"][0]).then_inc(sem("tab_in"), 16)
                    split(at, 1)
                    roped(at, 0, 0, 0, 0, kh, P, 0, TOK, kn=0)
                    split(at, 2)
                    plain(at, 1, 1, vh[:, 0, :])

                elif kind == "gqa":
                    with act.Fori(0, turns) as i:
                        t = At(ph, i)
                        for k in range(2):
                            split(t, k + 1)
                            roped(t, k, k, k, 0, qh, P, 0, nt, kn=k)
                            attend(t, k, nt, P, GQA_HD ** -0.5, 2 * i + (4 * ph["kv"] + k))

                elif kind == "merge":
                    act.wait_ge(sem("v_lo"), at.v("v_lo"))
                    act.wait_ge(sem("y_lo"), at.v("y_lo"))
                    with act.Fori(0, turns) as i:
                        t = At(ph, i)
                        for k in range(2):
                            split(t, 2 * k + 1)
                            act.wait_ge(sem("product"), t.v("chunk", 2 * k + 1))
                            act.wait_ge(sem("free1"), t.v("free1", k - 1))
                            act.activation(tmp[:, k, 0:nt], pair(0)[:, 0:nt],
                                           ACT.Sigmoid).then_inc(sem("free0"), 1)
                            split(t, 2 * k + 2)

                elif kind == "ret":
                    act.wait_ge(sem("free1"), at.v("free1"))
                    with act.Fori(0, turns) as i:
                        t = At(ph, i)
                        act.dma_start(dec[:, :], a["dec"][bass.ds(i, 1)].rearrange("a p n -> (a p) n")).then_inc(
                            sem("dec_in"), 16)
                        split(t, 1)
                        roped(t, 0, 0, 0, 0, qh, P, 0, nt)
                        split(t, 2)
                        roped(t, 1, 1, 1, 1, kh, P, 0, TOK, scale=RET_DK ** -0.5)
                        for e in range(2):
                            split(t, 3 + e)
                            plain(t, 2 + e, e, vh[:, e, :])
                        units = 8 if nt > LAT else 6
                        for u in range(units):
                            w = LAT if u < 6 else CTX
                            act.wait_ge(sem("rs_sd"), t.v("rs_sd", u + 1))
                            if u >= 3:
                                act.wait_ge(sem("rs_used"), t.v("rs_used", u - 2))
                            act.activation(pth_f[:, (u % 3) * LAT:(u % 3) * LAT + w], prob[:, u % 3, 0:w],
                                           ACT.Copy).then_inc(sem("rs_hi"), 1)
                        for e in range(2):
                            if e == 0:
                                act.wait_ge(sem("rs_used"), t.v("rs_used", units))
                                act.wait_ge(sem("v_lo"), t.v("v_lo", 2))
                            act.activation(tmp[:, e, 0:nt], pair(e)[:, 0:nt], ACT.Copy)
                            act.activation(prob[:, e, 0:nt], pair(e)[:, 0:nt],
                                           ACT.Square).then_inc(sem(f"free{e}"), 1)
                        std(t, 0, nt, RET_DV)
                        for e in range(2):
                            split(t, 5 + e)
                            act.wait_ge(sem("product"), t.v("chunk", 5 + e))
                            act.activation(prob[:, e, 0:nt], pair(e)[:, 0:nt], ACT.Silu).then_inc(sem(f"free{e}"), 1)
                        for e in range(2):
                            act.wait_ge(sem("v_full"), t.v("v_full", 3 + e))
                            act.activation(yh[:, bass.ds(2 * i + e, 1), 0:nt], tmp[:, e, 0:nt],
                                           ACT.Copy).then_inc(sem("v_hi"), 1)

                elif kind == "z":
                    act.wait_ge(sem("mg_add"), at.v("mg_add"))
                    for t in range(KT):
                        act.activation(yh[:, t, 0:nt], xz[:, t, 0:nt], ACT.Copy).then_inc(sem("z_hi"), 1)
                    act.wait_ge(sem("z_lo"), at.v("z_lo", KT))
                    load_x(xspill if layer else a["xT"])
                    x_loads += 1

                elif kind == "out":
                    if at.v("chunk") + 2 * turns < NCHUNK:
                        with act.Fori(0, turns) as i:
                            for k in range(2):
                                split(At(ph, i), k + 1)
                    else:
                        with act.Fori(0, turns - 1) as i:
                            for k in range(2):
                                split(At(ph, i), k + 1)
                        split(At(ph, turns - 1), 1)

                elif kind == "ffn":
                    with act.Fori(0, turns) as i:
                        t = At(ph, i)
                        for k in range(2):
                            split(t, 2 * k + 1)
                            act.wait_ge(sem("product"), t.v("chunk", 2 * k + 1))
                            act.wait_ge(sem("free1"), t.v("free1", k - 1))
                            act.activation(tmp[:, k, 0:nt], pair(0)[:, 0:nt], ACT.Silu).then_inc(sem("free0"), 1)
                            split(t, 2 * k + 2)
                            act.wait_ge(sem("free1"), t.v("free1", k + 1))
                            act.activation(yh[:, bass.ds(2 * i + k, 1), 0:nt], prob[:, k, 0:nt],
                                           ACT.Copy).then_inc(sem("f_hi"), 1)

                elif kind == "final":
                    act.wait_ge(sem("free0"), at.v("free0"))
                    act.wait_ge(sem("free1"), at.v("free1"))
                    for t in range(KT):
                        if t >= 2:
                            act.wait_ge(sem("sq_used"), at.v("sq_used", t - 1))
                        act.activation(tmp[:, t % 2, 0:nt], xz[:, t, 0:nt], ACT.Square).then_inc(sem("sq"), 1)
                    act.wait_ge(sem("sq_used"), at.v("sq_used", KT))
                    act.activation(tmp[:, 2, 0:nt], pair(AUX)[:, 0:nt], ACT.Sqrt, bias=eps[:, :],
                                   scale=1.0 / D).then_inc(sem("n_std"), 1)
                    for t in range(KT):
                        act.wait_ge(sem("o_ready"), t + 1)
                        act.dma_start(a["out"][t * P:(t + 1) * P, :], xz[:, t, 0:LAT]).then_inc(sem("out_done"), 16)
                    act.wait_ge(sem("out_done"), 16 * KT)

        @block.vector
        def _(dve):
            def split(at, k):
                s = at.slot(k)
                dve.wait_ge(sem("w_hi"), at.v("chunk", k + 1))
                dve.tensor_tensor(wl[:, s, :], raw[:, s, :], wh[:, s, :].bitcast(F32), ALU.subtract).then_inc(
                    sem("w_lo"), 1)

            def plain(at, ke, slot, hi, lo, rows=P, nt=TOK):
                dve.wait_ge(sem("e_hi"), at.v("e_hi", ke + 1))
                dve.tensor_tensor(lo[0:rows, 0:nt], pair(slot)[0:rows, 0:nt], hi[0:rows, 0:nt].bitcast(F32),
                                  ALU.subtract).then_inc(sem(f"free{slot}"), 1)

            def rstd(at, k, nt):
                dve.wait_ge(sem("v_std"), at.v("v_std", k + 1))
                dve.reciprocal(tmp[:, 2, 0:nt], tmp[:, 2, 0:nt]).then_inc(sem("v_rstd"), 1)
                dve.wait_ge(sem("v_rstd"), at.v("v_rstd", k + 1))

            def roped(at, kv, kp, slot, kfree, hi, lo, rows, r0, nt, kn=None, gain=None):
                dve.wait_ge(sem(f"free{slot}"), at.v(f"free{slot}", kfree))
                if kn is not None:
                    rstd(at, kn, nt)
                    dve.scalar_tensor_tensor(out=tmp[:, 0, 0:nt], in0=tmp[:, 0, 0:nt], scalar=gain,
                                             in1=tmp[:, 2, 0:nt], op0=ALU.mult, op1=ALU.mult).then_inc(
                        sem("v_norm"), 1)
                    dve.wait_ge(sem("v_norm"), at.v("v_norm", kn + 1))
                dve.tensor_tensor(tmp[0:rows, 1, 0:LAT], tmp[0:rows, 0, 0:LAT], rope[0:rows, 0, :],
                                  ALU.mult).then_inc(sem("v_c"), 1)
                dve.wait_ge(sem("v_perm"), at.v("v_perm", kp + 1))
                dve.tensor_tensor(tmp[0:rows, 2, 0:LAT], ps[0:rows, 6 * BANK:7 * BANK], rope[0:rows, 1, :],
                                  ALU.mult).then_inc(sem("v_s"), 1)
                dve.wait_ge(sem("v_c"), at.v("v_c", kp + 1))
                dve.wait_ge(sem("v_s"), at.v("v_s", kp + 1))
                dve.tensor_tensor(tmp[0:rows, 0, 0:LAT], tmp[0:rows, 1, 0:LAT], tmp[0:rows, 2, 0:LAT],
                                  ALU.add).then_inc(sem("v_full"), 1)
                dve.wait_ge(sem("v_full"), at.v("v_full", kv[1] + 1))
                dve.wait_ge(sem("v_hi"), at.v("v_hi", kv[0] + 1))
                dve.tensor_tensor(lo[r0:rows, 0:nt], tmp[r0:rows, 0, 0:nt], hi[r0:rows, 0:nt].bitcast(F32),
                                  ALU.subtract).then_inc(sem("v_lo"), 1)

            def attend(at, ka, nt, scale, head):
                nq, a0, b0 = nt // P, ka * (nt // P), ka * (nt // P) // 2
                for n in range(nq + 2):
                    if n < nq:
                        w = TOK if n < 4 else CTX
                        dve.wait_ge(sem("s_ready"), at.v("s_ready", a0 + n + 1))
                        dve.tensor_reduce(mx[:, n:n + 1], ps[:, (4 + 2 * (n % 2)) * BANK:(4 + 2 * (n % 2)) * BANK + w], AX.X,
                                          ALU.max).then_inc(sem("s_max"), 1)
                        dve.wait_ge(sem("s_max"), at.v("s_max", a0 + n + 1))
                        dve.tensor_scalar(nm[:, n:n + 1], mx[:, n:n + 1], -scale, None, ALU.mult).then_inc(
                            sem("s_nm"), 1)
                    m = n - 1
                    if 0 <= m < nq:
                        dve.wait_ge(sem("s_exp"), at.v("s_exp", a0 + m + 1))
                        dve.reciprocal(ri[:, m:m + 1], rs[:, m:m + 1]).then_inc(sem("s_rinv"), 1)
                    m = n - 2
                    if 0 <= m < nq:
                        st = 6 if m < 4 else 2
                        cols = slice((m % 2) * P, (m % 2) * P + P)
                        dve.wait_ge(sem("t_hi"), at.v("t_hi", a0 + m + 1))
                        dve.tensor_tensor(ptl[:, 0:st, cols],
                                          pair(1)[:, 0:st * P].rearrange("p (s q) -> p s q", q=P),
                                          pth[:, 0:st, cols].bitcast(F32), ALU.subtract).then_inc(sem("t_lo"), 1)
                    b = n // 2 - 2
                    if n % 2 == 0 and b >= 0:
                        y_lo(at, b0, b, head)
                y_lo(at, b0, nq // 2 - 1, head)

            def y_lo(at, b0, b, head):
                dve.wait_ge(sem("y_hi"), at.v("y_hi", b0 + b + 1))
                cols = slice(2 * P * b, 2 * P * (b + 1))
                dve.tensor_tensor(yl[:, bass.ds(head, 1), cols], pair(0)[:, cols].unsqueeze(1),
                                  yh[:, bass.ds(head, 1), cols].bitcast(F32),
                                  ALU.subtract).then_inc(sem("y_lo"), 1)

            dve.memset(ones[:, :], 1.0).then_inc(sem("ones_set"), 1)
            dve.memset(eps[:, :], EPS).then_inc(sem("eps_set"), 1)
            dve.wait_ge(sem("c_hi"), 1)
            dve.tensor_tensor(cl[:, :, :], csil[:, :, :], ch[:, :, :].bitcast(F32), ALU.subtract).then_inc(
                sem("c_lo"), 1)
            dve.wait_ge(sem("const_in"), 64)
            split(At(PHASES[0]), 0)
            x_loads = 1
            tabs = 0

            for ph in PHASES:
                kind, layer, at = ph["kind"], ph["layer"], At(ph)
                nt, turns = ph.get("nt"), ph["turns"]
                g0 = layer * G_LAYER
                if kind == "mod":
                    with dve.Fori(0, turns) as i:
                        for k in range(2):
                            split(At(ph, i), k + 1)
                    end = At(ph, end=True)
                    dve.wait_ge(sem("product"), end.v("chunk"))
                    dve.tensor_tensor(
                        mods[:, :, :], ps[:, 7 * BANK:7 * BANK + 2 * N_MOD * KT].rearrange("p (j u) -> p j u", u=2),
                        bmod[:, layer, :].unsqueeze(2).to_broadcast([P, N_MOD * KT, 2]), ALU.add).then_inc(
                        sem("mod"), 1)
                    dve.wait_ge(sem("mod"), 3 * layer + 1)
                    for j in range(2):
                        dve.scalar_tensor_tensor(
                            out=gm[:, j, :, :], in0=mods[:, (3 * j + 1) * KT:(3 * j + 2) * KT, :], scalar=1.0,
                            in1=gains[:, g0 + j * KT:g0 + (j + 1) * KT].unsqueeze(2).to_broadcast([P, KT, 2]),
                            op0=ALU.add, op1=ALU.mult).then_inc(sem("mod"), 1)
                    dve.wait_ge(sem("mod"), 3 * layer + 3)

                elif kind == "norm":
                    gi = 0 if ph["first"] else 1
                    dve.wait_ge(sem("n_std"), at.v("n_std", 1))
                    dve.reciprocal(tmp[:, 2, 0:nt], tmp[:, 2, 0:nt]).then_inc(sem("n_rstd"), 1)
                    dve.wait_ge(sem("n_rstd"), at.v("n_rstd", 1))
                    for t in range(KT + 1):
                        if t < KT:
                            if t >= 2:
                                dve.wait_ge(sem("n_hi"), at.v("n_hi", t - 1))
                                dve.wait_ge(sem("n_full"), at.v("n_full", t - 1))
                            dve.tensor_tensor(tmp[:, t % 2, 0:nt], xz[:, t, 0:nt], tmp[:, 2, 0:nt],
                                              ALU.mult).then_inc(sem("n_t1"), 1)
                        m = t - 1
                        if m >= 0:
                            if m >= 2:
                                dve.wait_ge(sem("n_lo"), at.v("n_lo", m - 1))
                            dve.wait_ge(sem("n_t1"), at.v("n_t1", m + 1))
                            for u, (r0, r1) in enumerate(ranges(nt)):
                                ins = dve.tensor_scalar(prob[:, m % 2, r0:r1], tmp[:, m % 2, r0:r1],
                                                        gm[:, gi, m, u:u + 1],
                                                        mods[:, 3 * gi * KT + m, u:u + 1], ALU.mult, ALU.add)
                            ins.then_inc(sem("n_full"), 1)

                elif kind == "mla_in":
                    for j, nt_j in enumerate((TOK if layer < DEPTH - 1 else LAT, TOK)):
                        for k in range(RKT):
                            split(at, 2 * j + k + 1)
                        rstd(at, j, nt_j)
                        for k in range(RKT):
                            col = g0 + 2 * KT + j * RKT + k
                            dve.scalar_tensor_tensor(out=tmp[:, k, 0:nt_j], in0=tmp[:, k, 0:nt_j],
                                                     scalar=gains[:, col:col + 1], in1=tmp[:, 2, 0:nt_j],
                                                     op0=ALU.mult, op1=ALU.mult).then_inc(sem("v_norm"), 1)
                        for k in range(RKT):
                            dve.wait_ge(sem("v_norm"), at.v("v_norm", 2 * j + k + 1))
                            dve.wait_ge(sem("v_hi"), at.v("v_hi", 2 * j + k + 1))
                            dve.tensor_tensor(ranks[:, j, 1, k, 0:nt_j], tmp[:, k, 0:nt_j],
                                              ranks[:, j, 0, k, 0:nt_j].bitcast(F32), ALU.subtract).then_inc(
                                sem("v_lo"), 1)
                    split(at, 5)
                    split(at, 6)
                    tabs += 1
                    dve.wait_ge(sem("tab_in"), 16 * tabs)
                    roped(at, (4, 0), 0, 0, 3, kh, kl, MLA_QK, MLA_NOPE, TOK)

                elif kind == "mla":
                    with dve.Fori(0, turns) as i:
                        t = At(ph, i)
                        split(t, 1)
                        plain(t, 0, 0, kh, kl, rows=MLA_NOPE)
                        plain(t, 1, 1, vh[:, 0, :], vl[:, 0, :])
                        split(t, 2)
                        roped(t, (0, 0), 0, 0, 2, qh, ql, MLA_QK, 0, nt)
                        attend(t, 0, nt, MLA_QK ** -0.5, i)

                elif kind == "gqa_kv":
                    if ph["kv"] == 0:
                        tabs += 1
                        dve.wait_ge(sem("tab_in"), 16 * tabs)
                    split(at, 1)
                    roped(at, (0, 0), 0, 0, 1, kh, kl, P, 0, TOK, kn=0,
                          gain=gains[:, g0 + 2 * KT + 2 * RKT + 1:g0 + 2 * KT + 2 * RKT + 2])
                    split(at, 2)
                    plain(at, 0, 1, vh[:, 0, :], vl[:, 0, :])

                elif kind == "gqa":
                    with dve.Fori(0, turns) as i:
                        t = At(ph, i)
                        for k in range(2):
                            split(t, k + 1)
                            roped(t, (k, k), k, 0, k + 1, qh, ql, P, 0, nt, kn=k,
                                  gain=gains[:, g0 + 2 * KT + 2 * RKT:g0 + 2 * KT + 2 * RKT + 1])
                            attend(t, k, nt, GQA_HD ** -0.5, 2 * i + (4 * ph["kv"] + k))

                elif kind == "merge":
                    with dve.Fori(0, turns) as i:
                        t = At(ph, i)
                        for k in range(2):
                            split(t, 2 * k + 1)
                            split(t, 2 * k + 2)
                            dve.wait_ge(sem("free0"), t.v("free0", k + 1))
                            dve.wait_ge(sem("product"), t.v("chunk", 2 * k + 2))
                            z = xz[:, bass.ds(2 * i + k, 1), 0:nt]
                            dve.tensor_tensor(z if ph["first"] else prob[:, k:k + 1, 0:nt],
                                              pair(1)[:, 0:nt].unsqueeze(1), tmp[:, k:k + 1, 0:nt],
                                              ALU.mult).then_inc(sem("free1"), 1)
                            if not ph["first"]:
                                dve.wait_ge(sem("free1"), t.v("free1", k + 1))
                                dve.tensor_tensor(z, z, prob[:, k:k + 1, 0:nt], ALU.add).then_inc(sem("mg_add"), 1)
                                dve.wait_ge(sem("mg_add"), t.v("mg_add", k + 1))

                elif kind == "ret":
                    with dve.Fori(0, turns) as i:
                        t = At(ph, i)
                        split(t, 1)
                        roped(t, (0, 0), 0, 0, 1, qh, ql, P, 0, nt)
                        split(t, 2)
                        roped(t, (1, 1), 1, 1, 1, kh, kl, P, 0, TOK)
                        for e in range(2):
                            split(t, 3 + e)
                            plain(t, e, e, vh[:, e, :], vl[:, e, :])
                        units = 8 if nt > LAT else 6
                        dve.wait_ge(sem("dec_in"), t.v("dec", 1) * 16)
                        for u in range(units):
                            w = LAT if u < 6 else CTX
                            d0 = (3 * P - P * u if u < 4 else DEC1 + P - P * (u - 4) if u < 6
                                  else 3 * P - P * (u - 6))
                            dve.wait_ge(sem("rs_ready"), t.v("rs_ready", u + 1))
                            if u >= 3:
                                dve.wait_ge(sem("rs_lo"), t.v("rs_lo", u - 2))
                            dve.tensor_tensor(prob[:, u % 3, 0:w], ps[:, (4 + u % 3) * BANK:(4 + u % 3) * BANK + w],
                                              dec[:, d0:d0 + w], ALU.mult).then_inc(sem("rs_sd"), 1)
                        rstd(t, 0, nt)
                        for e in range(2):
                            dve.tensor_tensor(tmp[:, e, 0:nt], tmp[:, e, 0:nt], tmp[:, 2, 0:nt],
                                              ALU.mult).then_inc(sem("v_norm"), 1)
                        for e in range(2):
                            split(t, 5 + e)
                            dve.wait_ge(sem("v_norm"), t.v("v_norm", e + 1))
                            dve.wait_ge(sem(f"free{e}"), t.v(f"free{e}", 4))
                            dve.tensor_tensor(tmp[:, e, 0:nt], tmp[:, e, 0:nt], prob[:, e, 0:nt],
                                              ALU.mult).then_inc(sem("v_full"), 1)
                        for e in range(2):
                            dve.wait_ge(sem("v_full"), t.v("v_full", 3 + e))
                            dve.wait_ge(sem("v_hi"), t.v("v_hi", 3 + e))
                            dve.tensor_tensor(yl[:, bass.ds(2 * i + e, 1), 0:nt], tmp[:, e:e + 1, 0:nt],
                                              yh[:, bass.ds(2 * i + e, 1), 0:nt].bitcast(F32), ALU.subtract).then_inc(
                                sem("v_lo"), 1)

                elif kind == "z":
                    for t in range(KT):
                        dve.wait_ge(sem("z_hi"), at.v("z_hi", t + 1))
                        dve.tensor_tensor(yl[:, t, 0:nt], xz[:, t, 0:nt], yh[:, t, 0:nt].bitcast(F32),
                                          ALU.subtract).then_inc(sem("z_lo"), 1)
                    x_loads += 1

                elif kind == "out":
                    if ph["mod"] == 2:
                        dve.wait_ge(sem("x_in"), 16 * KT * x_loads)
                    for k in range(2):
                        dve.wait_ge(sem(f"free{k}"), at.v(f"free{k}"))

                    def turn(i, last=False):
                        t = At(ph, i)
                        for k in range(2):
                            if not (last and k == 1):
                                split(t, k + 1)
                            dve.wait_ge(sem("product"), t.v("chunk", k + 1))
                            for u, (r0, r1) in enumerate(ranges(nt)):
                                m = ph["mod"] * KT + k
                                scalar = mods[:, bass.ds(2 * i + m, 1), u:u + 1].rearrange("p a b -> p (a b)")
                                ins = dve.scalar_tensor_tensor(
                                    out=xz[:, bass.ds(2 * i + k, 1), r0:r1], in0=pair(k)[:, r0:r1].unsqueeze(1),
                                    scalar=scalar, in1=xz[:, bass.ds(2 * i + k, 1), r0:r1], op0=ALU.mult, op1=ALU.add)
                            ins.then_inc(sem(f"free{k}"), 1)
                    if at.v("chunk") + 2 * turns < NCHUNK:
                        with dve.Fori(0, turns) as i:
                            turn(i)
                    else:
                        with dve.Fori(0, turns - 1) as i:
                            turn(i)
                        turn(turns - 1, last=True)

                elif kind == "ffn":
                    with dve.Fori(0, turns) as i:
                        t = At(ph, i)
                        for k in range(2):
                            split(t, 2 * k + 1)
                            split(t, 2 * k + 2)
                            dve.wait_ge(sem("free0"), t.v("free0", k + 1))
                            dve.wait_ge(sem("product"), t.v("chunk", 2 * k + 2))
                            dve.wait_ge(sem("f_lo"), t.v("f_lo", k - 1))
                            dve.tensor_tensor(prob[:, k, 0:nt], pair(1)[:, 0:nt], tmp[:, k, 0:nt],
                                              ALU.mult).then_inc(sem("free1"), 1)

                elif kind == "final":
                    dve.wait_ge(sem("n_std"), at.v("n_std", 1))
                    dve.reciprocal(tmp[:, 2, 0:nt], tmp[:, 2, 0:nt]).then_inc(sem("n_rstd"), 1)
                    dve.wait_ge(sem("n_rstd"), at.v("n_rstd", 1))
                    for t in range(KT):
                        dve.scalar_tensor_tensor(out=xz[:, t, 0:nt], in0=xz[:, t, 0:nt],
                                                 scalar=gains[:, G_FINAL + t:G_FINAL + t + 1],
                                                 in1=tmp[:, 2, 0:nt], op0=ALU.mult, op1=ALU.mult).then_inc(
                            sem("o_ready"), 1)

        @block.gpsimd
        def _(pool):
            def attend(at, ka, nt):
                nq, a0 = nt // P, ka * (nt // P)
                for n in range(nq):
                    w = TOK if n < 4 else CTX
                    pool.wait_ge(sem("s_rinv"), at.v("s_rinv", a0 + n + 1))
                    pool.tensor_tensor(prob[:, n % 3, 0:w], prob[:, n % 3, 0:w],
                                       ri[:, n:n + 1].to_broadcast([P, w]), ALU.mult).then_inc(sem("s_pn"), 1)

            for k in range(2):
                pool.memset(mark[:, k:k + 1], 0.0).then_inc(sem("f_lo"), 1)
            for ph in PHASES:
                kind, layer, at = ph["kind"], ph["layer"], At(ph)
                nt, turns = ph.get("nt"), ph["turns"]
                if kind == "norm":
                    for t in range(KT):
                        pool.wait_ge(sem("n_hi"), at.v("n_hi", t + 1))
                        pool.wait_ge(sem("n_full"), at.v("n_full", t + 1))
                        pool.tensor_tensor(hl[:, t, 0:nt], prob[:, t % 2, 0:nt], hh[:, t, 0:nt].bitcast(F32),
                                           ALU.subtract).then_inc(sem("n_lo"), 1)
                elif kind == "mla":
                    with pool.Fori(0, turns) as i:
                        attend(At(ph, i), 0, nt)
                elif kind == "gqa":
                    with pool.Fori(0, turns) as i:
                        for k in range(2):
                            attend(At(ph, i), k, nt)
                elif kind == "ret":
                    units = 8 if nt > LAT else 6
                    with pool.Fori(0, turns) as i:
                        t = At(ph, i)
                        for u in range(units):
                            w = LAT if u < 6 else CTX
                            pool.wait_ge(sem("rs_hi"), t.v("rs_hi", u + 1))
                            cols = slice((u % 3) * LAT, (u % 3) * LAT + w)
                            pool.tensor_tensor(ptl_f[:, cols], prob[:, u % 3, 0:w], pth_f[:, cols].bitcast(F32),
                                               ALU.subtract).then_inc(sem("rs_lo"), 1)
                elif kind == "ffn":
                    with pool.Fori(0, turns) as i:
                        t = At(ph, i)
                        for k in range(2):
                            pool.wait_ge(sem("f_hi"), t.v("f_hi", k + 1))
                            pool.tensor_tensor(yl[:, bass.ds(2 * i + k, 1), 0:nt], prob[:, k:k + 1, 0:nt],
                                               yh[:, bass.ds(2 * i + k, 1), 0:nt].bitcast(F32), ALU.subtract).then_inc(
                                sem("f_lo"), 1)

        @block.tensor
        def _(pe):
            def three(outs, lhs, rhs, start, stop):
                for n, (w, x) in enumerate(((0, 0), (0, 1), (1, 0))):
                    for out, cols in outs:
                        ins = pe.matmul(out, lhs[w], rhs[x](cols), start=start and n == 0, stop=stop and n == 2)
                return ins

            def project(at, kc, slot, kfree, mov, kts, nt, cut, rows=P, kt0=0, ktn=None, last=True):
                s = at.slot(kc)
                if kfree is not None and (at.base.get(f"free{slot}", 0) + kfree > 0 or not isinstance(at.i, int)):
                    pe.wait_ge(sem(f"free{slot}"), at.v(f"free{slot}", kfree))
                pe.wait_ge(sem("w_lo"), at.v("chunk", kc + 1))
                for kt in range(kts):
                    g = kt0 + kt
                    outs = [(pair(slot)[0:rows, r0:r1], (r0, r1)) for r0, r1 in ranges(nt)]
                    ins = three(outs, [w[:, s, cut(kt)] for w in (wh, wl)],
                                [lambda c, x=x: x(g, c) for x in mov], g == 0, g == (ktn or kts) - 1)
                ins.then_inc(sem("product"), 1)
                return ins

            def project_v(at, kc, slot, kfree, src, kts, cut):
                s = at.slot(kc)
                pe.wait_ge(sem(f"free{slot}"), at.v(f"free{slot}", kfree))
                pe.wait_ge(sem("w_lo"), at.v("chunk", kc + 1))
                for tt in range(TOK // P):
                    for kt in range(kts):
                        out = pair(slot)[:, tt * P:(tt + 1) * P]
                        ins = three([(out, None)], [x(kt, (tt * P, (tt + 1) * P)) for x in src],
                                    [lambda c, w=w: w[:, s, cut(kt)] for w in (wh, wl)], kt == 0, kt == kts - 1)
                return ins

            H = [lambda k, c, x=x: x[:, k, c[0]:c[1]] for x in (hh, hl)]
            Y = [lambda k, c, x=x: x[:, k, c[0]:c[1]] for x in (yh, yl)]
            R = [[lambda k, c, j=j, x=x: ranks[:, j, x, k, c[0]:c[1]] for x in range(2)] for j in range(2)]
            whole = lambda kt: slice(kt * P, (kt + 1) * P)

            def stats(at, src, slots, nt, k):
                for n, x in enumerate(slots):
                    for r0, r1 in ranges(nt):
                        ins = pe.matmul(pair(AUX)[:, r0:r1], ones[:, :], src[:, x, r0:r1], start=n == 0,
                                        stop=n == len(slots) - 1)
                ins.then_inc(sem("v_stat"), 1)

            def rotate(which, rows):
                pe.matmul(ps[0:rows, 6 * BANK:7 * BANK], perm[0:rows, which, 0:rows], tmp[0:rows, 0, 0:LAT],
                          start=True, stop=True).then_inc(sem("v_perm"), 1)

            def attend(at, ka, nt, rows):
                nq, a0, b0 = nt // P, ka * (nt // P), ka * (nt // P) // 2
                for n in range(nq + 2):
                    if n < nq:
                        lat = n < 4
                        k0 = 0 if lat else LAT
                        if n >= 2:
                            pe.wait_ge(sem("s_exp"), at.v("s_exp", a0 + n - 1))
                        base = (4 + 2 * (n % 2)) * BANK
                        spans = [(0, LAT), (LAT, TOK)] if lat else [(LAT, TOK)]
                        outs = [(ps[:, base + c0 - k0:base + c1 - k0], (c0, c1)) for c0, c1 in spans]
                        three(outs, [q[0:rows, n * P:(n + 1) * P] for q in (qh, ql)],
                              [lambda c, x=x: x[0:rows, c[0]:c[1]] for x in (kh, kl)], True, True).then_inc(
                            sem("s_ready"), 1)
                    m = n - 2
                    if 0 <= m < nq:
                        st = 6 if m < 4 else 2
                        pe.wait_ge(sem("s_pn"), at.v("s_pn", a0 + m + 1))
                        if m:
                            pe.wait_ge(sem("t_lo"), at.v("t_lo", a0 + m))
                        for s in range(st):
                            ins = pe.transpose(pair(1)[:, s * P:(s + 1) * P], prob[:, m % 3, s * P:(s + 1) * P],
                                               ident[:, :])
                        ins.then_inc(sem("t_ready"), 1)
                    b = n // 2 - 2
                    if n % 2 == 0 and b >= 0:
                        values(at, a0, b0, b)
                values(at, a0, b0, nq // 2 - 1)
                pe.wait_ge(sem("y_lo"), at.v("y_lo", b0 + nq // 2))

            def values(at, a0, b0, b):
                lat = b < 2
                st, v0 = (6, 0) if lat else (2, 4)
                pe.wait_ge(sem("t_lo"), at.v("t_lo", a0 + 2 * b + 2))
                cols = (2 * P * b, 2 * P * (b + 1))
                for s in range(st):
                    ins = three([(pair(0)[:, cols[0]:cols[1]], None)],
                                [v[:, 0, (v0 + s) * P:(v0 + s + 1) * P] for v in (vh, vl)],
                                [lambda c, x=x: x[:, s, :] for x in (pth, ptl)], s == 0, s == st - 1)
                ins.then_inc(sem("y_ready"), 1)

            pe.wait_ge(sem("c_lo"), 1)
            pe.wait_ge(sem("ones_set"), 1)

            for ph in PHASES:
                kind, layer, at = ph["kind"], ph["layer"], At(ph)
                nt, turns = ph.get("nt"), ph["turns"]
                if kind == "mod":
                    with pe.Fori(0, turns) as i:
                        t = At(ph, i)
                        for k in range(2):
                            s = t.slot(k)
                            pe.wait_ge(sem("w_lo"), t.v("chunk", k + 1))
                            out = ps[:, bass.ds(4 * i + (7 * BANK + 2 * k), 2)]
                            for kt in range(KT):
                                ins = three([(out, None)], [w[:, s, whole(kt)] for w in (wh, wl)],
                                            [lambda c, x=x: x[:, kt, :] for x in (ch, cl)], kt == 0, kt == KT - 1)
                            ins.then_inc(sem("product"), 1)

                elif kind in ("norm", "final"):
                    for t in range(KT):
                        pe.wait_ge(sem("sq"), at.v("sq", t + 1))
                        for r0, r1 in ranges(nt):
                            ins = pe.matmul(pair(AUX)[:, r0:r1], ones[:, :], tmp[:, t % 2, r0:r1], start=t == 0,
                                            stop=t == KT - 1)
                        ins.then_inc(sem("sq_used"), 1)
                    if kind == "norm":
                        pe.wait_ge(sem("n_lo"), at.v("n_lo", KT))

                elif kind == "mla_in":
                    for j, nt_j in enumerate((TOK if layer < DEPTH - 1 else LAT, TOK)):
                        for k in range(RKT):
                            project(at, 2 * j + k, k, j, H, KT, nt_j, whole)
                        for k in range(RKT):
                            pe.wait_ge(sem(f"free{k}"), at.v(f"free{k}", j + 1))
                        stats(at, prob, (0, 1), nt_j, j)
                    cut = lambda kt: slice(kt * P, kt * P + MLA_QK)
                    project(at, 4, 0, 2, H, KT // 2, TOK, cut, rows=MLA_QK, ktn=KT)
                    project(at, 5, 0, None, H, KT // 2, TOK, cut, rows=MLA_QK, kt0=KT // 2, ktn=KT)
                    pe.wait_ge(sem("free0"), at.v("free0", 3))
                    rotate(1, MLA_QK)

                elif kind == "mla":
                    pe.wait_ge(sem("v_lo"), at.v("v_lo"))
                    with pe.Fori(0, turns) as i:
                        t = At(ph, i)
                        s = t.slot(0)
                        pe.wait_ge(sem("free0"), t.v("free0"))
                        pe.wait_ge(sem("w_lo"), t.v("chunk", 1))
                        for kt in range(RKT):
                            ins = three([(pair(0)[:, r0:r1], (r0, r1)) for r0, r1 in ranges(TOK)],
                                        [w[:, s, kt * 256:kt * 256 + P] for w in (wh, wl)],
                                        [lambda c, x=x: x(kt, c) for x in R[1]], kt == 0, kt == RKT - 1)
                        ins.then_inc(sem("k_ready"), 1)
                        project_v(t, 0, 1, 0, R[1], RKT, lambda kt: slice(kt * 256 + 64, kt * 256 + 192)).then_inc(
                            sem("product"), 1)
                        project(t, 1, 0, 1, R[0], RKT, nt, lambda kt: slice(kt * P, kt * P + MLA_QK), rows=MLA_QK)
                        pe.wait_ge(sem("free0"), t.v("free0", 2))
                        rotate(1, MLA_QK)
                        pe.wait_ge(sem("v_lo"), t.v("v_lo", 1))
                        pe.wait_ge(sem("free1"), t.v("free1", 1))
                        attend(t, 0, nt, MLA_QK)

                elif kind == "gqa_kv":
                    project(at, 0, 0, 0, H, KT, TOK, whole)
                    pe.wait_ge(sem("free0"), at.v("free0", 1))
                    stats(at, tmp, (1,), TOK, 0)
                    project_v(at, 1, 1, 0, H, KT, whole).then_inc(sem("product"), 1)
                    pe.wait_ge(sem("v_norm"), at.v("v_norm", 1))
                    rotate(0, P)
                    pe.wait_ge(sem("free1"), at.v("free1", 1))

                elif kind == "gqa":
                    with pe.Fori(0, turns) as i:
                        t = At(ph, i)
                        for k in range(2):
                            project(t, k, 0, k, H, KT, nt, whole)
                            pe.wait_ge(sem("free0"), t.v("free0", k + 1))
                            stats(t, tmp, (1,), nt, k)
                            pe.wait_ge(sem("v_norm"), t.v("v_norm", k + 1))
                            rotate(0, P)
                            pe.wait_ge(sem("v_lo"), t.v("v_lo", k + 1))
                            attend(t, k, nt, P)

                elif kind == "merge":
                    pe.wait_ge(sem("v_lo"), at.v("v_lo"))
                    pe.wait_ge(sem("y_lo"), at.v("y_lo"))
                    with pe.Fori(0, turns) as i:
                        t = At(ph, i)
                        for k in range(2):
                            project(t, 2 * k, 0, k, H, KT, nt, whole)
                            project(t, 2 * k + 1, 1, k, Y, KT, nt, whole)

                elif kind == "ret":
                    units = 8 if nt > LAT else 6
                    with pe.Fori(0, turns) as i:
                        t = At(ph, i)
                        project(t, 0, 0, 0, H, KT, nt, whole)
                        project(t, 1, 1, 0, H, KT, TOK, whole)
                        pe.wait_ge(sem("free0"), t.v("free0", 1))
                        rotate(0, P)
                        project_v(t, 2, 0, 1, H, KT, whole).then_inc(sem("product"), 1)
                        pe.wait_ge(sem("free1"), t.v("free1", 1))
                        pe.wait_ge(sem("v_s"), t.v("v_s", 1))
                        rotate(0, P)
                        project_v(t, 3, 1, 1, H, KT, whole).then_inc(sem("product"), 1)
                        pe.wait_ge(sem("v_lo"), t.v("v_lo", 2))
                        for e in range(2):
                            pe.wait_ge(sem(f"free{e}"), t.v(f"free{e}", 2))

                        def span(u):
                            return (0, LAT) if u < 6 else (LAT, TOK)

                        def score(u):
                            if u >= 3:
                                pe.wait_ge(sem("rs_sd"), t.v("rs_sd", u - 2))
                            tile = u if u < 6 else u - 2
                            r0, r1 = span(u)
                            three([(ps[:, (4 + u % 3) * BANK:(4 + u % 3) * BANK + r1 - r0], (r0, r1))],
                                  [x[:, tile * P:(tile + 1) * P] for x in (kh, kl)],
                                  [lambda c, x=x: x[:, c[0]:c[1]] for x in (qh, ql)], True, True).then_inc(
                                sem("rs_ready"), 1)

                        score(0)
                        score(1)
                        for u in range(units):
                            if u + 2 < units:
                                score(u + 2)
                            pe.wait_ge(sem("rs_lo"), t.v("rs_lo", u + 1))
                            tile = u if u < 6 else u - 2
                            r0, r1 = span(u)
                            for e in range(2):
                                ins = three([(pair(e)[:, r0:r1], None)],
                                            [v[:, e, tile * P:(tile + 1) * P] for v in (vh, vl)],
                                            [lambda c, x=x: x[:, (u % 3) * LAT:(u % 3) * LAT + r1 - r0]
                                             for x in (pth_f, ptl_f)], u in (0, 6), u in (5, 7))
                            ins.then_inc(sem("rs_used"), 1)
                        for e in range(2):
                            pe.wait_ge(sem(f"free{e}"), t.v(f"free{e}", 3))
                        stats(t, prob, (0, 1), nt, 0)
                        for e in range(2):
                            project(t, 4 + e, e, 3, H, KT, nt, whole)

                elif kind == "out":
                    if ph["mod"] == 2:
                        pe.wait_ge(sem("z_lo"), at.v("z_lo"))
                    else:
                        pe.wait_ge(sem("f_lo"), at.v("f_lo"))
                    with pe.Fori(0, turns) as i:
                        t = At(ph, i)
                        for k in range(2):
                            project(t, k, k, 0, Y, ph["kt"], nt, whole)

                elif kind == "ffn":
                    with pe.Fori(0, turns) as i:
                        t = At(ph, i)
                        for k in range(2):
                            for j in range(2):
                                project(t, 2 * k + j, j, k, H, KT, nt, whole)


def rope_table(dim, lead):
    half = dim // 4
    inv = (ROPE_BASE ** (-np.arange(half) / half)).astype(np.float32)
    tok = np.arange(LAT)
    c, s = np.ones((P, LAT)), np.zeros((P, LAT))
    for part, pos in enumerate((tok // GRID_W, tok % GRID_W)):
        ang = (inv[:, None] * pos[None, :].astype(np.float32)).astype(np.float64)
        for h in range(2):
            rows = slice(lead + (2 * part + h) * half, lead + (2 * part + h + 1) * half)
            c[rows], s[rows] = np.cos(ang), np.sin(ang)
    return np.stack([c, s], 1).astype(np.float32)


def perm_table(dim, lead):
    half = dim // 4
    m = np.zeros((P, P), np.float32)
    for part in range(2):
        for r in range(half):
            lo, hi = lead + 2 * part * half + r, lead + (2 * part + 1) * half + r
            m[hi, lo], m[lo, hi] = -1.0, 1.0
    return m


def decay_table():
    out = np.zeros((RET_HEADS, P, DEC), np.float64)
    p = np.arange(P)[:, None]
    for h in range(RET_HEADS):
        f, b = (np.log1p(-np.exp2(-(5.0 + off) - h)) for off in (0.0, 0.5))
        d = np.arange(DEC1)[None, :] - 3 * P - p
        out[h, :, :DEC1] = np.exp(f * np.maximum(d, 0)) * (d >= 0) + np.exp(b * np.maximum(-d, 0)) * (d <= 0)
        d = np.arange(DEC2)[None, :] - P - p
        out[h, :, DEC1:] = np.exp(f * (CTX + d)) + np.exp(b * (LAT - d))
    return out.astype(np.float32)


def stream_of(w):
    out = np.zeros((NCHUNK, P, CH), np.float32)
    n = 0

    def put(m, at=0, step=P):
        nonlocal n
        kt, cols = m.shape[0] // P, m.shape[1]
        out[n].reshape(P, CH // step, step)[:, :kt, at:at + cols] = m.reshape(kt, P, cols).transpose(1, 0, 2)
        n += 1

    for layer in range(DEPTH):
        win = w["w_in"][layer]
        col = lambda o, k=0, c=P: win[:, o + k * P:o + k * P + c]
        for j in range(N_MOD * KT):
            put(w["w_mod"][layer][:, j * P:(j + 1) * P])
        for o in (O_CQ, O_CKV):
            for k in range(RKT):
                put(col(o, k))
        for k in range(2):
            put(col(O_KR, 0, MLA_ROPE)[k * D // 2:(k + 1) * D // 2], at=MLA_NOPE)
        for h in range(MLA_HEADS):
            step = MLA_NOPE + MLA_V
            put(w["w_mla_kvb"][layer][:, h * step:(h + 1) * step], step=256)
            put(w["w_mla_qb"][layer][:, h * MLA_QK:(h + 1) * MLA_QK])

        def merge(branch, name):
            for m in range(KT):
                put(col(O_GATE + branch * D, m))
                put(w[name][layer][:, m * P:(m + 1) * P])

        merge(1, "w_mla_o")
        for kv in range(GQA_KV):
            put(col(O_GK, kv))
            put(col(O_GV, kv))
            for h in range(GQA_HEADS // GQA_KV):
                put(col(O_GQ, kv * GQA_HEADS // GQA_KV + h))
        merge(2, "w_gqa_o")
        for h in range(RET_HEADS):
            put(col(O_RQ, h))
            put(col(O_RK, h))
            for o in (O_RV, O_RG):
                for e in range(2):
                    put(col(o, 2 * h + e))
        merge(0, "w_ret_o")
        for m in range(KT):
            put(w["w_out"][layer][:, m * P:(m + 1) * P])
        for t0, tiles in GROUPS:
            for t in range(t0, t0 + tiles):
                for half in range(2):
                    put(w["w_ffn_in"][layer][:, half * FFN + t * P:half * FFN + (t + 1) * P])
            for m in range(KT):
                put(w["w_ffn_out"][layer][t0 * P:(t0 + tiles) * P, m * P:(m + 1) * P])
    assert n == NCHUNK
    return out


def kernel(**inputs):
    import concourse.bacc as bacc
    from concourse.bass_utils import run_bass_kernel_spmd as run

    w = {name: np.asarray(x) for name, x in inputs.items()}

    def tiles(v):
        return v.reshape(-1, P).T

    gains = [tiles(w[name][layer]) for layer in range(DEPTH)
             for name in ("g_mix", "g_ffn", "g_mla_q", "g_mla_kv", "g_gqa_q", "g_gqa_k")] + [tiles(w["g_final"])]
    arrays = {
        "xT": np.ascontiguousarray(np.concatenate([w["x"][0], w["ctx"][0]], 0).T),
        "cvec": np.ascontiguousarray(np.stack([tiles(w["c"][0]), tiles(w["c_ctx"])], 2)),
        "bmod": np.ascontiguousarray(np.stack([tiles(b) for b in w["b_mod"]], 1)),
        "gains": np.ascontiguousarray(np.concatenate(gains, 1)),
        "stream": stream_of(w),
        "rope": np.stack([rope_table(RET_DK, 0), rope_table(MLA_ROPE, MLA_NOPE)]),
        "perm": np.ascontiguousarray(np.stack([perm_table(RET_DK, 0), perm_table(MLA_ROPE, MLA_NOPE)], 1)),
        "ident": np.eye(P, dtype=np.float32),
        "dec": decay_table(),
    }
    nc = bacc.Bacc("TRN2", target_bir_lowering=False, num_devices=1, dynamic_dma_scratch_size=1024)
    a = {name: nc.dram_tensor(f"in_{name}", x.shape, mybir.dt.from_np(x.dtype), kind="ExternalInput").ap()
         for name, x in arrays.items()}
    a["out"] = nc.dram_tensor("out", (D, LAT), F32, kind="ExternalOutput").ap()
    build(nc, a)
    r = run(nc, [{f"in_{name}": x for name, x in arrays.items()}], core_ids=[0])
    return np.ascontiguousarray(r.results[0]["out"].T)[None]
```

```python
from contextlib import ExitStack

import numpy as np

import concourse.bass as bass
from concourse import mybir

F32 = mybir.dt.float32
F32R = mybir.dt.float32r
ALU = mybir.AluOpType
ACT = mybir.ActivationFunctionType
AX = mybir.AxisListType

P = 128
D = 1024
LAT = 512
CTX = 256
TOK = LAT + CTX
DEPTH = 2
KT = D // P
GRID_W = 64
ROPE_BASE = 10000.0
EPS = 1e-6

RET_HEADS, RET_DK, RET_DV = 4, 128, 256
MLA_HEADS, MLA_RANK, MLA_NOPE, MLA_ROPE, MLA_V = 8, 256, 64, 32, 128
MLA_QK = MLA_NOPE + MLA_ROPE
RKT = MLA_RANK // P
GQA_HEADS, GQA_KV, GQA_HD = 8, 2, 128
FFN = 2816
FT = FFN // P
GROUPS = [(0, 8), (8, 8), (16, 6)]
N_MOD = 6
CH = KT * P

O_RQ = 0
O_RK = O_RQ + RET_HEADS * RET_DK
O_RV = O_RK + RET_HEADS * RET_DK
O_RG = O_RV + RET_HEADS * RET_DV
O_CQ = O_RG + RET_HEADS * RET_DV
O_CKV = O_CQ + MLA_RANK
O_KR = O_CKV + MLA_RANK
O_GQ = O_KR + MLA_ROPE
O_GK = O_GQ + GQA_HEADS * GQA_HD
O_GV = O_GK + GQA_KV * GQA_HD
O_GATE = O_GV + GQA_KV * GQA_HD

G_LAYER = 2 * KT + 2 * RKT + 2
G_FINAL = DEPTH * G_LAYER
NGAIN = G_FINAL + KT

DEC1 = LAT + 3 * P
DEC2 = LAT + P
DEC = DEC1 + DEC2


def add(a, b, times=1):
    out = dict(a)
    for name, n in b.items():
        out[name] = out.get(name, 0) + n * times
    return out


PLAIN = {"e_hi": 1}
ROPED = {"v_perm": 1, "v_c": 1, "v_s": 1, "v_full": 1, "v_hi": 1, "v_lo": 1}
NORMED = {"v_stat": 1, "v_std": 1, "v_rstd": 1, "v_norm": 1}


def attention(nq):
    return {"s_ready": nq, "s_max": nq, "s_nm": nq, "s_exp": nq, "s_rinv": nq, "s_pn": nq,
            "t_ready": nq, "t_hi": nq, "t_lo": nq, "y_ready": nq // 2, "y_hi": nq // 2, "y_lo": nq // 2}


def total(*parts):
    out = {}
    for part in parts:
        out = add(out, part)
    return out


def plan():
    phases, now = [], {"f_lo": 2, "y_lo": 1}

    def phase(kind, layer, turns, per, once=(), **args):
        nonlocal now
        once = dict(once)
        phases.append(dict(kind=kind, layer=layer, turns=turns, per=per, base=dict(now), once=once, **args))
        now = add(add(now, once), per, turns)

    for layer in range(DEPTH):
        full = layer < DEPTH - 1
        nt = TOK if full else LAT
        nq = nt // P
        units = 8 if full else 6
        norm = {"sq": KT, "sq_used": KT, "n_std": 1, "n_rstd": 1, "n_t1": KT, "n_hi": KT, "n_full": KT, "n_lo": KT}
        if layer == 0:
            phase("mod", layer, KT, {"chunk": 2})
        phase("mods", layer, 0, {}, {"mod": 2 if layer == 0 else 3})
        phase("norm", layer, 0, {}, norm, nt=TOK, first=True)
        phase("mla_in", layer, 0, {}, total(
            {"chunk": 6, "free0": 3, "free1": 2, "v_stat": 2, "v_std": 2, "v_rstd": 2,
             "v_norm": 4, "v_hi": 5, "v_lo": 5, "tab": 1}, ROPED))
        nmod = 4 if layer == 0 else 0
        head = total({"chunk": 2 + nmod, "free0": 3, "k_ready": 1}, PLAIN, PLAIN, ROPED)
        att = attention(nq)
        phase("mla_first", layer, 0, {}, head, nt=nt, nmod=nmod)
        phase("mla", layer, MLA_HEADS // 2 - 1, total(head, head, att, att), nt=nt, nmod=nmod)
        phase("mla_last", layer, 0, {}, total(head, att, att), nt=nt, nmod=nmod)
        if layer == 0:
            phase("mods", layer, 0, {}, {"mod": 2}, rest=True)
        merge = {"chunk": 4, "free0": 2, "free1": 2, "mg_add": 2}
        phase("merge", layer, KT // 2, add(merge, {"mg_add": -2}), nt=nt, branch=1, first=True)
        query = total({"chunk": 1, "free0": 1, "v_stat": 1, "v_std": 1, "v_rstd": 1, "v_norm": 1}, ROPED)
        phase("gqa", layer, GQA_KV, total({"chunk": 2, "free0": 1, "free1": 1}, PLAIN, ROPED, NORMED,
                                          *[query] * 4, *[att] * 4), {"tab": 1}, nt=nt)
        phase("merge", layer, KT // 2, merge, nt=nt, branch=2, first=False)
        phase("ret", layer, RET_HEADS, total(
            {"chunk": 6, "free0": 4, "free1": 4, "dec": 1, "rs_ready": units, "rs_sd": units,
             "rs_hi": units, "rs_lo": units, "rs_used": units, "v_stat": 1, "v_std": 1, "v_rstd": 1,
             "v_norm": 2, "v_full": 2, "v_hi": 2, "v_lo": 2}, ROPED, ROPED, PLAIN), nt=nt)
        phase("merge", layer, KT // 2, merge, nt=nt, branch=0, first=False)
        phase("z", layer, 0, {}, {"z_hi": KT, "z_lo": KT}, nt=nt)
        phase("out", layer, KT // 2, {"chunk": 2, "free0": 1, "free1": 1},
              nt=nt, kt=KT, mod=2, nmod=0)
        phase("norm", layer, 0, {}, norm, nt=nt, first=False)
        for g, (t0, n) in enumerate(GROUPS):
            phase("ffn", layer, n // 2, {"chunk": 4, "free0": 2, "free1": 2, "f_hi": 2, "f_lo": 2},
                  nt=nt)
            nmod = 2 if layer == 0 else 0
            phase("out", layer, KT // 2, {"chunk": 2 + 2 * nmod, "free0": 1, "free1": 1},
                  nt=nt, kt=n, mod=5, group=g, nmod=nmod)
    phase("final", DEPTH - 1, 0, {}, {}, nt=LAT)
    return phases, now


PHASES, TOTALS = plan()
NCHUNK = TOTALS["chunk"]


class At:

    def __init__(self, ph, i=0, end=False):
        self.base, self.per, self.i = ph["base"], ph["per"], i
        if end:
            self.base, self.i = add(add(ph["base"], ph["once"]), ph["per"], ph["turns"]), 0

    def v(self, name, k=0):
        per = self.per.get(name, 0)
        at = self.base.get(name, 0) + k
        return at + self.i * per if per else at

    def slot(self, k):
        return (self.base.get("chunk", 0) + k) % 2

    def half(self, k):
        return (self.base.get("chunk", 0) + k) // 2 + 1 + self.i * (self.per.get("chunk", 0) // 2)


def ranges(nt):
    return [(0, LAT)] + ([(LAT, nt)] if nt > LAT else [])


def build(nc, a):
    ctx = ExitStack()
    with ctx:
        def sb(name, shape, dt=F32):
            return ctx.enter_context(nc.sbuf_tensor(name, shape, dt))

        sems = {}

        def sem(name):
            if name not in sems:
                sems[name] = ctx.enter_context(nc.semaphore(name))
            return sems[name]

        at = (nc.sbuf_base + 31) // 32 * 32
        arena = sb("arena", [P, KT * TOK + 8])
        xz = nc.alloc_sbuf_tensor_at("xz", [P, KT, TOK], F32, offset=at)
        ranks = nc.alloc_sbuf_tensor_at("ranks", [P, 2, 2, RKT, TOK], F32R, offset=at)
        hh, hl = sb("hh", [P, KT, TOK], F32R), sb("hl", [P, KT, TOK], F32R)
        yh, yl = sb("yh", [P, KT, TOK], F32R), sb("yl", [P, KT, TOK], F32R)
        raw = sb("raw", [P, 2, CH])
        wh, wl = sb("wh", [P, 2, CH], F32R), sb("wl", [P, 2, CH], F32R)
        kh, kl = sb("kh", [P, TOK], F32R), sb("kl", [P, TOK], F32R)
        qh, ql = sb("qh", [P, TOK], F32R), sb("ql", [P, TOK], F32R)
        q2h, q2l = sb("q2h", [P, TOK], F32R), sb("q2l", [P, TOK], F32R)
        vh, vl = sb("vh", [P, 2, TOK], F32R), sb("vl", [P, 2, TOK], F32R)
        tmp = sb("tmp", [P, 3, TOK])
        prob = sb("prob", [P, 3, TOK])
        pth, ptl = sb("pth", [P, 6, 2 * P], F32R), sb("ptl", [P, 6, 2 * P], F32R)
        rope = sb("rope", [P, 2, LAT])
        at = (nc.sbuf_base + 31) // 32 * 32
        fence = sb("fence", [P, DEC + 8])
        dec = nc.alloc_sbuf_tensor_at("dec", [P, DEC], F32, offset=at)
        k2h = nc.alloc_sbuf_tensor_at("k2h", [P, TOK], F32R, offset=at)
        k2l = nc.alloc_sbuf_tensor_at("k2l", [P, TOK], F32R, offset=at + 4 * TOK)
        keys, queries = ((kh, kl), (k2h, k2l)), ((qh, ql), (q2h, q2l))
        perm = sb("perm", [P, 2, P])
        ident, ones = sb("ident", [P, P]), sb("ones", [P, P])
        eps = sb("eps", [P, 1])
        gains = sb("gains", [P, NGAIN])
        bmod = sb("bmod", [P, DEPTH, N_MOD * KT])
        cvec, csil = sb("cvec", [P, KT, 2]), sb("csil", [P, KT, 2])
        ch, cl = sb("ch", [P, KT, 2], F32R), sb("cl", [P, KT, 2], F32R)
        mods = sb("mods", [P, N_MOD * KT, 2])
        gm = sb("gm", [P, 2, KT, 2])
        mx, nm = sb("mx", [P, 6]), sb("nm", [P, 6])
        mark = sb("mark", [P, 3])
        rs, ri = sb("rs", [P, 6]), sb("ri", [P, 6])
        qsc = sb("qsc", [P, 2, 6])
        ps = ctx.enter_context(nc.psum_tensor("ps", [P, 8 * LAT], F32))
        BANK = LAT

        def pair(slot):
            return ps[:, 2 * BANK * slot:2 * BANK * slot + TOK]

        AUX = 2
        TURN = 0
        TRANS = 2 * BANK
        OUTS = TRANS + TOK
        SCORES = (4 * BANK, 6 * BANK)
        QSUM = TOK
        MODS = (TOK + P, 7 * BANK)

        vh_f = vh[:, :, :].rearrange("p a b -> p (a b)")
        vl_f = vl[:, :, :].rearrange("p a b -> p (a b)")
        pth_f = pth[:, :, :].rearrange("p a b -> p (a b)")
        ptl_f = ptl[:, :, :].rearrange("p a b -> p (a b)")
        xspill = nc.dram_tensor("xspill", (D, TOK), F32, kind="Internal").ap()

        block = ctx.enter_context(nc.Block())

        @block.sync
        def _(sp):
            for s in range(2):
                sp.dma_start(raw[:, s, :], a["stream"][s]).then_inc(sem(f"raw_in{s}"), 16)
            with sp.Fori(1, NCHUNK // 2) as i:
                for s in range(2):
                    sp.wait_ge(sem("w_lo"), 2 * i + (s - 1))
                    src = a["stream"][bass.ds(2 * i + s, 1)].rearrange("a p n -> (a p) n")
                    sp.dma_start(raw[:, s, :], src).then_inc(sem(f"raw_in{s}"), 16)
            sp.wait_ge(sem("out_done"), 16 * KT)

        @block.scalar
        def _(act):
            def split(at, k):
                s = at.slot(k)
                act.wait_ge(sem(f"raw_in{s}"), at.half(k) * 16)
                used = at.v("chunk", k - 1)
                if not isinstance(used, int) or used > 0:
                    act.wait_ge(sem("product"), used)
                act.activation(wh[:, s, :], raw[:, s, :], ACT.Copy).then_inc(sem("w_hi"), 1)

            def plain(at, kc, slot, dst, rows=P, nt=TOK):
                act.wait_ge(sem("product"), at.v("chunk", kc + 1))
                act.activation(dst[0:rows, 0:nt], pair(slot)[0:rows, 0:nt], ACT.Copy).then_inc(sem("e_hi"), 1)

            def std(at, k, nt, n, rows=P):
                act.wait_ge(sem("v_stat"), at.v("v_stat", k + 1))
                act.activation(tmp[0:rows, 2, 0:nt], pair(AUX)[0:rows, 0:nt], ACT.Sqrt, bias=eps[0:rows, :],
                               scale=1.0 / n).then_inc(sem("v_std"), 1)

            def roped(at, kc, kv, kf, slot, dst, rows, r0, nt, scale=1.0, kn=None):
                act.wait_ge(sem("product"), at.v("chunk", kc + 1))
                act.wait_ge(sem("v_lo"), at.v("v_lo", kv))
                if kn is None:
                    act.activation(tmp[0:rows, 0, 0:nt], pair(slot)[0:rows, 0:nt], ACT.Copy,
                                   scale=scale).then_inc(sem(f"free{slot}"), 1)
                else:
                    act.activation(tmp[0:rows, 0, 0:nt], pair(slot)[0:rows, 0:nt], ACT.Copy)
                    act.activation(tmp[0:rows, 1, 0:nt], pair(slot)[0:rows, 0:nt],
                                   ACT.Square).then_inc(sem(f"free{slot}"), 1)
                    std(at, kn, nt, GQA_HD)
                act.wait_ge(sem("v_full"), at.v("v_full", kf + 1))
                act.activation(dst[r0:rows, 0:nt], tmp[r0:rows, 0, 0:nt], ACT.Copy).then_inc(sem("v_hi"), 1)

            def attend(at, ka, nt, scale, head, fill=lambda n: None):
                nq, a0, b0 = nt // P, ka * (nt // P), ka * (nt // P) // 2
                for n in range(nq + 2):
                    if n > 3 and n % 2 == 0:
                        y_hi(at, b0, n // 2 - 2, head)
                    if n < nq:
                        w = TOK if n < 4 else CTX
                        act.wait_ge(sem("s_nm"), at.v("s_nm", a0 + n + 1))
                        if n >= 3:
                            act.wait_ge(sem("t_ready"), at.v("t_ready", a0 + n - 2))
                        s0 = SCORES[n % 2]
                        act.activation(prob[:, n % 3, 0:w], ps[:, s0:s0 + w], ACT.Exp, bias=nm[:, n:n + 1],
                                       scale=scale(n), accum_out=rs[:, n:n + 1]).then_inc(sem("s_exp"), 1)
                    m = n - 2
                    if 0 <= m < nq:
                        st = 6 if m < 4 else 2
                        act.wait_ge(sem("t_ready"), at.v("t_ready", a0 + m + 1))
                        act.activation(pth[:, 0:st, (m % 2) * P:(m % 2) * P + P],
                                       ps[:, TRANS:TRANS + st * P].rearrange("p (s q) -> p s q", q=P),
                                       ACT.Copy).then_inc(sem("t_hi"), 1)
                    fill(n)
                y_hi(at, b0, nq // 2 - 1, head)

            def y_hi(at, b0, b, head):
                act.wait_ge(sem("y_ready"), at.v("y_ready", b0 + b + 1))
                act.activation(yh[:, bass.ds(head, 1), 2 * P * b:2 * P * (b + 1)], ps[:, OUTS:OUTS + 2 * P],
                               ACT.Copy).then_inc(sem("y_hi"), 1)

            def mla_head(at, kp, par, nt, nmod):
                c0 = kp * (2 + nmod)

                def fill(n):
                    if n == 0:
                        split(at, c0 + 1)
                        act.wait_ge(sem("k_ready"), at.v("k_ready", kp + 1))
                        act.activation(keys[par][0][0:MLA_NOPE, :], pair(0)[0:MLA_NOPE, :], ACT.Copy).then_inc(
                            sem("e_hi"), 1)
                    if n == 1:
                        plain(at, c0, 0, vh[:, par, :])
                    if n == 2:
                        split(at, c0 + 2)
                        act.wait_ge(sem("product"), at.v("chunk", c0 + 2))
                        act.wait_ge(sem("v_lo"), at.v("v_lo", kp))
                        act.activation(tmp[0:MLA_QK, 0, 0:nt], pair(0)[0:MLA_QK, 0:nt], ACT.Copy).then_inc(
                            sem("free0"), 1)
                    if n == 3 and nmod:
                        split(at, c0 + 3)
                    if n == 4:
                        act.wait_ge(sem("v_full"), at.v("v_full", kp + 1))
                        act.activation(queries[par][0][0:MLA_QK, 0:nt], tmp[0:MLA_QK, 0, 0:nt],
                                       ACT.Copy).then_inc(sem("v_hi"), 1)
                        if nmod:
                            split(at, c0 + 4)
                    if n == 5 and nmod:
                        split(at, c0 + 5)
                        split(at, c0 + 6)
                return fill

            def gqa_query(at, kq, par, nt, layer):
                gain = gains[:, layer * G_LAYER + 2 * KT + 2 * RKT:layer * G_LAYER + 2 * KT + 2 * RKT + 1]

                def fill(n):
                    if n == 0:
                        split(at, kq + 3)
                    if n == 2:
                        act.wait_ge(sem("product"), at.v("chunk", kq + 3))
                        act.wait_ge(sem("v_lo"), at.v("v_lo", kq + 1))
                        act.activation(tmp[:, 0, 0:nt], pair(0)[:, 0:nt], ACT.Copy, scale=gain)
                        act.activation(tmp[:, 1, 0:nt], pair(0)[:, 0:nt], ACT.Square).then_inc(sem("free0"), 1)
                    if n == 4:
                        act.wait_ge(sem("v_stat"), at.v("v_stat", kq + 2))
                        act.activation(qsc[:, par, 0:nt // P], ps[:, QSUM:QSUM + nt // P], ACT.Sqrt,
                                       bias=eps[:, :], scale=1.0 / GQA_HD).then_inc(sem("v_std"), 1)
                    if n == 5:
                        act.wait_ge(sem("v_full"), at.v("v_full", kq + 2))
                        act.activation(queries[par][0][:, 0:nt], tmp[:, 0, 0:nt], ACT.Copy).then_inc(
                            sem("v_hi"), 1)
                return fill

            def load_x(src):
                for t in range(KT):
                    act.dma_start(xz[:, t, :], src[t * P:(t + 1) * P, :]).then_inc(sem("x_in"), 16)

            act.dma_start(cvec[:, :, :], a["cvec"]).then_inc(sem("c_in"), 16)
            for dst, name in ((gains[:, :], "gains"), (bmod[:, :, :], "bmod"), (perm[:, :, :], "perm"),
                              (ident[:, :], "ident")):
                act.dma_start(dst, a[name]).then_inc(sem("const_in"), 16)
            load_x(a["xT"])
            act.wait_ge(sem("c_in"), 16)
            act.activation(csil[:, :, :], cvec[:, :, :], ACT.Silu).then_inc(sem("c_silu"), 1)
            act.wait_ge(sem("c_silu"), 1)
            act.activation(ch[:, :, :], csil[:, :, :], ACT.Copy).then_inc(sem("c_hi"), 1)
            act.wait_ge(sem("const_in"), 64)
            act.wait_ge(sem("eps_set"), 1)
            split(At(PHASES[0]), 0)
            x_loads = 1

            for ph in PHASES:
                kind, layer, at, end = ph["kind"], ph["layer"], At(ph), At(ph, end=True)
                nt, turns = ph.get("nt"), ph["turns"]
                if kind == "mod":
                    for k in range(2):
                        split(At(ph, 0), k + 1)
                    with act.Fori(1, turns) as i:
                        for k in range(2):
                            split(At(ph, i), k + 1)

                elif kind == "norm":
                    if layer == 0 and ph["first"]:
                        act.wait_ge(sem("x_in"), 16 * KT)
                    elif at.v("free0"):
                        act.wait_ge(sem("free0"), at.v("free0"))
                        act.wait_ge(sem("free1"), at.v("free1"))
                        if ph["first"]:
                            for t in range(KT):
                                act.dma_start(xspill[t * P:(t + 1) * P, :], xz[:, t, :]).then_inc(sem("x_out"), 16)
                    for t in range(KT):
                        if t >= 2:
                            act.wait_ge(sem("sq_used"), at.v("sq_used", t - 1))
                        act.activation(tmp[:, t % 2, 0:nt], xz[:, t, 0:nt], ACT.Square).then_inc(sem("sq"), 1)
                    act.wait_ge(sem("sq_used"), at.v("sq_used", KT))
                    act.activation(tmp[:, 2, 0:nt], pair(AUX)[:, 0:nt], ACT.Sqrt, bias=eps[:, :],
                                   scale=1.0 / D).then_inc(sem("n_std"), 1)
                    gi = 0 if ph["first"] else 1
                    act.wait_ge(sem("mod"), at.v("mod"))
                    for t in range(KT):
                        act.wait_ge(sem("n_t1"), at.v("n_t1", t + 1))
                        for u, (r0, r1) in enumerate(ranges(nt)):
                            ins = act.activation(hh[:, t, r0:r1], tmp[:, t % 2, r0:r1], ACT.Identity,
                                                 bias=mods[:, 3 * gi * KT + t, u:u + 1],
                                                 scale=gm[:, gi, t, u:u + 1])
                        ins.then_inc(sem("n_hi"), 1)

                elif kind == "mla_in":
                    if layer:
                        act.wait_ge(sem("x_out"), 16 * KT)
                    act.dma_start(rope[:, :, :], a["rope"][1]).then_inc(sem("tab_in"), 16)
                    for j, (nt_j, which) in enumerate(((TOK if layer < DEPTH - 1 else LAT, 0), (TOK, 1))):
                        for k in range(RKT):
                            split(at, 2 * j + k + 1)
                            act.wait_ge(sem("product"), at.v("chunk", 2 * j + k + 1))
                            if j:
                                act.wait_ge(sem("v_lo"), at.v("v_lo", 2))
                            elif k == 0:
                                act.wait_ge(sem("n_lo"), at.v("n_lo"))
                            act.activation(tmp[:, k, 0:nt_j], pair(k)[:, 0:nt_j], ACT.Copy)
                            act.activation(prob[:, k, 0:nt_j], pair(k)[:, 0:nt_j],
                                           ACT.Square).then_inc(sem(f"free{k}"), 1)
                        std(at, j, nt_j, MLA_RANK)
                        for k in range(RKT):
                            act.wait_ge(sem("v_norm"), at.v("v_norm", 2 * j + k + 1))
                            act.activation(ranks[:, which, 0, k, 0:nt_j], tmp[:, k, 0:nt_j],
                                           ACT.Copy).then_inc(sem("v_hi"), 1)
                    split(at, 5)
                    split(at, 6)
                    roped(at, 5, 4, 0, 0, kh, MLA_QK, MLA_NOPE, TOK)
                    act.activation(k2h[MLA_NOPE:MLA_QK, :], tmp[MLA_NOPE:MLA_QK, 0, :], ACT.Copy).then_inc(
                        sem("v_hi"), 1)

                elif kind == "mla_first":
                    fill = mla_head(at, 0, 0, nt, ph["nmod"])
                    for n in range(6):
                        fill(n)

                elif kind == "mla":
                    with act.Fori(0, turns) as i:
                        t = At(ph, i)
                        for k in range(2):
                            attend(t, k, nt, lambda n: MLA_QK ** -0.5, 2 * i + k,
                                   mla_head(t, k, 1 - k, nt, ph["nmod"]))

                elif kind == "mla_last":
                    attend(at, 0, nt, lambda n: MLA_QK ** -0.5, MLA_HEADS - 2, mla_head(at, 0, 1, nt, ph["nmod"]))
                    attend(at, 1, nt, lambda n: MLA_QK ** -0.5, MLA_HEADS - 1)

                elif kind == "gqa":
                    act.wait_ge(sem("free1"), at.v("free1"))
                    act.dma_start(rope[:, :, :], a["rope"][0]).then_inc(sem("tab_in"), 16)
                    with act.Fori(0, turns) as i:
                        t = At(ph, i)
                        split(t, 1)
                        roped(t, 0, 0, 0, 0, kh, P, 0, TOK, kn=0)
                        split(t, 2)
                        plain(t, 1, 1, vh[:, 0, :])
                        fills = [gqa_query(t, k, k % 2, nt, layer) for k in range(4)]
                        for n in range(6):
                            fills[0](n)
                        for k in range(4):
                            attend(t, k, nt, lambda n, par=k % 2: qsc[:, par, n:n + 1], 4 * i + k,
                                   *fills[k + 1:k + 2])

                elif kind == "merge":
                    act.wait_ge(sem("v_lo"), at.v("v_lo"))
                    act.wait_ge(sem("y_lo"), at.v("y_lo"))
                    with act.Fori(0, turns) as i:
                        t = At(ph, i)
                        for k in range(2):
                            split(t, 2 * k + 1)
                            act.wait_ge(sem("product"), t.v("chunk", 2 * k + 1))
                            act.wait_ge(sem("free1"), t.v("free1", k - 1))
                            act.activation(tmp[:, k, 0:nt], pair(0)[:, 0:nt],
                                           ACT.Sigmoid).then_inc(sem("free0"), 1)
                            split(t, 2 * k + 2)

                elif kind == "ret":
                    act.wait_ge(sem("free1"), at.v("free1"))
                    with act.Fori(0, turns) as i:
                        t = At(ph, i)
                        act.dma_start(dec[:, :], a["dec"][bass.ds(i, 1)].rearrange("a p n -> (a p) n")).then_inc(
                            sem("dec_in"), 16)
                        split(t, 1)
                        roped(t, 0, 0, 0, 0, qh, P, 0, nt)
                        split(t, 2)
                        roped(t, 1, 1, 1, 1, kh, P, 0, TOK, scale=RET_DK ** -0.5)
                        for e in range(2):
                            split(t, 3 + e)
                            act.wait_ge(sem("product"), t.v("chunk", 3 + e))
                            if e == 0:
                                act.wait_ge(sem("v_lo"), t.v("v_lo", 2))
                            act.activation(tmp[:, 1 + e, 0:nt], pair(e)[:, 0:nt], ACT.Silu).then_inc(
                                sem(f"free{e}"), 1)
                        split(t, 5)
                        act.wait_ge(sem("product"), t.v("chunk", 6))
                        act.activation(vh_f[:, :], ps[:, 0:2 * TOK], ACT.Copy).then_inc(sem("e_hi"), 1)
                        units = 8 if nt > LAT else 6
                        for u in range(units):
                            w = LAT if u < 6 else CTX
                            act.wait_ge(sem("rs_sd"), t.v("rs_sd", u + 1))
                            if u >= 3:
                                act.wait_ge(sem("rs_used"), t.v("rs_used", u - 2))
                            act.activation(pth_f[:, (u % 3) * LAT:(u % 3) * LAT + w], prob[:, u % 3, 0:w],
                                           ACT.Copy).then_inc(sem("rs_hi"), 1)
                        act.wait_ge(sem("rs_used"), t.v("rs_used", units))
                        for e in range(2):
                            act.activation(prob[:, e, 0:nt], pair(e)[:, 0:nt], ACT.Copy)
                            act.activation((tmp[:, 0, 0:nt], prob[:, 2, 0:nt])[e], pair(e)[:, 0:nt],
                                           ACT.Square).then_inc(sem(f"free{e}"), 1)
                        split(t, 6)
                        act.wait_ge(sem("v_stat"), t.v("v_stat", 1))
                        act.activation(prob[:, 2, 0:nt], pair(AUX)[:, 0:nt], ACT.Sqrt, bias=eps[:, :],
                                       scale=1.0 / RET_DV).then_inc(sem("v_std"), 1)
                        for e in range(2):
                            act.wait_ge(sem("v_full"), t.v("v_full", 3 + e))
                            act.activation(yh[:, bass.ds(2 * i + e, 1), 0:nt], prob[:, e, 0:nt],
                                           ACT.Copy).then_inc(sem("v_hi"), 1)

                elif kind == "z":
                    act.wait_ge(sem("mg_add"), at.v("mg_add"))
                    for t in range(KT):
                        act.activation(yh[:, t, 0:nt], xz[:, t, 0:nt], ACT.Copy).then_inc(sem("z_hi"), 1)
                    act.wait_ge(sem("z_lo"), at.v("z_lo", KT))
                    load_x(xspill if layer else a["xT"])
                    x_loads += 1

                elif kind == "out":
                    if at.v("chunk") + 2 * turns < NCHUNK:
                        with act.Fori(0, turns) as i:
                            for k in range(2 + 2 * ph["nmod"]):
                                split(At(ph, i), k + 1)
                    else:
                        with act.Fori(0, turns - 1) as i:
                            for k in range(2):
                                split(At(ph, i), k + 1)
                        split(At(ph, turns - 1), 1)

                elif kind == "ffn":
                    with act.Fori(0, turns) as i:
                        t = At(ph, i)
                        for k in range(2):
                            split(t, 2 * k + 1)
                            act.wait_ge(sem("product"), t.v("chunk", 2 * k + 1))
                            act.wait_ge(sem("free1"), t.v("free1", k - 1))
                            act.activation(tmp[:, k, 0:nt], pair(0)[:, 0:nt], ACT.Silu).then_inc(sem("free0"), 1)
                            split(t, 2 * k + 2)
                            act.wait_ge(sem("free1"), t.v("free1", k + 1))
                            act.activation(yh[:, bass.ds(2 * i + k, 1), 0:nt], prob[:, k, 0:nt],
                                           ACT.Copy).then_inc(sem("f_hi"), 1)

                elif kind == "final":
                    act.wait_ge(sem("free0"), at.v("free0"))
                    act.wait_ge(sem("free1"), at.v("free1"))
                    for t in range(KT):
                        if t >= 2:
                            act.wait_ge(sem("sq_used"), at.v("sq_used", t - 1))
                        act.activation(tmp[:, t % 2, 0:nt], xz[:, t, 0:nt], ACT.Square).then_inc(sem("sq"), 1)
                    act.wait_ge(sem("sq_used"), at.v("sq_used", KT))
                    act.activation(tmp[:, 2, 0:nt], pair(AUX)[:, 0:nt], ACT.Sqrt, bias=eps[:, :],
                                   scale=1.0 / D).then_inc(sem("n_std"), 1)
                    for t in range(KT):
                        act.wait_ge(sem("o_ready"), t + 1)
                        act.dma_start(a["out"][t * P:(t + 1) * P, :], xz[:, t, 0:LAT]).then_inc(sem("out_done"), 16)
                    act.wait_ge(sem("out_done"), 16 * KT)

        @block.vector
        def _(dve):
            def split(at, k):
                s = at.slot(k)
                dve.wait_ge(sem("w_hi"), at.v("chunk", k + 1))
                dve.tensor_tensor(wl[:, s, :], raw[:, s, :], wh[:, s, :].bitcast(F32), ALU.subtract).then_inc(
                    sem("w_lo"), 1)

            def plain(at, ke, slot, hi, lo, rows=P, nt=TOK):
                dve.wait_ge(sem("e_hi"), at.v("e_hi", ke + 1))
                dve.tensor_tensor(lo[0:rows, 0:nt], pair(slot)[0:rows, 0:nt], hi[0:rows, 0:nt].bitcast(F32),
                                  ALU.subtract).then_inc(sem(f"free{slot}"), 1)

            def rstd(at, k, nt):
                dve.wait_ge(sem("v_std"), at.v("v_std", k + 1))
                dve.reciprocal(tmp[:, 2, 0:nt], tmp[:, 2, 0:nt]).then_inc(sem("v_rstd"), 1)
                dve.wait_ge(sem("v_rstd"), at.v("v_rstd", k + 1))

            def roped(at, kv, kp, slot, kfree, hi, lo, rows, r0, nt, kn=None, gain=None):
                dve.wait_ge(sem(f"free{slot}"), at.v(f"free{slot}", kfree))
                if kn is not None:
                    rstd(at, kn, nt)
                    dve.scalar_tensor_tensor(out=tmp[:, 0, 0:nt], in0=tmp[:, 0, 0:nt], scalar=gain,
                                             in1=tmp[:, 2, 0:nt], op0=ALU.mult, op1=ALU.mult).then_inc(
                        sem("v_norm"), 1)
                    dve.wait_ge(sem("v_norm"), at.v("v_norm", kn + 1))
                dve.tensor_tensor(tmp[0:rows, 1, 0:LAT], tmp[0:rows, 0, 0:LAT], rope[0:rows, 0, :],
                                  ALU.mult).then_inc(sem("v_c"), 1)
                dve.wait_ge(sem("v_perm"), at.v("v_perm", kp + 1))
                dve.tensor_tensor(tmp[0:rows, 2, 0:LAT], ps[0:rows, 6 * BANK:7 * BANK], rope[0:rows, 1, :],
                                  ALU.mult).then_inc(sem("v_s"), 1)
                dve.wait_ge(sem("v_c"), at.v("v_c", kp + 1))
                dve.wait_ge(sem("v_s"), at.v("v_s", kp + 1))
                dve.tensor_tensor(tmp[0:rows, 0, 0:LAT], tmp[0:rows, 1, 0:LAT], tmp[0:rows, 2, 0:LAT],
                                  ALU.add).then_inc(sem("v_full"), 1)
                dve.wait_ge(sem("v_full"), at.v("v_full", kv[1] + 1))
                dve.wait_ge(sem("v_hi"), at.v("v_hi", kv[0] + 1))
                dve.tensor_tensor(lo[r0:rows, 0:nt], tmp[r0:rows, 0, 0:nt], hi[r0:rows, 0:nt].bitcast(F32),
                                  ALU.subtract).then_inc(sem("v_lo"), 1)

            def attend(at, ka, nt, scale, head, fill=lambda n: None):
                nq, a0, b0 = nt // P, ka * (nt // P), ka * (nt // P) // 2
                for n in range(nq + 2):
                    if n > 3 and n % 2 == 0:
                        y_lo(at, b0, n // 2 - 2, head)
                    if n < nq:
                        w = TOK if n < 4 else CTX
                        s0 = SCORES[n % 2]
                        dve.wait_ge(sem("s_ready"), at.v("s_ready", a0 + n + 1))
                        dve.tensor_reduce(mx[:, n:n + 1], ps[:, s0:s0 + w], AX.X, ALU.max).then_inc(
                            sem("s_max"), 1)
                        dve.wait_ge(sem("s_max"), at.v("s_max", a0 + n + 1))
                        dve.tensor_scalar(nm[:, n:n + 1], mx[:, n:n + 1], scale(n), -1.0, ALU.mult,
                                          ALU.mult).then_inc(sem("s_nm"), 1)
                    m = n - 1
                    if 0 <= m < nq:
                        dve.wait_ge(sem("s_exp"), at.v("s_exp", a0 + m + 1))
                        dve.reciprocal(ri[:, m:m + 1], rs[:, m:m + 1]).then_inc(sem("s_rinv"), 1)
                    m = n - 2
                    if 0 <= m < nq:
                        st = 6 if m < 4 else 2
                        cols = slice((m % 2) * P, (m % 2) * P + P)
                        dve.wait_ge(sem("t_hi"), at.v("t_hi", a0 + m + 1))
                        dve.tensor_tensor(ptl[:, 0:st, cols],
                                          ps[:, TRANS:TRANS + st * P].rearrange("p (s q) -> p s q", q=P),
                                          pth[:, 0:st, cols].bitcast(F32), ALU.subtract).then_inc(sem("t_lo"), 1)
                    fill(n)
                y_lo(at, b0, nq // 2 - 1, head)

            def y_lo(at, b0, b, head):
                dve.wait_ge(sem("y_hi"), at.v("y_hi", b0 + b + 1))
                cols = slice(2 * P * b, 2 * P * (b + 1))
                dve.tensor_tensor(yl[:, bass.ds(head, 1), cols], ps[:, OUTS:OUTS + 2 * P].unsqueeze(1),
                                  yh[:, bass.ds(head, 1), cols].bitcast(F32),
                                  ALU.subtract).then_inc(sem("y_lo"), 1)

            def cosine(at, kv, rows):
                dve.tensor_tensor(tmp[0:rows, 1, 0:LAT], tmp[0:rows, 0, 0:LAT], rope[0:rows, 0, :],
                                  ALU.mult).then_inc(sem("v_c"), 1)

            def sine(at, kv, rows):
                dve.wait_ge(sem("v_perm"), at.v("v_perm", kv + 1))
                dve.tensor_tensor(tmp[0:rows, 2, 0:LAT], ps[0:rows, TURN:TURN + LAT], rope[0:rows, 1, :],
                                  ALU.mult).then_inc(sem("v_s"), 1)
                dve.wait_ge(sem("v_c"), at.v("v_c", kv + 1))
                dve.wait_ge(sem("v_s"), at.v("v_s", kv + 1))
                dve.tensor_tensor(tmp[0:rows, 0, 0:LAT], tmp[0:rows, 1, 0:LAT], tmp[0:rows, 2, 0:LAT],
                                  ALU.add).then_inc(sem("v_full"), 1)

            def query_lo(at, kv, par, rows, nt):
                dve.wait_ge(sem("v_full"), at.v("v_full", kv + 1))
                dve.wait_ge(sem("v_hi"), at.v("v_hi", kv + 1))
                dve.tensor_tensor(queries[par][1][0:rows, 0:nt], tmp[0:rows, 0, 0:nt],
                                  queries[par][0][0:rows, 0:nt].bitcast(F32), ALU.subtract).then_inc(
                    sem("v_lo"), 1)

            def mla_head(at, kp, par, nt, nmod):
                c0 = kp * (2 + nmod)

                def fill(n):
                    if n == 0:
                        split(at, c0 + 1)
                        plain(at, 2 * kp, 0, *keys[par], rows=MLA_NOPE)
                    if n == 1:
                        plain(at, 2 * kp + 1, 0, vh[:, par, :], vl[:, par, :])
                    if n == 2:
                        split(at, c0 + 2)
                    if n == 3:
                        dve.wait_ge(sem("free0"), at.v("free0", 3 * kp + 3))
                        cosine(at, kp, MLA_QK)
                        if nmod:
                            split(at, c0 + 3)
                    if n == 4:
                        sine(at, kp, MLA_QK)
                        if nmod:
                            split(at, c0 + 4)
                    if n == 5:
                        query_lo(at, kp, par, MLA_QK, nt)
                        if nmod:
                            split(at, c0 + 5)
                            split(at, c0 + 6)
                return fill

            def gqa_query(at, kq, par, nt):
                nq = nt // P

                def fill(n):
                    if n == 0:
                        split(at, kq + 3)
                    if n == 4:
                        dve.wait_ge(sem("v_std"), at.v("v_std", kq + 2))
                        dve.reciprocal(qsc[:, par, 0:nq], qsc[:, par, 0:nq]).then_inc(sem("v_rstd"), 1)
                        cosine(at, kq + 1, P)
                        dve.wait_ge(sem("v_rstd"), at.v("v_rstd", kq + 2))
                        dve.tensor_scalar(qsc[:, par, 0:nq], qsc[:, par, 0:nq], GQA_HD ** -0.5, None,
                                          ALU.mult).then_inc(sem("v_norm"), 1)
                        sine(at, kq + 1, P)
                    if n == 5:
                        dve.wait_ge(sem("v_norm"), at.v("v_norm", kq + 2))
                        query_lo(at, kq + 1, par, P, nt)
                return fill

            dve.memset(ones[:, :], 1.0).then_inc(sem("ones_set"), 1)
            dve.memset(eps[:, :], EPS).then_inc(sem("eps_set"), 1)
            dve.wait_ge(sem("c_hi"), 1)
            dve.tensor_tensor(cl[:, :, :], csil[:, :, :], ch[:, :, :].bitcast(F32), ALU.subtract).then_inc(
                sem("c_lo"), 1)
            dve.wait_ge(sem("const_in"), 64)
            split(At(PHASES[0]), 0)
            x_loads = 1
            tabs = 0

            for ph in PHASES:
                kind, layer, at = ph["kind"], ph["layer"], At(ph)
                nt, turns = ph.get("nt"), ph["turns"]
                g0 = layer * G_LAYER
                if kind == "mod":
                    with dve.Fori(0, turns) as i:
                        for k in range(2):
                            split(At(ph, i), k + 1)

                elif kind == "mods":
                    js = (2 * KT, N_MOD * KT) if ph.get("rest") else (0, N_MOD * KT if layer else 2 * KT)
                    done = at.v("mod")
                    dve.wait_ge(sem("product"), at.v("chunk"))
                    dve.tensor_tensor(
                        mods[:, js[0]:js[1], :],
                        ps[:, MODS[layer] + 2 * js[0]:MODS[layer] + 2 * js[1]].rearrange("p (j u) -> p j u", u=2),
                        bmod[:, layer, js[0]:js[1]].unsqueeze(2).to_broadcast([P, js[1] - js[0], 2]),
                        ALU.add).then_inc(sem("mod"), 1)
                    dve.wait_ge(sem("mod"), done + 1)
                    for j in range(2):
                        if js[0] <= (3 * j + 1) * KT < js[1]:
                            done += 1
                            dve.scalar_tensor_tensor(
                                out=gm[:, j, :, :], in0=mods[:, (3 * j + 1) * KT:(3 * j + 2) * KT, :], scalar=1.0,
                                in1=gains[:, g0 + j * KT:g0 + (j + 1) * KT].unsqueeze(2).to_broadcast([P, KT, 2]),
                                op0=ALU.add, op1=ALU.mult).then_inc(sem("mod"), 1)
                    dve.wait_ge(sem("mod"), done + 1)

                elif kind == "norm":
                    gi = 0 if ph["first"] else 1
                    dve.wait_ge(sem("n_std"), at.v("n_std", 1))
                    dve.reciprocal(tmp[:, 2, 0:nt], tmp[:, 2, 0:nt]).then_inc(sem("n_rstd"), 1)
                    dve.wait_ge(sem("n_rstd"), at.v("n_rstd", 1))
                    for t in range(KT + 1):
                        if t < KT:
                            if t >= 2:
                                dve.wait_ge(sem("n_hi"), at.v("n_hi", t - 1))
                                dve.wait_ge(sem("n_full"), at.v("n_full", t - 1))
                            dve.tensor_tensor(tmp[:, t % 2, 0:nt], xz[:, t, 0:nt], tmp[:, 2, 0:nt],
                                              ALU.mult).then_inc(sem("n_t1"), 1)
                        m = t - 1
                        if m >= 0:
                            if m >= 2:
                                dve.wait_ge(sem("n_lo"), at.v("n_lo", m - 1))
                            dve.wait_ge(sem("n_t1"), at.v("n_t1", m + 1))
                            for u, (r0, r1) in enumerate(ranges(nt)):
                                ins = dve.tensor_scalar(prob[:, m % 2, r0:r1], tmp[:, m % 2, r0:r1],
                                                        gm[:, gi, m, u:u + 1],
                                                        mods[:, 3 * gi * KT + m, u:u + 1], ALU.mult, ALU.add)
                            ins.then_inc(sem("n_full"), 1)

                elif kind == "mla_in":
                    for j, nt_j in enumerate((TOK if layer < DEPTH - 1 else LAT, TOK)):
                        for k in range(RKT):
                            split(at, 2 * j + k + 1)
                        rstd(at, j, nt_j)
                        for k in range(RKT):
                            col = g0 + 2 * KT + j * RKT + k
                            dve.scalar_tensor_tensor(out=tmp[:, k, 0:nt_j], in0=tmp[:, k, 0:nt_j],
                                                     scalar=gains[:, col:col + 1], in1=tmp[:, 2, 0:nt_j],
                                                     op0=ALU.mult, op1=ALU.mult).then_inc(sem("v_norm"), 1)
                        for k in range(RKT):
                            dve.wait_ge(sem("v_norm"), at.v("v_norm", 2 * j + k + 1))
                            dve.wait_ge(sem("v_hi"), at.v("v_hi", 2 * j + k + 1))
                            dve.tensor_tensor(ranks[:, j, 1, k, 0:nt_j], tmp[:, k, 0:nt_j],
                                              ranks[:, j, 0, k, 0:nt_j].bitcast(F32), ALU.subtract).then_inc(
                                sem("v_lo"), 1)
                    split(at, 5)
                    split(at, 6)
                    tabs += 1
                    dve.wait_ge(sem("tab_in"), 16 * tabs)
                    roped(at, (4, 0), 0, 0, 3, kh, kl, MLA_QK, MLA_NOPE, TOK)
                    rows = slice(MLA_NOPE, MLA_QK)
                    dve.wait_ge(sem("v_hi"), at.v("v_hi", 6))
                    dve.tensor_tensor(k2l[rows, :], tmp[rows, 0, :], k2h[rows, :].bitcast(F32),
                                      ALU.subtract).then_inc(sem("v_lo"), 1)

                elif kind == "mla_first":
                    fill = mla_head(at, 0, 0, nt, ph["nmod"])
                    for n in range(6):
                        fill(n)

                elif kind == "mla":
                    with dve.Fori(0, turns) as i:
                        t = At(ph, i)
                        for k in range(2):
                            attend(t, k, nt, lambda n: MLA_QK ** -0.5, 2 * i + k,
                                   mla_head(t, k, 1 - k, nt, ph["nmod"]))

                elif kind == "mla_last":
                    attend(at, 0, nt, lambda n: MLA_QK ** -0.5, MLA_HEADS - 2, mla_head(at, 0, 1, nt, ph["nmod"]))
                    attend(at, 1, nt, lambda n: MLA_QK ** -0.5, MLA_HEADS - 1)

                elif kind == "gqa":
                    tabs += 1
                    dve.wait_ge(sem("tab_in"), 16 * tabs)
                    with dve.Fori(0, turns) as i:
                        t = At(ph, i)
                        split(t, 1)
                        roped(t, (0, 0), 0, 0, 1, kh, kl, P, 0, TOK, kn=0,
                              gain=gains[:, g0 + 2 * KT + 2 * RKT + 1:g0 + 2 * KT + 2 * RKT + 2])
                        split(t, 2)
                        plain(t, 0, 1, vh[:, 0, :], vl[:, 0, :])
                        fills = [gqa_query(t, k, k % 2, nt) for k in range(4)]
                        for n in range(6):
                            fills[0](n)
                        for k in range(4):
                            attend(t, k, nt, lambda n, par=k % 2: qsc[:, par, n:n + 1], 4 * i + k,
                                   *fills[k + 1:k + 2])

                elif kind == "merge":
                    with dve.Fori(0, turns) as i:
                        t = At(ph, i)
                        for k in range(2):
                            split(t, 2 * k + 1)
                            split(t, 2 * k + 2)
                            dve.wait_ge(sem("free0"), t.v("free0", k + 1))
                            dve.wait_ge(sem("product"), t.v("chunk", 2 * k + 2))
                            z = xz[:, bass.ds(2 * i + k, 1), 0:nt]
                            dve.tensor_tensor(z if ph["first"] else prob[:, k:k + 1, 0:nt],
                                              pair(1)[:, 0:nt].unsqueeze(1), tmp[:, k:k + 1, 0:nt],
                                              ALU.mult).then_inc(sem("free1"), 1)
                            if not ph["first"]:
                                dve.wait_ge(sem("free1"), t.v("free1", k + 1))
                                dve.tensor_tensor(z, z, prob[:, k:k + 1, 0:nt], ALU.add).then_inc(sem("mg_add"), 1)
                                dve.wait_ge(sem("mg_add"), t.v("mg_add", k + 1))

                elif kind == "ret":
                    with dve.Fori(0, turns) as i:
                        t = At(ph, i)
                        split(t, 1)
                        roped(t, (0, 0), 0, 0, 1, qh, ql, P, 0, nt)
                        split(t, 2)
                        roped(t, (1, 1), 1, 1, 1, kh, kl, P, 0, TOK)
                        for k in range(3, 6):
                            split(t, k)
                        dve.wait_ge(sem("e_hi"), t.v("e_hi", 1))
                        for e, cols in enumerate((slice(0, 2 * BANK), slice(2 * BANK, 3 * BANK))):
                            dve.tensor_tensor(vl_f[:, cols], ps[:, cols], vh_f[:, cols].bitcast(F32),
                                              ALU.subtract).then_inc(sem(f"free{e}"), 1)
                        units = 8 if nt > LAT else 6
                        dve.wait_ge(sem("dec_in"), t.v("dec", 1) * 16)
                        for u in range(units):
                            w = LAT if u < 6 else CTX
                            d0 = (3 * P - P * u if u < 4 else DEC1 + P - P * (u - 4) if u < 6
                                  else 3 * P - P * (u - 6))
                            dve.wait_ge(sem("rs_ready"), t.v("rs_ready", u + 1))
                            if u >= 3:
                                dve.wait_ge(sem("rs_lo"), t.v("rs_lo", u - 2))
                            dve.tensor_tensor(prob[:, u % 3, 0:w], ps[:, (4 + u % 3) * BANK:(4 + u % 3) * BANK + w],
                                              dec[:, d0:d0 + w], ALU.mult).then_inc(sem("rs_sd"), 1)
                        split(t, 6)
                        dve.wait_ge(sem("v_std"), t.v("v_std", 1))
                        dve.reciprocal(prob[:, 2, 0:nt], prob[:, 2, 0:nt]).then_inc(sem("v_rstd"), 1)
                        for e in range(2):
                            dve.tensor_tensor(prob[:, e, 0:nt], prob[:, e, 0:nt], tmp[:, 1 + e, 0:nt],
                                              ALU.mult).then_inc(sem("v_norm"), 1)
                        dve.wait_ge(sem("v_rstd"), t.v("v_rstd", 1))
                        for e in range(2):
                            dve.wait_ge(sem("v_norm"), t.v("v_norm", e + 1))
                            dve.tensor_tensor(prob[:, e, 0:nt], prob[:, e, 0:nt], prob[:, 2, 0:nt],
                                              ALU.mult).then_inc(sem("v_full"), 1)
                        for e in range(2):
                            dve.wait_ge(sem("v_full"), t.v("v_full", 3 + e))
                            dve.wait_ge(sem("v_hi"), t.v("v_hi", 3 + e))
                            dve.tensor_tensor(yl[:, bass.ds(2 * i + e, 1), 0:nt], prob[:, e:e + 1, 0:nt],
                                              yh[:, bass.ds(2 * i + e, 1), 0:nt].bitcast(F32),
                                              ALU.subtract).then_inc(sem("v_lo"), 1)

                elif kind == "z":
                    for t in range(KT):
                        dve.wait_ge(sem("z_hi"), at.v("z_hi", t + 1))
                        dve.tensor_tensor(yl[:, t, 0:nt], xz[:, t, 0:nt], yh[:, t, 0:nt].bitcast(F32),
                                          ALU.subtract).then_inc(sem("z_lo"), 1)
                    x_loads += 1

                elif kind == "out":
                    if ph["mod"] == 2:
                        dve.wait_ge(sem("x_in"), 16 * KT * x_loads)
                    for k in range(2):
                        dve.wait_ge(sem(f"free{k}"), at.v(f"free{k}"))

                    def turn(i, last=False):
                        t = At(ph, i)
                        step = 1 + ph["nmod"]
                        for k in range(2):
                            if not (last and k == 1):
                                split(t, k * step + 1)
                            dve.wait_ge(sem("product"), t.v("chunk", k * step + 1))
                            for u, (r0, r1) in enumerate(ranges(nt)):
                                m = ph["mod"] * KT + k
                                scalar = mods[:, bass.ds(2 * i + m, 1), u:u + 1].rearrange("p a b -> p (a b)")
                                ins = dve.scalar_tensor_tensor(
                                    out=xz[:, bass.ds(2 * i + k, 1), r0:r1], in0=pair(k)[:, r0:r1].unsqueeze(1),
                                    scalar=scalar, in1=xz[:, bass.ds(2 * i + k, 1), r0:r1], op0=ALU.mult, op1=ALU.add)
                            ins.then_inc(sem(f"free{k}"), 1)
                            for r in range(ph["nmod"]):
                                split(t, k * step + 2 + r)
                    if at.v("chunk") + 2 * turns < NCHUNK:
                        with dve.Fori(0, turns) as i:
                            turn(i)
                    else:
                        with dve.Fori(0, turns - 1) as i:
                            turn(i)
                        turn(turns - 1, last=True)

                elif kind == "ffn":
                    with dve.Fori(0, turns) as i:
                        t = At(ph, i)
                        for k in range(2):
                            split(t, 2 * k + 1)
                            split(t, 2 * k + 2)
                            dve.wait_ge(sem("free0"), t.v("free0", k + 1))
                            dve.wait_ge(sem("product"), t.v("chunk", 2 * k + 2))
                            dve.wait_ge(sem("f_lo"), t.v("f_lo", k - 1))
                            dve.tensor_tensor(prob[:, k, 0:nt], pair(1)[:, 0:nt], tmp[:, k, 0:nt],
                                              ALU.mult).then_inc(sem("free1"), 1)

                elif kind == "final":
                    dve.wait_ge(sem("n_std"), at.v("n_std", 1))
                    dve.reciprocal(tmp[:, 2, 0:nt], tmp[:, 2, 0:nt]).then_inc(sem("n_rstd"), 1)
                    dve.wait_ge(sem("n_rstd"), at.v("n_rstd", 1))
                    for t in range(KT):
                        dve.scalar_tensor_tensor(out=xz[:, t, 0:nt], in0=xz[:, t, 0:nt],
                                                 scalar=gains[:, G_FINAL + t:G_FINAL + t + 1],
                                                 in1=tmp[:, 2, 0:nt], op0=ALU.mult, op1=ALU.mult).then_inc(
                            sem("o_ready"), 1)

        @block.gpsimd
        def _(pool):
            def attend(at, ka, nt):
                nq, a0 = nt // P, ka * (nt // P)
                for n in range(nq):
                    w = TOK if n < 4 else CTX
                    pool.wait_ge(sem("s_rinv"), at.v("s_rinv", a0 + n + 1))
                    pool.tensor_tensor(prob[:, n % 3, 0:w], prob[:, n % 3, 0:w],
                                       ri[:, n:n + 1].to_broadcast([P, w]), ALU.mult).then_inc(sem("s_pn"), 1)

            for k in range(2):
                pool.memset(mark[:, k:k + 1], 0.0).then_inc(sem("f_lo"), 1)
            pool.memset(mark[:, 2:3], 0.0).then_inc(sem("y_lo"), 1)
            for ph in PHASES:
                kind, layer, at = ph["kind"], ph["layer"], At(ph)
                nt, turns = ph.get("nt"), ph["turns"]
                if kind == "norm":
                    for t in range(KT):
                        pool.wait_ge(sem("n_hi"), at.v("n_hi", t + 1))
                        pool.wait_ge(sem("n_full"), at.v("n_full", t + 1))
                        pool.tensor_tensor(hl[:, t, 0:nt], prob[:, t % 2, 0:nt], hh[:, t, 0:nt].bitcast(F32),
                                           ALU.subtract).then_inc(sem("n_lo"), 1)
                elif kind in ("mla", "gqa"):
                    with pool.Fori(0, turns) as i:
                        for k in range(2 if kind == "mla" else 4):
                            attend(At(ph, i), k, nt)
                elif kind == "mla_last":
                    for k in range(2):
                        attend(at, k, nt)
                elif kind == "ret":
                    units = 8 if nt > LAT else 6
                    with pool.Fori(0, turns) as i:
                        t = At(ph, i)
                        for u in range(units):
                            w = LAT if u < 6 else CTX
                            pool.wait_ge(sem("rs_hi"), t.v("rs_hi", u + 1))
                            cols = slice((u % 3) * LAT, (u % 3) * LAT + w)
                            pool.tensor_tensor(ptl_f[:, cols], prob[:, u % 3, 0:w], pth_f[:, cols].bitcast(F32),
                                               ALU.subtract).then_inc(sem("rs_lo"), 1)
                elif kind == "ffn":
                    with pool.Fori(0, turns) as i:
                        t = At(ph, i)
                        for k in range(2):
                            pool.wait_ge(sem("f_hi"), t.v("f_hi", k + 1))
                            pool.tensor_tensor(yl[:, bass.ds(2 * i + k, 1), 0:nt], prob[:, k:k + 1, 0:nt],
                                               yh[:, bass.ds(2 * i + k, 1), 0:nt].bitcast(F32), ALU.subtract).then_inc(
                                sem("f_lo"), 1)

        @block.tensor
        def _(pe):
            def three(outs, lhs, rhs, start, stop):
                for n, (w, x) in enumerate(((0, 0), (0, 1), (1, 0))):
                    for out, cols in outs:
                        ins = pe.matmul(out, lhs[w], rhs[x](cols), start=start and n == 0, stop=stop and n == 2)
                return ins

            def project(at, kc, slot, kfree, mov, kts, nt, cut, rows=P, kt0=0, ktn=None, done=True, piece=False, late={}):
                s = at.slot(kc)
                if kfree is not None and (at.base.get(f"free{slot}", 0) + kfree > 0 or not isinstance(at.i, int)):
                    pe.wait_ge(sem(f"free{slot}"), at.v(f"free{slot}", kfree))
                pe.wait_ge(sem("w_lo"), at.v("chunk", kc + 1))
                for kt in range(kts):
                    g = kt0 + kt
                    if kt in late:
                        pe.wait_ge(sem(late[kt][0]), late[kt][1])
                    outs = [(pair(slot)[0:rows, r0:r1], (r0, r1)) for r0, r1 in ranges(nt)]
                    ins = three(outs, [w[:, s, cut(kt if piece else g)] for w in (wh, wl)],
                                [lambda c, x=x: x(g, c) for x in mov], g == 0, g == (ktn or kts) - 1)
                if done:
                    ins.then_inc(sem("product"), 1)
                return ins

            def project_v(at, kc, slot, kfree, src, kts, cut):
                s = at.slot(kc)
                pe.wait_ge(sem(f"free{slot}"), at.v(f"free{slot}", kfree))
                pe.wait_ge(sem("w_lo"), at.v("chunk", kc + 1))
                for tt in range(TOK // P):
                    for kt in range(kts):
                        out = pair(slot)[:, tt * P:(tt + 1) * P]
                        ins = three([(out, None)], [x(kt, (tt * P, (tt + 1) * P)) for x in src],
                                    [lambda c, w=w: w[:, s, cut(kt)] for w in (wh, wl)], kt == 0, kt == kts - 1)
                return ins

            H = [lambda k, c, x=x: x[:, k, c[0]:c[1]] for x in (hh, hl)]
            Y = [lambda k, c, x=x: x[:, k, c[0]:c[1]] for x in (yh, yl)]
            R = [[lambda k, c, j=j, x=x: ranks[:, j, x, k, c[0]:c[1]] for x in range(2)] for j in range(2)]
            whole = lambda kt: slice(kt * P, (kt + 1) * P)

            def stats(at, src, slots, nt, k):
                for n, x in enumerate(slots):
                    for r0, r1 in ranges(nt):
                        ins = pe.matmul(pair(AUX)[:, r0:r1], ones[:, :], src[:, x, r0:r1], start=n == 0,
                                        stop=n == len(slots) - 1)
                ins.then_inc(sem("v_stat"), 1)

            def rotate(which, rows, bank=6 * BANK):
                pe.matmul(ps[0:rows, bank:bank + LAT], perm[0:rows, which, 0:rows], tmp[0:rows, 0, 0:LAT],
                          start=True, stop=True).then_inc(sem("v_perm"), 1)

            def attend(at, ka, par, kpar, vpar, nt, rows, fill=lambda n: None):
                nq, a0, b0 = nt // P, ka * (nt // P), ka * (nt // P) // 2
                for n in range(nq + 2):
                    if n < nq:
                        if n >= 2:
                            pe.wait_ge(sem("s_exp"), at.v("s_exp", a0 + n - 1))
                        s0 = SCORES[n % 2]
                        spans = [(s0, (0, LAT)), (s0 + LAT, (LAT, TOK))] if n < 4 else [(s0, (LAT, TOK))]
                        outs = [(ps[:, o:o + c[1] - c[0]], c) for o, c in spans]
                        three(outs, [q[0:rows, n * P:(n + 1) * P] for q in queries[par]],
                              [lambda c, x=x: x[0:rows, c[0]:c[1]] for x in keys[kpar]], True, True).then_inc(
                            sem("s_ready"), 1)
                    m = n - 2
                    if 0 <= m < nq:
                        st = 6 if m < 4 else 2
                        pe.wait_ge(sem("s_pn"), at.v("s_pn", a0 + m + 1))
                        if m:
                            pe.wait_ge(sem("t_lo"), at.v("t_lo", a0 + m))
                        if m % 2 == 0:
                            pe.wait_ge(sem("y_lo"), at.v("y_lo", b0 + m // 2))
                        for s in range(st):
                            ins = pe.transpose(ps[:, TRANS + s * P:TRANS + (s + 1) * P],
                                               prob[:, m % 3, s * P:(s + 1) * P], ident[:, :])
                        ins.then_inc(sem("t_ready"), 1)
                    fill(n)
                    if n > 2 and n % 2:
                        values(at, a0, b0, (n - 3) // 2, vpar)

            def values(at, a0, b0, b, vpar):
                lat = b < 2
                st, v0 = (6, 0) if lat else (2, 4)
                pe.wait_ge(sem("t_lo"), at.v("t_lo", a0 + 2 * b + 2))
                for s in range(st):
                    ins = three([(ps[:, OUTS:OUTS + 2 * P], None)],
                                [v[:, vpar, (v0 + s) * P:(v0 + s + 1) * P] for v in (vh, vl)],
                                [lambda c, x=x: x[:, s, :] for x in (pth, ptl)], s == 0, s == st - 1)
                ins.then_inc(sem("y_ready"), 1)

            def mod_chunk(at, kc, j, home=MODS[0]):
                s = at.slot(kc)
                pe.wait_ge(sem("w_lo"), at.v("chunk", kc + 1))
                out = ps[:, bass.ds(2 * j + home, 2)]
                for kt in range(KT):
                    ins = three([(out, None)], [w[:, s, whole(kt)] for w in (wh, wl)],
                                [lambda c, x=x: x[:, kt, :] for x in (ch, cl)], kt == 0, kt == KT - 1)
                ins.then_inc(sem("product"), 1)

            def mla_head(at, kp, head, nt, nmod):
                c0 = kp * (2 + nmod)
                def fill(n):
                    s = at.slot(c0)
                    if n == 0:
                        pe.wait_ge(sem("free0"), at.v("free0", 3 * kp))
                        pe.wait_ge(sem("v_s"), at.v("v_s", kp))
                        pe.wait_ge(sem("w_lo"), at.v("chunk", c0 + 1))
                        for kt in range(RKT):
                            ins = three([(pair(0)[:, r0:r1], (r0, r1)) for r0, r1 in ranges(TOK)],
                                        [w[:, s, kt * 256:kt * 256 + P] for w in (wh, wl)],
                                        [lambda c, x=x: x(kt, c) for x in R[1]], kt == 0, kt == RKT - 1)
                        ins.then_inc(sem("k_ready"), 1)
                    if n == 1:
                        project_v(at, c0, 0, 3 * kp + 1, R[1], RKT,
                                  lambda kt: slice(kt * 256 + 64, kt * 256 + 192)).then_inc(sem("product"), 1)
                    if n == 2:
                        project(at, c0 + 1, 0, 3 * kp + 2, R[0], RKT, nt,
                                lambda kt: slice(kt * P, kt * P + MLA_QK), rows=MLA_QK)
                    if n == 3:
                        pe.wait_ge(sem("free0"), at.v("free0", 3 * kp + 3))
                        rotate(1, MLA_QK, TURN)
                    if nmod and n >= 3:
                        for r in ((), (), (), (0,), (1,), (2, 3), (), ())[n]:
                            mod_chunk(at, c0 + 2 + r, 4 * head + (2 * KT + r))
                return fill

            def gqa_query(at, kq, nt):
                def fill(n):
                    if n == 0:
                        pe.wait_ge(sem("v_s"), at.v("v_s", kq + 1))
                    if n < 2:
                        project(at, kq + 2, 0, kq + 1 if n == 0 else None, H, KT // 2, nt, whole, kt0=n * KT // 2,
                                ktn=KT, done=n == 1)
                    if n == 3:
                        pe.wait_ge(sem("free0"), at.v("free0", kq + 2))
                        for j in range(nt // P):
                            ins = pe.matmul(ps[:, QSUM + j:QSUM + j + 1], tmp[:, 1, j * P:(j + 1) * P],
                                            ones[:, 0:1], start=True, stop=True)
                        ins.then_inc(sem("v_stat"), 1)
                        rotate(0, P, TURN)
                return fill

            pe.wait_ge(sem("c_lo"), 1)
            pe.wait_ge(sem("ones_set"), 1)

            for ph in PHASES:
                kind, layer, at = ph["kind"], ph["layer"], At(ph)
                nt, turns = ph.get("nt"), ph["turns"]
                if kind == "mod":
                    with pe.Fori(0, turns) as i:
                        for k in range(2):
                            mod_chunk(At(ph, i), k, 2 * i + k)

                elif kind in ("norm", "final"):
                    for t in range(KT):
                        pe.wait_ge(sem("sq"), at.v("sq", t + 1))
                        for r0, r1 in ranges(nt):
                            ins = pe.matmul(pair(AUX)[:, r0:r1], ones[:, :], tmp[:, t % 2, r0:r1], start=t == 0,
                                            stop=t == KT - 1)
                        ins.then_inc(sem("sq_used"), 1)
                    if kind == "norm":
                        pe.wait_ge(sem("n_lo"), at.v("n_lo", KT))

                elif kind == "mla_in":
                    for j, nt_j in enumerate((TOK if layer < DEPTH - 1 else LAT, TOK)):
                        for k in range(RKT):
                            project(at, 2 * j + k, k, j, H, KT, nt_j, whole)
                        for k in range(RKT):
                            pe.wait_ge(sem(f"free{k}"), at.v(f"free{k}", j + 1))
                        stats(at, prob, (0, 1), nt_j, j)
                    cut = lambda kt: slice(kt * P, kt * P + MLA_QK)
                    project(at, 4, 0, 2, H, KT // 2, TOK, cut, rows=MLA_QK, ktn=KT, piece=True)
                    project(at, 5, 0, None, H, KT // 2, TOK, cut, rows=MLA_QK, kt0=KT // 2, ktn=KT, piece=True)
                    pe.wait_ge(sem("free0"), at.v("free0", 3))
                    rotate(1, MLA_QK)

                elif kind == "mla_first":
                    pe.wait_ge(sem("v_lo"), at.v("v_lo"))
                    fill = mla_head(at, 0, 0, nt, ph["nmod"])
                    for n in range(6):
                        fill(n)
                    pe.wait_ge(sem("v_lo"), at.v("v_lo", 1))

                elif kind == "mla":
                    with pe.Fori(0, turns) as i:
                        t = At(ph, i)
                        for k in range(2):
                            attend(t, k, k, k, k, nt, MLA_QK, mla_head(t, k, 2 * i + (k + 1), nt, ph["nmod"]))
                            pe.wait_ge(sem("v_lo"), t.v("v_lo", k + 1))

                elif kind == "mla_last":
                    attend(at, 0, 0, 0, 0, nt, MLA_QK, mla_head(at, 0, MLA_HEADS - 1, nt, ph["nmod"]))
                    pe.wait_ge(sem("v_lo"), at.v("v_lo", 1))
                    attend(at, 1, 1, 1, 1, nt, MLA_QK)

                elif kind == "gqa":
                    with pe.Fori(0, turns) as i:
                        t = At(ph, i)
                        pe.wait_ge(sem("y_lo"), t.v("y_lo"))
                        project(t, 0, 0, 0, H, KT, TOK, whole)
                        pe.wait_ge(sem("free0"), t.v("free0", 1))
                        stats(t, tmp, (1,), TOK, 0)
                        project_v(t, 1, 1, 0, H, KT, whole).then_inc(sem("product"), 1)
                        pe.wait_ge(sem("v_norm"), t.v("v_norm", 1))
                        rotate(0, P)
                        pe.wait_ge(sem("free1"), t.v("free1", 1))
                        fills = [gqa_query(t, k, nt) for k in range(4)]
                        for n in range(6):
                            fills[0](n)
                        for k in range(4):
                            pe.wait_ge(sem("v_lo"), t.v("v_lo", k + 2))
                            attend(t, k, k % 2, 0, 0, nt, P, *fills[k + 1:k + 2])

                elif kind == "merge":
                    pe.wait_ge(sem("v_lo"), at.v("v_lo"))
                    pe.wait_ge(sem("y_lo"), at.v("y_lo"))
                    pe.wait_ge(sem("mod"), at.v("mod"))
                    with pe.Fori(0, turns) as i:
                        t = At(ph, i)
                        for k in range(2):
                            project(t, 2 * k, 0, k, H, KT, nt, whole)
                            project(t, 2 * k + 1, 1, k, Y, KT, nt, whole)

                elif kind == "ret":
                    units = 8 if nt > LAT else 6
                    with pe.Fori(0, turns) as i:
                        t = At(ph, i)
                        project(t, 0, 0, 0, H, KT, nt, whole)
                        project(t, 1, 1, 0, H, KT, TOK, whole)
                        pe.wait_ge(sem("free0"), t.v("free0", 1))
                        rotate(0, P)
                        project(t, 2, 0, 1, H, KT, nt, whole)
                        pe.wait_ge(sem("free1"), t.v("free1", 1))
                        pe.wait_ge(sem("v_s"), t.v("v_s", 1))
                        rotate(0, P)
                        project(t, 3, 1, 1, H, KT, nt, whole)
                        pe.wait_ge(sem("w_lo"), t.v("chunk", 6))
                        for e in range(2):
                            pe.wait_ge(sem(f"free{e}"), t.v(f"free{e}", 2))
                        assert t.slot(4) == 0
                        for tt in range(TOK // P):
                            for kt in range(KT):
                                ins = three([(ps[:, tt * 2 * P:(tt + 1) * 2 * P].rearrange("p (a b) -> p a b", b=P), None)],
                                            [x(kt, (tt * P, (tt + 1) * P)) for x in H],
                                            [lambda c, w=w: w[:, :, whole(kt)] for w in (wh, wl)],
                                            kt == 0, kt == KT - 1)
                        ins.then_inc(sem("product"), 2)
                        pe.wait_ge(sem("v_lo"), t.v("v_lo", 2))
                        for e in range(2):
                            pe.wait_ge(sem(f"free{e}"), t.v(f"free{e}", 3))

                        def span(u):
                            return (0, LAT) if u < 6 else (LAT, TOK)

                        def score(u):
                            if u >= 3:
                                pe.wait_ge(sem("rs_sd"), t.v("rs_sd", u - 2))
                            tile = u if u < 6 else u - 2
                            r0, r1 = span(u)
                            three([(ps[:, (4 + u % 3) * BANK:(4 + u % 3) * BANK + r1 - r0], (r0, r1))],
                                  [x[:, tile * P:(tile + 1) * P] for x in (kh, kl)],
                                  [lambda c, x=x: x[:, c[0]:c[1]] for x in (qh, ql)], True, True).then_inc(
                                sem("rs_ready"), 1)

                        score(0)
                        score(1)
                        for u in range(units):
                            if u + 2 < units:
                                score(u + 2)
                            pe.wait_ge(sem("rs_lo"), t.v("rs_lo", u + 1))
                            tile = u if u < 6 else u - 2
                            r0, r1 = span(u)
                            for e in range(2):
                                ins = three([(pair(e)[:, r0:r1], None)],
                                            [v[:, tile * 2 * P + e * P:tile * 2 * P + (e + 1) * P] for v in (vh_f, vl_f)],
                                            [lambda c, x=x: x[:, (u % 3) * LAT:(u % 3) * LAT + r1 - r0]
                                             for x in (pth_f, ptl_f)], u in (0, 6), u in (5, 7))
                            ins.then_inc(sem("rs_used"), 1)
                        for e in range(2):
                            pe.wait_ge(sem(f"free{e}"), t.v(f"free{e}", 4))
                        for r0, r1 in ranges(nt):
                            for e, x in enumerate((tmp[:, 0, r0:r1], prob[:, 2, r0:r1])):
                                ins = pe.matmul(pair(AUX)[:, r0:r1], ones[:, :], x, start=e == 0, stop=e == 1)
                        ins.then_inc(sem("v_stat"), 1)

                elif kind == "out":
                    name, kts, step = ("z_lo" if ph["mod"] == 2 else "f_lo"), ph["kt"], 1 + ph["nmod"]
                    pe.wait_ge(sem(name), at.v(name, 1 - kts))
                    late = {kt: (name, at.v(name, kt + 1 - kts)) for kt in range(1, kts)}
                    with pe.Fori(0, turns) as i:
                        t = At(ph, i)
                        for k in range(2):
                            project(t, k * step, k, 0, Y, kts, nt, whole, late=late)
                            for r in range(ph["nmod"]):
                                mod_chunk(t, k * step + 1 + r, 4 * i + (2 * KT * ph["group"] + 2 * k + r), MODS[1])

                elif kind == "ffn":
                    with pe.Fori(0, turns) as i:
                        t = At(ph, i)
                        for k in range(2):
                            for j in range(2):
                                project(t, 2 * k + j, j, k, H, KT, nt, whole)


def rope_table(dim, lead):
    half = dim // 4
    inv = (ROPE_BASE ** (-np.arange(half) / half)).astype(np.float32)
    tok = np.arange(LAT)
    c, s = np.ones((P, LAT)), np.zeros((P, LAT))
    for part, pos in enumerate((tok // GRID_W, tok % GRID_W)):
        ang = (inv[:, None] * pos[None, :].astype(np.float32)).astype(np.float64)
        for h in range(2):
            rows = slice(lead + (2 * part + h) * half, lead + (2 * part + h + 1) * half)
            c[rows], s[rows] = np.cos(ang), np.sin(ang)
    return np.stack([c, s], 1).astype(np.float32)


def perm_table(dim, lead):
    half = dim // 4
    m = np.zeros((P, P), np.float32)
    for part in range(2):
        for r in range(half):
            lo, hi = lead + 2 * part * half + r, lead + (2 * part + 1) * half + r
            m[hi, lo], m[lo, hi] = -1.0, 1.0
    return m


def decay_table():
    out = np.zeros((RET_HEADS, P, DEC), np.float64)
    p = np.arange(P)[:, None]
    for h in range(RET_HEADS):
        f, b = (np.log1p(-np.exp2(-(5.0 + off) - h)) for off in (0.0, 0.5))
        d = np.arange(DEC1)[None, :] - 3 * P - p
        out[h, :, :DEC1] = np.exp(f * np.maximum(d, 0)) * (d >= 0) + np.exp(b * np.maximum(-d, 0)) * (d <= 0)
        d = np.arange(DEC2)[None, :] - P - p
        out[h, :, DEC1:] = np.exp(f * (CTX + d)) + np.exp(b * (LAT - d))
    return out.astype(np.float32)


def stream_of(w):
    out = np.zeros((NCHUNK, P, CH), np.float32)
    n = 0

    def put(m, at=0, step=P):
        nonlocal n
        kt, cols = m.shape[0] // P, m.shape[1]
        out[n].reshape(P, CH // step, step)[:, :kt, at:at + cols] = m.reshape(kt, P, cols).transpose(1, 0, 2)
        n += 1

    for layer in range(DEPTH):
        win = w["w_in"][layer]
        col = lambda o, k=0, c=P: win[:, o + k * P:o + k * P + c]
        mod = lambda lay, j: put(w["w_mod"][lay][:, j * P:(j + 1) * P])
        if layer == 0:
            for j in range(2 * KT):
                mod(0, j)
        for o in (O_CQ, O_CKV):
            for k in range(RKT):
                put(col(o, k))
        for k in range(2):
            put(col(O_KR, 0, MLA_ROPE)[k * D // 2:(k + 1) * D // 2], at=MLA_NOPE)
        for h in range(MLA_HEADS):
            step = MLA_NOPE + MLA_V
            put(w["w_mla_kvb"][layer][:, h * step:(h + 1) * step], step=256)
            put(w["w_mla_qb"][layer][:, h * MLA_QK:(h + 1) * MLA_QK])
            if layer == 0:
                for r in range(4):
                    mod(0, 2 * KT + 4 * h + r)

        def merge(branch, name):
            for m in range(KT):
                put(col(O_GATE + branch * D, m))
                put(w[name][layer][:, m * P:(m + 1) * P])

        merge(1, "w_mla_o")
        for kv in range(GQA_KV):
            put(col(O_GK, kv))
            put(col(O_GV, kv))
            for h in range(GQA_HEADS // GQA_KV):
                put(col(O_GQ, kv * GQA_HEADS // GQA_KV + h))
        merge(2, "w_gqa_o")
        for h in range(RET_HEADS):
            put(col(O_RQ, h))
            put(col(O_RK, h))
            for o in (O_RG, O_RV):
                for e in range(2):
                    put(col(o, 2 * h + e))
        merge(0, "w_ret_o")
        for m in range(KT):
            put(w["w_out"][layer][:, m * P:(m + 1) * P])
        for g, (t0, tiles) in enumerate(GROUPS):
            for t in range(t0, t0 + tiles):
                for half in range(2):
                    put(w["w_ffn_in"][layer][:, half * FFN + t * P:half * FFN + (t + 1) * P])
            for m in range(KT):
                put(w["w_ffn_out"][layer][t0 * P:(t0 + tiles) * P, m * P:(m + 1) * P])
                if layer == 0:
                    for r in range(2):
                        mod(1, 2 * KT * g + 2 * m + r)
    assert n == NCHUNK
    return out


def kernel(**inputs):
    import concourse.bacc as bacc
    from concourse.bass_utils import run_bass_kernel_spmd as run

    w = {name: np.asarray(x) for name, x in inputs.items()}

    def tiles(v):
        return v.reshape(-1, P).T

    gains = [tiles(w[name][layer]) for layer in range(DEPTH)
             for name in ("g_mix", "g_ffn", "g_mla_q", "g_mla_kv", "g_gqa_q", "g_gqa_k")] + [tiles(w["g_final"])]
    arrays = {
        "xT": np.ascontiguousarray(np.concatenate([w["x"][0], w["ctx"][0]], 0).T),
        "cvec": np.ascontiguousarray(np.stack([tiles(w["c"][0]), tiles(w["c_ctx"])], 2)),
        "bmod": np.ascontiguousarray(np.stack([tiles(b) for b in w["b_mod"]], 1)),
        "gains": np.ascontiguousarray(np.concatenate(gains, 1)),
        "stream": stream_of(w),
        "rope": np.stack([rope_table(RET_DK, 0), rope_table(MLA_ROPE, MLA_NOPE)]),
        "perm": np.ascontiguousarray(np.stack([perm_table(RET_DK, 0), perm_table(MLA_ROPE, MLA_NOPE)], 1)),
        "ident": np.eye(P, dtype=np.float32),
        "dec": decay_table(),
    }
    nc = bacc.Bacc("TRN2", target_bir_lowering=False, num_devices=1, dynamic_dma_scratch_size=1024)
    a = {name: nc.dram_tensor(f"in_{name}", x.shape, mybir.dt.from_np(x.dtype), kind="ExternalInput").ap()
         for name, x in arrays.items()}
    a["out"] = nc.dram_tensor("out", (D, LAT), F32, kind="ExternalOutput").ap()
    build(nc, a)
    r = run(nc, [{f"in_{name}": x for name, x in arrays.items()}], core_ids=[0])
    return np.ascontiguousarray(r.results[0]["out"].T)[None]
```

```python
from contextlib import ExitStack

import numpy as np

import concourse.bass as bass
from concourse import mybir

F32 = mybir.dt.float32
F32R = mybir.dt.float32r
ALU = mybir.AluOpType
ACT = mybir.ActivationFunctionType
AX = mybir.AxisListType

P = 128
D = 1024
LAT = 512
CTX = 256
TOK = LAT + CTX
DEPTH = 2
KT = D // P
GRID_W = 64
ROPE_BASE = 10000.0
EPS = 1e-6

RET_HEADS, RET_DK, RET_DV = 4, 128, 256
MLA_HEADS, MLA_RANK, MLA_NOPE, MLA_ROPE, MLA_V = 8, 256, 64, 32, 128
MLA_QK = MLA_NOPE + MLA_ROPE
RKT = MLA_RANK // P
GQA_HEADS, GQA_KV, GQA_HD = 8, 2, 128
FFN = 2816
FT = FFN // P
GROUPS = [(0, 8), (8, 8), (16, 6)]
N_MOD = 6
EARLY = 2 * KT
CH = KT * P

O_RQ = 0
O_RK = O_RQ + RET_HEADS * RET_DK
O_RV = O_RK + RET_HEADS * RET_DK
O_RG = O_RV + RET_HEADS * RET_DV
O_CQ = O_RG + RET_HEADS * RET_DV
O_CKV = O_CQ + MLA_RANK
O_KR = O_CKV + MLA_RANK
O_GQ = O_KR + MLA_ROPE
O_GK = O_GQ + GQA_HEADS * GQA_HD
O_GV = O_GK + GQA_KV * GQA_HD
O_GATE = O_GV + GQA_KV * GQA_HD

G_LAYER = 2 * KT + 2 * RKT + 2
G_FINAL = DEPTH * G_LAYER
NGAIN = G_FINAL + KT

DEC1 = LAT + 3 * P
DEC2 = LAT + P
DEC = DEC1 + DEC2


def add(a, b, times=1):
    out = dict(a)
    for name, n in b.items():
        out[name] = out.get(name, 0) + n * times
    return out


PLAIN = {"e_hi": 1}
VECTOR = {"m_in": 1, "m_prod": 1, "m_row": 1, "m_fold": 1, "m_add": 1}
VALUES = {"vt": 1, "vt_hi": 1, "vt_lo": 1}
ROPED = {"v_perm": 1, "v_c": 1, "v_s": 1, "v_full": 1, "v_hi": 1, "v_lo": 1}
NORMED = {"v_stat": 1, "v_std": 1, "v_rstd": 1, "v_norm": 1}


LAG = {"s_rinv": 1, "s_pn": 1, "t_ready": 2, "t_hi": 2, "t_lo": 2, "y_ready": 2, "y_hi": 2, "y_lo": 2}


def attention(nq, first=0, last=0):
    out = {name: nq for name in ("s_ready", "s_max", "s_nm", "s_exp")}
    for name, lag in LAG.items():
        out[name] = (nq // 2 if name[0] == "y" else nq) + lag * (last - first)
    return out


def total(*parts):
    out = {}
    for part in parts:
        out = add(out, part)
    return out


def plan():
    phases, now = [], {"f_lo": 2, "y_lo": 1, "m_add": 1}

    def phase(kind, layer, turns, per, once=(), **args):
        nonlocal now
        once = dict(once)
        phases.append(dict(kind=kind, layer=layer, turns=turns, per=per, base=dict(now), once=once, **args))
        now = add(add(now, once), per, turns)

    for layer in range(DEPTH):
        full = layer < DEPTH - 1
        nt = TOK if full else LAT
        nq = nt // P
        units = 8 if full else 6
        squares = {"sq": KT, "sq_used": KT, "n_std": 1, "n_rstd": 1}
        norm = {"n_t1": KT, "n_hi": KT, "n_full": KT, "n_lo": KT}
        if layer == 0:
            phase("squares", layer, 0, {}, squares, nt=TOK)
            phase("mod", layer, 0, {}, {"m_prod": 4, "m_row": 4, "m_fold": 1, "m_add": 1})
        phase("mods", layer, 0, {}, {"mod": 1 + layer}, gains=range(1 + layer))
        summed = {"sq_used": 1, "n_std": 1, "n_rstd": 1}
        if layer:
            phase("summed", layer, 0, {}, summed, nt=TOK)
        phase("norm", layer, 0, {}, norm, nt=TOK, first=True)
        phase("mla_in", layer, 0, {}, total(
            {"chunk": 6, "free0": 3, "free1": 2, "v_stat": 2, "v_std": 2, "v_rstd": 2,
             "v_norm": 4, "v_hi": 5, "v_lo": 5, "tab": 1}, ROPED))
        head = total({"chunk": 2, "free0": 3, "k_ready": 1}, PLAIN, PLAIN, ROPED)
        att = attention(nq)
        phase("mla_first", layer, 0, {}, total(head, head, attention(nq, first=1)), nt=nt)
        phase("mla", layer, MLA_HEADS // 2 - 1, total(head, head, att, att), nt=nt)
        phase("mla_last", layer, 0, {}, attention(nq, last=1), nt=nt)
        nmod = 1 - layer
        merge = total({"chunk": 4, "free0": 2, "free1": 2, "mg_add": 2}, *[VECTOR] * (2 * nmod))
        phase("merge", layer, KT // 2, add(merge, {"mg_add": -2}), nt=nt, first=True, nmod=nmod, j0=2 * KT)
        phase("gqa_in", layer, 0, {}, total(
            {"tab": 1}, *[total({"chunk": 2, "free0": 1, "free1": 1}, VALUES, ROPED, NORMED)] * GQA_KV))
        query = total({"chunk": 1, "free0": 1}, NORMED, ROPED)
        phase("gqa_first", layer, 0, {}, total(query, query, attention(nq, first=1)), nt=nt)
        phase("gqa", layer, GQA_HEADS // 2 - 1, total(query, query, att, att), nt=nt)
        phase("gqa_last", layer, 0, {}, attention(nq, last=1), nt=nt)
        phase("merge", layer, KT // 2, merge, nt=nt, first=False, nmod=nmod, j0=3 * KT)
        phase("ret", layer, RET_HEADS, total(
            {"chunk": 6, "free0": 4, "free1": 4, "dec": 1, "rs_ready": units, "rs_sd": units,
             "rs_hi": units, "rs_lo": units, "rs_used": units, "v_stat": 1, "v_std": 1, "v_rstd": 1,
             "y_sq": 2, "v_full": 2, "v_hi": 2, "v_lo": 2}, ROPED, ROPED, VALUES), nt=nt)
        phase("merge", layer, KT // 2, merge, nt=nt, first=False, nmod=nmod, j0=4 * KT)
        phase("z", layer, 0, {}, {"z_hi": KT, "z_lo": KT}, nt=nt)
        phase("zero", layer, 0, {}, {"o_acc": 2})
        sums = {"o_sq": 2, "o_acc": 2}
        phase("out", layer, KT // 2, total({"chunk": 2, "free0": 1, "free1": 1}, sums, *[VECTOR] * (2 * nmod)),
              nt=nt, kt=KT, mod=2, nmod=nmod, j0=5 * KT, home=0, sums=True)
        if layer == 0:
            phase("mods", layer, 0, {}, {"mod": 1}, gains=(1,))
        phase("summed", layer, 0, {}, summed, nt=nt)
        phase("norm", layer, 0, {}, norm, nt=nt, first=False)
        for g, (t0, n) in enumerate(GROUPS):
            phase("ffn", layer, n // 2, {"chunk": 4, "free0": 2, "free1": 2, "f_hi": 2, "f_lo": 2},
                  nt=nt)
            nmod = 2 - 2 * layer
            last = g == len(GROUPS) - 1
            if last:
                phase("zero", layer, 0, {}, {"o_acc": 2})
            phase("out", layer, KT // 2, total({"chunk": 2, "free0": 1, "free1": 1}, sums if last else {},
                                               *[VECTOR] * (2 * nmod)),
                  nt=nt, kt=n, mod=5, nmod=nmod, j0=2 * KT * g, home=1, sums=last)
    phase("summed", DEPTH - 1, 0, {}, summed, nt=LAT)
    phase("final", DEPTH - 1, 0, {}, {}, nt=LAT)
    return phases, now


PHASES, TOTALS = plan()
NCHUNK = TOTALS["chunk"]


class At:

    def __init__(self, ph, i=0, end=False):
        self.base, self.per, self.i = ph["base"], ph["per"], i
        if end:
            self.base, self.i = add(add(ph["base"], ph["once"]), ph["per"], ph["turns"]), 0

    def v(self, name, k=0):
        per = self.per.get(name, 0)
        at = self.base.get(name, 0) + k
        return at + self.i * per if per else at

    def slot(self, k):
        return (self.base.get("chunk", 0) + k) % 2

    def half(self, k):
        return (self.base.get("chunk", 0) + k) // 2 + 1 + self.i * (self.per.get("chunk", 0) // 2)


class Tiles:

    def __init__(self, at, ka, nq, first):
        self.at, self.ka, self.nq, self.first = at, ka, nq, first

    def v(self, name, m):
        n = self.nq // 2 if name[0] == "y" else self.nq
        return self.at.v(name, self.ka * n + m + 1 + (0 if self.first else LAG.get(name, 0)))

    def steps(self, last):
        return self.nq + (3 if last else 0)

    def has(self, m):
        return m < self.nq and (m >= 0 or not self.first)

    def prob(self, m):
        return m % self.nq % (4 if self.nq == 4 else 3)

    def span(self, m):
        return 6 if m % self.nq < 4 else 2


def ranges(nt):
    return [(0, LAT)] + ([(LAT, nt)] if nt > LAT else [])


def build(nc, a):
    ctx = ExitStack()
    with ctx:
        def sb(name, shape, dt=F32):
            return ctx.enter_context(nc.sbuf_tensor(name, shape, dt))

        sems = {}

        def sem(name):
            if name not in sems:
                sems[name] = ctx.enter_context(nc.semaphore(name))
            return sems[name]

        at = (nc.sbuf_base + 31) // 32 * 32
        arena = sb("arena", [P, KT * TOK + 8])
        xz = nc.alloc_sbuf_tensor_at("xz", [P, KT, TOK], F32, offset=at)
        ranks = nc.alloc_sbuf_tensor_at("ranks", [P, 2, 2, RKT, TOK], F32R, offset=at)
        at = (nc.sbuf_base + 31) // 32 * 32
        early = nc.alloc_sbuf_tensor_at("early", [P, EARLY, CH], F32, offset=at)
        hh, hl = sb("hh", [P, KT, TOK], F32R), sb("hl", [P, KT, TOK], F32R)
        yh, yl = sb("yh", [P, KT, TOK], F32R), sb("yl", [P, KT, TOK], F32R)
        raw = sb("raw", [P, 2, CH])
        wh, wl = sb("wh", [P, 2, CH], F32R), sb("wl", [P, 2, CH], F32R)
        kh, kl = sb("kh", [P, TOK], F32R), sb("kl", [P, TOK], F32R)
        qh, ql = sb("qh", [P, TOK], F32R), sb("ql", [P, TOK], F32R)
        q2h, q2l = sb("q2h", [P, TOK], F32R), sb("q2l", [P, TOK], F32R)
        vh, vl = sb("vh", [P, 2, TOK], F32R), sb("vl", [P, 2, TOK], F32R)
        tmp = sb("tmp", [P, 3, TOK])
        prob = sb("prob", [P, 4, TOK])
        pth, ptl = sb("pth", [P, 6, 2 * P], F32R), sb("ptl", [P, 6, 2 * P], F32R)
        rope = sb("rope", [P, 2, LAT])
        at = (nc.sbuf_base + 31) // 32 * 32
        fence = sb("fence", [P, DEC + 8])
        dec = nc.alloc_sbuf_tensor_at("dec", [P, DEC], F32, offset=at)
        k2h = nc.alloc_sbuf_tensor_at("k2h", [P, TOK], F32R, offset=at)
        k2l = nc.alloc_sbuf_tensor_at("k2l", [P, TOK], F32R, offset=at + 4 * TOK)
        mraw = nc.alloc_sbuf_tensor_at("mraw", [P, CH], F32, offset=at)
        keys, queries = ((kh, kl), (k2h, k2l)), ((qh, ql), (q2h, q2l))
        prob_f = prob[:, :, :].rearrange("p a b -> p (a b)")
        perm = sb("perm", [P, 2, P])
        ident, ones = sb("ident", [P, P]), sb("ones", [P, P])
        eps = sb("eps", [P, 1])
        gains = sb("gains", [P, NGAIN])
        bmod = sb("bmod", [P, DEPTH, N_MOD * KT])
        cvec, csil = sb("cvec", [P, KT, 2]), sb("csil", [P, KT, 2])
        mods = sb("mods", [P, DEPTH, N_MOD * KT, 2])
        gm = sb("gm", [P, 2, KT, 2])
        mx, nm = sb("mx", [P, 6]), sb("nm", [P, 6])
        mark = sb("mark", [P, 4])
        rs, ri = sb("rs", [P, 6]), sb("ri", [P, 6])
        qsc = sb("qsc", [P, 2, 6])
        ps = ctx.enter_context(nc.psum_tensor("ps", [P, 8 * LAT], F32))
        BANK = LAT

        def home(kind, i, k=0):
            def at(b):
                n = k if b >= 0 else k - 1
                if kind.startswith("mla"):
                    return 2 * i + n
                return i + (n // 2 + GQA_HEADS // GQA_KV * (n % 2))
            return at

        def pair(slot):
            return ps[:, 2 * BANK * slot:2 * BANK * slot + TOK]

        AUX = 2
        TURN = 0
        TRANS = 2 * BANK
        OUTS = TRANS + TOK
        SCORES = (4 * BANK, 6 * BANK)
        QSUM = TOK
        ROW = 5 * BANK
        FOLD = (6 * BANK, 7 * BANK)

        vh_f = vh[:, :, :].rearrange("p a b -> p (a b)")
        vl_f = vl[:, :, :].rearrange("p a b -> p (a b)")
        pth_f = pth[:, :, :].rearrange("p a b -> p (a b)")
        ptl_f = ptl[:, :, :].rearrange("p a b -> p (a b)")
        xspill = nc.dram_tensor("xspill", (D, TOK), F32, kind="Internal").ap()

        block = ctx.enter_context(nc.Block())

        @block.sync
        def _(sp):
            for t in range(KT):
                sp.dma_start(xz[:, t, :], a["xT"][t * P:(t + 1) * P, :]).then_inc(sem("x_in"), 16)
            for s in range(2):
                sp.dma_start(raw[:, s, :], a["stream"][s]).then_inc(sem(f"raw_in{s}"), 16)
            for j in range(EARLY):
                sp.dma_start(early[:, j, :], a["wmod"][j]).then_inc(sem(f"early{j // 4}"), 16)
            with sp.Fori(1, NCHUNK // 2) as i:
                for s in range(2):
                    sp.wait_ge(sem("w_lo"), 2 * i + (s - 1))
                    src = a["stream"][bass.ds(2 * i + s, 1)].rearrange("a p n -> (a p) n")
                    sp.dma_start(raw[:, s, :], src).then_inc(sem(f"raw_in{s}"), 16)
            sp.wait_ge(sem("out_done"), 16 * KT)

        @block.scalar
        def _(act):
            def split(at, k):
                s = at.slot(k)
                act.wait_ge(sem(f"raw_in{s}"), at.half(k) * 16)
                used = at.v("chunk", k - 1)
                if not isinstance(used, int) or used > 0:
                    act.wait_ge(sem("product"), used)
                act.activation(wh[:, s, :], raw[:, s, :], ACT.Copy).then_inc(sem("w_hi"), 1)

            def plain(at, kc, slot, dst, rows=P, nt=TOK):
                act.wait_ge(sem("product"), at.v("chunk", kc + 1))
                act.activation(dst[0:rows, 0:nt], pair(slot)[0:rows, 0:nt], ACT.Copy).then_inc(sem("e_hi"), 1)

            def std(at, k, nt, n, rows=P):
                act.wait_ge(sem("v_stat"), at.v("v_stat", k + 1))
                act.activation(tmp[0:rows, 2, 0:nt], pair(AUX)[0:rows, 0:nt], ACT.Sqrt, bias=eps[0:rows, :],
                               scale=1.0 / n).then_inc(sem("v_std"), 1)

            def roped(at, kc, kv, kf, slot, dst, rows, r0, nt, scale=1.0, before=lambda: None):
                act.wait_ge(sem("product"), at.v("chunk", kc + 1))
                act.wait_ge(sem("v_lo"), at.v("v_lo", kv))
                act.activation(tmp[0:rows, 0, 0:nt], pair(slot)[0:rows, 0:nt], ACT.Copy,
                               scale=scale).then_inc(sem(f"free{slot}"), 1)
                before()
                act.wait_ge(sem("v_full"), at.v("v_full", kf + 1))
                act.activation(dst[r0:rows, 0:nt], tmp[r0:rows, 0, 0:nt], ACT.Copy).then_inc(sem("v_hi"), 1)

            def heads(ph):
                if ph["kind"].startswith("mla"):
                    return (lambda at, kp, par: mla_head(at, kp, par, ph["nt"])), lambda par: lambda n: MLA_QK ** -0.5
                return ((lambda at, kq, par: gqa_query(at, kq, par, ph["nt"], ph["layer"])),
                        lambda par: lambda n: qsc[:, par, n:n + 1])

            def attend(at, ka, nt, scale, home, fill=lambda n: None, first=False, last=False):
                c = Tiles(at, ka, nt // P, first)
                for n in range(c.steps(last)):
                    if n < c.nq:
                        w = TOK if n < 4 else CTX
                        act.wait_ge(sem("s_nm"), c.v("s_nm", n))
                        slots = 4 if c.nq == 4 else 3
                        if c.has(n - slots):
                            act.wait_ge(sem("t_ready"), c.v("t_ready", n - slots))
                        s0 = SCORES[n % 2]
                        act.activation(prob[:, c.prob(n), 0:w], ps[:, s0:s0 + w], ACT.Exp, bias=nm[:, n:n + 1],
                                       scale=scale(n), accum_out=rs[:, n:n + 1]).then_inc(sem("s_exp"), 1)
                    if n % 2 == 0:
                        if c.has(n - 3):
                            y_hi(c, n // 2 - 2, home)
                        fill(n)
                    m = n - 2
                    if c.has(m):
                        st = c.span(m)
                        act.wait_ge(sem("t_ready"), c.v("t_ready", m))
                        act.activation(pth[:, 0:st, (m % 2) * P:(m % 2) * P + P],
                                       ps[:, TRANS:TRANS + st * P].rearrange("p (s q) -> p s q", q=P),
                                       ACT.Copy).then_inc(sem("t_hi"), 1)
                    if n % 2:
                        fill(n)

            def y_hi(c, b, home):
                col = 2 * P * (b % (c.nq // 2))
                act.wait_ge(sem("y_ready"), c.v("y_ready", b))
                act.activation(yh[:, bass.ds(home(b), 1), col:col + 2 * P], ps[:, OUTS:OUTS + 2 * P],
                               ACT.Copy).then_inc(sem("y_hi"), 1)

            def mla_head(at, kp, par, nt):
                def fill(n):
                    if n == 0:
                        split(at, 2 * kp + 1)
                        act.wait_ge(sem("product"), at.v("chunk", 2 * kp + 1))
                        act.wait_ge(sem("v_lo"), at.v("v_lo", kp))
                        act.activation(tmp[0:MLA_QK, 0, 0:nt], pair(0)[0:MLA_QK, 0:nt], ACT.Copy).then_inc(
                            sem("free0"), 1)
                    if n == 2:
                        act.wait_ge(sem("v_full"), at.v("v_full", kp + 1))
                        act.activation(queries[par][0][0:MLA_QK, 0:nt], tmp[0:MLA_QK, 0, 0:nt],
                                       ACT.Copy).then_inc(sem("v_hi"), 1)
                        act.wait_ge(sem("k_ready"), at.v("k_ready", kp + 1))
                        act.activation(keys[par][0][0:MLA_NOPE, :], pair(0)[0:MLA_NOPE, :], ACT.Copy).then_inc(
                            sem("e_hi"), 1)
                    if n == 3:
                        split(at, 2 * kp + 2)
                        plain(at, 2 * kp + 1, 0, vh[:, par, :])
                return fill

            def gqa_query(at, kq, par, nt, layer):
                col = layer * G_LAYER + 2 * KT + 2 * RKT

                def fill(n):
                    if n == 0:
                        split(at, kq + 1)
                    if n == 1:
                        act.wait_ge(sem("product"), at.v("chunk", kq + 1))
                        act.wait_ge(sem("v_lo"), at.v("v_lo", kq))
                        act.activation(tmp[:, 0, 0:nt], pair(0)[:, 0:nt], ACT.Copy, scale=gains[:, col:col + 1])
                        act.activation(tmp[:, 2, 0:nt], pair(0)[:, 0:nt], ACT.Square).then_inc(sem("free0"), 1)
                    if n == 3:
                        act.wait_ge(sem("v_stat"), at.v("v_stat", kq + 1))
                        act.activation(qsc[:, par, 0:nt // P], ps[:, QSUM:QSUM + nt // P], ACT.Sqrt,
                                       bias=eps[:, :], scale=1.0 / GQA_HD).then_inc(sem("v_std"), 1)
                        act.wait_ge(sem("v_full"), at.v("v_full", kq + 1))
                        act.activation(queries[par][0][:, 0:nt], tmp[:, 0, 0:nt], ACT.Copy).then_inc(
                            sem("v_hi"), 1)
                return fill

            def mod_load(j):
                act.dma_start(mraw[:, :], a["wmod"][bass.ds(j, 1)].rearrange("a p n -> (a p) n")).then_inc(
                    sem("m_in"), 16)

            def mod_row(at, km):
                act.wait_ge(sem("m_prod"), at.v("m_prod", km + 1))
                act.activation(tmp[0:2, 2, (km % 2) * P:(km % 2 + 1) * P], ps[0:2, ROW:ROW + P],
                               ACT.Copy).then_inc(sem("m_row"), 1)

            def root(at, n, nt):
                act.wait_ge(sem("sq_used"), at.v("sq_used", n))
                act.activation(tmp[:, 2, 0:nt], pair(AUX)[:, 0:nt], ACT.Sqrt, bias=eps[:, :],
                               scale=1.0 / D).then_inc(sem("n_std"), 1)

            def square(t, i, k, nt):
                act.wait_ge(sem(f"free{k}"), t.v(f"free{k}", 1))
                act.wait_ge(sem("o_acc"), t.v("o_acc", k - 1))
                act.activation(tmp[:, k:k + 1, 0:nt], xz[:, bass.ds(2 * i + k, 1), 0:nt],
                               ACT.Square).then_inc(sem("o_sq"), 1)

            def load_x(src, t):
                act.dma_start(xz[:, t, :], src[t * P:(t + 1) * P, :]).then_inc(sem("x_in"), 16)

            act.dma_start(cvec[:, :, :], a["cvec"]).then_inc(sem("c_in"), 16)
            for dst, name in ((gains[:, :], "gains"), (bmod[:, :, :], "bmod"), (perm[:, :, :], "perm"),
                              (ident[:, :], "ident")):
                act.dma_start(dst, a[name]).then_inc(sem("const_in"), 16)
            act.wait_ge(sem("c_in"), 16)
            act.activation(csil[:, :, :], cvec[:, :, :], ACT.Silu).then_inc(sem("c_silu"), 1)
            act.wait_ge(sem("const_in"), 64)
            act.wait_ge(sem("eps_set"), 1)
            split(At(PHASES[0]), 0)

            for ph in PHASES:
                kind, layer, at, end = ph["kind"], ph["layer"], At(ph), At(ph, end=True)
                nt, turns = ph.get("nt"), ph["turns"]
                if kind == "mod":
                    for g in range(EARLY // 4):
                        act.wait_ge(sem("m_prod"), g + 1)
                        act.activation(prob_f[0:2, g * BANK:(g + 1) * BANK], ps[0:2, (4 + g) * BANK:(5 + g) * BANK],
                                       ACT.Copy).then_inc(sem("m_row"), 1)

                elif kind == "squares":
                    act.wait_ge(sem("x_in"), 16 * KT)
                    for t in range(KT):
                        if t >= 2:
                            act.wait_ge(sem("sq_used"), at.v("sq_used", t - 1))
                        act.activation(tmp[:, t % 2, 0:nt], xz[:, t, 0:nt], ACT.Square).then_inc(sem("sq"), 1)
                    root(at, KT, nt)

                elif kind == "summed":
                    root(at, 1, nt)

                elif kind == "norm":
                    gi = 0 if ph["first"] else 1
                    if layer and ph["first"]:
                        for t in range(KT):
                            act.dma_start(xspill[t * P:(t + 1) * P, :], xz[:, t, :]).then_inc(sem("x_out"), 16)
                    act.wait_ge(sem("mod"), at.v("mod"))
                    for t in range(KT):
                        act.wait_ge(sem("n_t1"), at.v("n_t1", t + 1))
                        for u, (r0, r1) in enumerate(ranges(nt)):
                            ins = act.activation(hh[:, t, r0:r1], tmp[:, t % 2, r0:r1], ACT.Identity,
                                                 bias=mods[:, layer, 3 * gi * KT + t, u:u + 1],
                                                 scale=gm[:, gi, t, u:u + 1])
                        ins.then_inc(sem("n_hi"), 1)

                elif kind == "mla_in":
                    if layer:
                        act.wait_ge(sem("x_out"), 16 * KT)
                    act.dma_start(rope[:, :, :], a["rope"][1]).then_inc(sem("tab_in"), 16)
                    for j, (nt_j, which) in enumerate(((TOK if layer < DEPTH - 1 else LAT, 0), (TOK, 1))):
                        for k in range(RKT):
                            split(at, 2 * j + k + 1)
                            act.wait_ge(sem("product"), at.v("chunk", 2 * j + k + 1))
                            if j:
                                act.wait_ge(sem("v_lo"), at.v("v_lo", 2))
                            elif k == 0:
                                act.wait_ge(sem("n_lo"), at.v("n_lo"))
                            act.activation(tmp[:, k, 0:nt_j], pair(k)[:, 0:nt_j], ACT.Copy)
                            act.activation(prob[:, k, 0:nt_j], pair(k)[:, 0:nt_j],
                                           ACT.Square).then_inc(sem(f"free{k}"), 1)
                        std(at, j, nt_j, MLA_RANK)
                        for k in range(RKT):
                            act.wait_ge(sem("v_norm"), at.v("v_norm", 2 * j + k + 1))
                            act.activation(ranks[:, which, 0, k, 0:nt_j], tmp[:, k, 0:nt_j],
                                           ACT.Copy).then_inc(sem("v_hi"), 1)
                    split(at, 5)
                    split(at, 6)
                    roped(at, 5, 4, 0, 0, kh, MLA_QK, MLA_NOPE, TOK)
                    act.activation(k2h[MLA_NOPE:MLA_QK, :], tmp[MLA_NOPE:MLA_QK, 0, :], ACT.Copy).then_inc(
                        sem("v_hi"), 1)

                elif kind in ("mla_first", "gqa_first"):
                    head, scale = heads(ph)
                    fill = head(at, 0, 0)
                    for n in range(4):
                        fill(n)
                    attend(at, 0, nt, scale(0), home(kind, 0), head(at, 1, 1), first=True)

                elif kind in ("mla", "gqa"):
                    head, scale = heads(ph)
                    with act.Fori(0, turns) as i:
                        t = At(ph, i)
                        for k in range(2):
                            attend(t, k, nt, scale(1 - k), home(kind, i, k + 1), head(t, k, k))

                elif kind in ("mla_last", "gqa_last"):
                    attend(at, 0, nt, heads(ph)[1](1), home(kind, MLA_HEADS // 2 - 1, 1), last=True)

                elif kind == "gqa_in":
                    act.wait_ge(sem("free1"), at.v("free1"))
                    act.dma_start(rope[:, :, :], a["rope"][0]).then_inc(sem("tab_in"), 16)
                    for j in range(GQA_KV):
                        split(at, 2 * j + 1)
                        act.wait_ge(sem("product"), at.v("chunk", 2 * j + 1))
                        act.wait_ge(sem("v_lo"), at.v("v_lo", j))
                        act.activation(tmp[:, 0, :], pair(0)[:, :], ACT.Copy)
                        act.activation(tmp[:, 1, :], pair(0)[:, :], ACT.Square).then_inc(sem("free0"), 1)
                        split(at, 2 * j + 2)
                        act.wait_ge(sem("product"), at.v("chunk", 2 * j + 2))
                        act.activation(prob[:, 0, :], pair(1)[:, :], ACT.Copy).then_inc(sem("free1"), 1)
                        std(at, j, TOK, GQA_HD)
                        act.wait_ge(sem("vt"), at.v("vt", j + 1))
                        act.activation(vh[:, j, :], pair(1)[:, :], ACT.Copy).then_inc(sem("vt_hi"), 1)
                        act.wait_ge(sem("v_full"), at.v("v_full", j + 1))
                        act.activation(keys[j][0][:, :], tmp[:, 0, :], ACT.Copy).then_inc(sem("v_hi"), 1)

                elif kind == "merge":
                    with act.Fori(0, turns) as i:
                        t = At(ph, i)
                        for k in range(2):
                            c = 2 * k
                            if ph["nmod"]:
                                mod_load(2 * i + (ph["j0"] + k))
                            split(t, c + 1)
                            act.wait_ge(sem("v_lo"), at.v("v_lo"))
                            act.wait_ge(sem("y_lo"), at.v("y_lo"))
                            act.wait_ge(sem("product"), t.v("chunk", c + 1))
                            act.wait_ge(sem("free1"), t.v("free1", k - 1))
                            act.activation(tmp[:, k, 0:nt], pair(0)[:, 0:nt],
                                           ACT.Sigmoid).then_inc(sem("free0"), 1)
                            if ph["nmod"]:
                                mod_row(t, k)
                            split(t, c + 2)

                elif kind == "ret":
                    act.wait_ge(sem("free1"), at.v("free1"))
                    split(at, 1)

                    def turn(i, last=False):
                        t = At(ph, i)
                        act.dma_start(dec[:, :], a["dec"][bass.ds(i, 1)].rearrange("a p n -> (a p) n")).then_inc(
                            sem("dec_in"), 16)
                        act.wait_ge(sem("v_lo"), t.v("v_lo"))
                        for e in range(2):
                            if e:
                                split(t, 2)
                            act.wait_ge(sem("product"), t.v("chunk", e + 1))
                            act.activation(prob[:, e, :], pair(e)[:, :], ACT.Copy).then_inc(sem(f"free{e}"), 1)
                        split(t, 3)
                        act.wait_ge(sem("product"), t.v("chunk", 3))
                        act.activation(tmp[:, 0, 0:nt], pair(0)[:, 0:nt], ACT.Copy).then_inc(sem("free0"), 1)
                        act.wait_ge(sem("vt"), t.v("vt", 1))
                        act.activation(vh_f[:, :], ps[:, 5 * BANK:8 * BANK], ACT.Copy).then_inc(sem("vt_hi"), 1)
                        split(t, 4)
                        act.wait_ge(sem("v_full"), t.v("v_full", 1))
                        act.activation(qh[:, 0:nt], tmp[:, 0, 0:nt], ACT.Copy).then_inc(sem("v_hi"), 1)
                        roped(t, 3, 1, 1, 1, kh, P, 0, TOK, scale=RET_DK ** -0.5, before=lambda: split(t, 5))
                        for e in range(2):
                            act.wait_ge(sem("product"), t.v("chunk", 5 + e))
                            if e == 0:
                                act.wait_ge(sem("v_lo"), t.v("v_lo", 2))
                            act.activation(tmp[:, 1 + e, 0:nt], pair(e)[:, 0:nt], ACT.Silu).then_inc(
                                sem(f"free{e}"), 1)
                            if e == 0:
                                split(t, 6)
                        units = 8 if nt > LAT else 6
                        for u in range(units):
                            w = LAT if u < 6 else CTX
                            act.wait_ge(sem("rs_sd"), t.v("rs_sd", u + 1))
                            if u >= 3:
                                act.wait_ge(sem("rs_used"), t.v("rs_used", u - 2))
                            act.activation(pth_f[:, (u % 3) * LAT:(u % 3) * LAT + w], prob[:, u % 3, 0:w],
                                           ACT.Copy).then_inc(sem("rs_hi"), 1)
                        act.wait_ge(sem("rs_used"), t.v("rs_used", units))
                        for e in range(2):
                            act.activation((tmp[:, 0, 0:nt], prob[:, 2, 0:nt])[e], pair(e)[:, 0:nt],
                                           ACT.Square).then_inc(sem("y_sq"), 1)
                        if not last:
                            split(t, 7)
                        act.wait_ge(sem("v_stat"), t.v("v_stat", 1))
                        act.activation(prob[:, 2, 0:nt], pair(AUX)[:, 0:nt], ACT.Sqrt, bias=eps[:, :],
                                       scale=1.0 / RET_DV).then_inc(sem("v_std"), 1)
                        for e in range(2):
                            act.wait_ge(sem("v_full"), t.v("v_full", 3 + e))
                            act.activation(yh[:, bass.ds(2 * i + e, 1), 0:nt], prob[:, e, 0:nt],
                                           ACT.Copy).then_inc(sem("v_hi"), 1)

                    with act.Fori(0, turns - 1) as i:
                        turn(i)
                    turn(turns - 1, last=True)

                elif kind == "z":
                    act.wait_ge(sem("mg_add"), at.v("mg_add"))
                    for t in range(KT + 2):
                        if t < KT:
                            act.activation(yh[:, t, 0:nt], xz[:, t, 0:nt], ACT.Copy).then_inc(sem("z_hi"), 1)
                        if t >= 2:
                            act.wait_ge(sem("z_lo"), at.v("z_lo", t - 1))
                            load_x(xspill if layer else a["xT"], t - 2)

                elif kind == "out":
                    if at.v("chunk") + 2 * turns < NCHUNK:
                        with act.Fori(0, turns) as i:
                            t = At(ph, i)
                            for k in range(2):
                                for km in range(k * ph["nmod"], (k + 1) * ph["nmod"]):
                                    mod_load(2 * ph["nmod"] * i + (ph["j0"] + ph["home"] * N_MOD * KT + km))
                                    if km == k * ph["nmod"]:
                                        split(t, k + 1)
                                    mod_row(t, km)
                                if not ph["nmod"]:
                                    split(t, k + 1)
                                if ph["sums"]:
                                    square(t, i, k, nt)
                    else:
                        with act.Fori(0, turns - 1) as i:
                            for k in range(2):
                                split(At(ph, i), k + 1)
                                square(At(ph, i), i, k, nt)
                        split(At(ph, turns - 1), 1)
                        for k in range(2):
                            square(At(ph, turns - 1), turns - 1, k, nt)

                elif kind == "ffn":
                    with act.Fori(0, turns) as i:
                        t = At(ph, i)
                        for k in range(2):
                            split(t, 2 * k + 1)
                            act.wait_ge(sem("product"), t.v("chunk", 2 * k + 1))
                            act.wait_ge(sem("free1"), t.v("free1", k - 1))
                            act.activation(tmp[:, k, 0:nt], pair(0)[:, 0:nt], ACT.Silu).then_inc(sem("free0"), 1)
                            split(t, 2 * k + 2)
                            act.wait_ge(sem("free1"), t.v("free1", k + 1))
                            act.activation(yh[:, bass.ds(2 * i + k, 1), 0:nt], prob[:, k, 0:nt],
                                           ACT.Copy).then_inc(sem("f_hi"), 1)

                elif kind == "final":
                    for t in range(KT):
                        act.wait_ge(sem("o_ready"), t + 1)
                        act.dma_start(a["out"][t * P:(t + 1) * P, :], xz[:, t, 0:LAT]).then_inc(sem("out_done"), 16)
                    act.wait_ge(sem("out_done"), 16 * KT)

        @block.vector
        def _(dve):
            def split(at, k):
                s = at.slot(k)
                dve.wait_ge(sem("w_hi"), at.v("chunk", k + 1))
                dve.tensor_tensor(wl[:, s, :], raw[:, s, :], wh[:, s, :].bitcast(F32), ALU.subtract).then_inc(
                    sem("w_lo"), 1)

            def plain(at, ke, slot, hi, lo, rows=P, nt=TOK):
                dve.wait_ge(sem("e_hi"), at.v("e_hi", ke + 1))
                dve.tensor_tensor(lo[0:rows, 0:nt], pair(slot)[0:rows, 0:nt], hi[0:rows, 0:nt].bitcast(F32),
                                  ALU.subtract).then_inc(sem(f"free{slot}"), 1)

            def rstd(at, k, nt):
                dve.wait_ge(sem("v_std"), at.v("v_std", k + 1))
                dve.reciprocal(tmp[:, 2, 0:nt], tmp[:, 2, 0:nt]).then_inc(sem("v_rstd"), 1)
                dve.wait_ge(sem("v_rstd"), at.v("v_rstd", k + 1))

            def roped(at, kv, kp, slot, kfree, hi, lo, rows, r0, nt, bank=6 * BANK):
                dve.wait_ge(sem(f"free{slot}"), at.v(f"free{slot}", kfree))
                dve.tensor_tensor(tmp[0:rows, 1, 0:LAT], tmp[0:rows, 0, 0:LAT], rope[0:rows, 0, :],
                                  ALU.mult).then_inc(sem("v_c"), 1)
                dve.wait_ge(sem("v_perm"), at.v("v_perm", kp + 1))
                dve.tensor_tensor(tmp[0:rows, 2, 0:LAT], ps[0:rows, bank:bank + LAT], rope[0:rows, 1, :],
                                  ALU.mult).then_inc(sem("v_s"), 1)
                dve.wait_ge(sem("v_c"), at.v("v_c", kp + 1))
                dve.wait_ge(sem("v_s"), at.v("v_s", kp + 1))
                dve.tensor_tensor(tmp[0:rows, 0, 0:LAT], tmp[0:rows, 1, 0:LAT], tmp[0:rows, 2, 0:LAT],
                                  ALU.add).then_inc(sem("v_full"), 1)
                dve.wait_ge(sem("v_full"), at.v("v_full", kv[1] + 1))
                dve.wait_ge(sem("v_hi"), at.v("v_hi", kv[0] + 1))
                dve.tensor_tensor(lo[r0:rows, 0:nt], tmp[r0:rows, 0, 0:nt], hi[r0:rows, 0:nt].bitcast(F32),
                                  ALU.subtract).then_inc(sem("v_lo"), 1)

            def attend(at, ka, nt, scale, home, fill=lambda n: None, first=False, last=False):
                c = Tiles(at, ka, nt // P, first)
                for n in range(c.steps(last)):
                    if n < c.nq:
                        w = TOK if n < 4 else CTX
                        s0 = SCORES[n % 2]
                        dve.wait_ge(sem("s_ready"), c.v("s_ready", n))
                        dve.tensor_reduce(mx[:, n:n + 1], ps[:, s0:s0 + w], AX.X, ALU.max).then_inc(
                            sem("s_max"), 1)
                        dve.wait_ge(sem("s_max"), c.v("s_max", n))
                        dve.tensor_scalar(nm[:, n:n + 1], mx[:, n:n + 1], scale(n), -1.0, ALU.mult,
                                          ALU.mult).then_inc(sem("s_nm"), 1)
                    m = n - 1
                    if c.has(m):
                        col = m % c.nq
                        dve.wait_ge(sem("s_exp"), c.v("s_exp", m))
                        dve.reciprocal(ri[:, col:col + 1], rs[:, col:col + 1]).then_inc(sem("s_rinv"), 1)
                    if n % 2 == 0:
                        if c.has(n - 3):
                            y_lo(c, n // 2 - 2, home)
                        fill(n)
                    m = n - 2
                    if c.has(m):
                        st = c.span(m)
                        cols = slice((m % 2) * P, (m % 2) * P + P)
                        dve.wait_ge(sem("t_hi"), c.v("t_hi", m))
                        dve.tensor_tensor(ptl[:, 0:st, cols],
                                          ps[:, TRANS:TRANS + st * P].rearrange("p (s q) -> p s q", q=P),
                                          pth[:, 0:st, cols].bitcast(F32), ALU.subtract).then_inc(sem("t_lo"), 1)
                    if n % 2:
                        fill(n)

            def y_lo(c, b, home):
                dve.wait_ge(sem("y_hi"), c.v("y_hi", b))
                col = 2 * P * (b % (c.nq // 2))
                cols = slice(col, col + 2 * P)
                dve.tensor_tensor(yl[:, bass.ds(home(b), 1), cols], ps[:, OUTS:OUTS + 2 * P].unsqueeze(1),
                                  yh[:, bass.ds(home(b), 1), cols].bitcast(F32),
                                  ALU.subtract).then_inc(sem("y_lo"), 1)

            def cosine(at, kv, rows):
                dve.tensor_tensor(tmp[0:rows, 1, 0:LAT], tmp[0:rows, 0, 0:LAT], rope[0:rows, 0, :],
                                  ALU.mult).then_inc(sem("v_c"), 1)

            def sine(at, kv, rows):
                dve.wait_ge(sem("v_perm"), at.v("v_perm", kv + 1))
                dve.tensor_tensor(tmp[0:rows, 2, 0:LAT], ps[0:rows, TURN:TURN + LAT], rope[0:rows, 1, :],
                                  ALU.mult).then_inc(sem("v_s"), 1)
                dve.wait_ge(sem("v_c"), at.v("v_c", kv + 1))
                dve.wait_ge(sem("v_s"), at.v("v_s", kv + 1))
                dve.tensor_tensor(tmp[0:rows, 0, 0:LAT], tmp[0:rows, 1, 0:LAT], tmp[0:rows, 2, 0:LAT],
                                  ALU.add).then_inc(sem("v_full"), 1)

            def query_lo(at, kv, par, rows, nt):
                dve.wait_ge(sem("v_full"), at.v("v_full", kv + 1))
                dve.wait_ge(sem("v_hi"), at.v("v_hi", kv + 1))
                dve.tensor_tensor(queries[par][1][0:rows, 0:nt], tmp[0:rows, 0, 0:nt],
                                  queries[par][0][0:rows, 0:nt].bitcast(F32), ALU.subtract).then_inc(
                    sem("v_lo"), 1)

            def mla_head(at, kp, par, nt):
                def fill(n):
                    if n == 0:
                        split(at, 2 * kp + 1)
                    if n == 1:
                        dve.wait_ge(sem("free0"), at.v("free0", 3 * kp + 1))
                        cosine(at, kp, MLA_QK)
                        sine(at, kp, MLA_QK)
                    if n == 2:
                        query_lo(at, kp, par, MLA_QK, nt)
                        plain(at, 2 * kp, 0, *keys[par], rows=MLA_NOPE)
                    if n == 3:
                        split(at, 2 * kp + 2)
                        plain(at, 2 * kp + 1, 0, vh[:, par, :], vl[:, par, :])
                return fill

            def gqa_query(at, kq, par, nt):
                nq = nt // P

                def fill(n):
                    if n == 0:
                        split(at, kq + 1)
                    if n == 1:
                        dve.wait_ge(sem("free0"), at.v("free0", kq + 1))
                        cosine(at, kq, P)
                    if n == 2:
                        sine(at, kq, P)
                    if n == 3:
                        dve.wait_ge(sem("v_std"), at.v("v_std", kq + 1))
                        dve.reciprocal(qsc[:, par, 0:nq], qsc[:, par, 0:nq]).then_inc(sem("v_rstd"), 1)
                        dve.wait_ge(sem("v_rstd"), at.v("v_rstd", kq + 1))
                        dve.tensor_scalar(qsc[:, par, 0:nq], qsc[:, par, 0:nq], GQA_HD ** -0.5, None,
                                          ALU.mult).then_inc(sem("v_norm"), 1)
                        dve.wait_ge(sem("v_norm"), at.v("v_norm", kq + 1))
                        query_lo(at, kq, par, P, nt)
                return fill

            def heads(ph):
                if ph["kind"].startswith("mla"):
                    return (lambda at, kp, par: mla_head(at, kp, par, ph["nt"])), lambda par: lambda n: MLA_QK ** -0.5
                return ((lambda at, kq, par: gqa_query(at, kq, par, ph["nt"])),
                        lambda par: lambda n: qsc[:, par, n:n + 1])

            def mod_add(at, km, layer, j):
                dve.wait_ge(sem("m_fold"), at.v("m_fold", km + 1))
                dve.tensor_tensor(mods[:, layer, bass.ds(j, 1), :], ps[:, FOLD[km % 2]:FOLD[km % 2] + 2].unsqueeze(1),
                                  bmod[:, layer, bass.ds(j, 1)].unsqueeze(2).to_broadcast([P, 1, 2]),
                                  ALU.add).then_inc(sem("m_add"), 1)

            dve.memset(ones[:, :], 1.0).then_inc(sem("ones_set"), 1)
            dve.memset(eps[:, :], EPS).then_inc(sem("eps_set"), 1)
            dve.wait_ge(sem("const_in"), 64)
            split(At(PHASES[0]), 0)
            x_loads = 1
            tabs = 0

            for ph in PHASES:
                kind, layer, at = ph["kind"], ph["layer"], At(ph)
                nt, turns = ph.get("nt"), ph["turns"]
                g0 = layer * G_LAYER
                if kind == "mod":
                    dve.wait_ge(sem("m_fold"), 1)
                    dve.tensor_tensor(mods[:, 0, 0:EARLY, :], ps[:, 0:2 * EARLY].rearrange("p (j u) -> p j u", u=2),
                                      bmod[:, 0, 0:EARLY].unsqueeze(2).to_broadcast([P, EARLY, 2]),
                                      ALU.add).then_inc(sem("m_add"), 1)

                elif kind == "mods":
                    dve.wait_ge(sem("m_add"), at.v("m_add"))
                    for n, j in enumerate(ph["gains"]):
                        dve.scalar_tensor_tensor(
                            out=gm[:, j, :, :], in0=mods[:, layer, (3 * j + 1) * KT:(3 * j + 2) * KT, :], scalar=1.0,
                            in1=gains[:, g0 + j * KT:g0 + (j + 1) * KT].unsqueeze(2).to_broadcast([P, KT, 2]),
                            op0=ALU.add, op1=ALU.mult).then_inc(sem("mod"), 1)
                        dve.wait_ge(sem("mod"), at.v("mod", n + 1))

                elif kind in ("squares", "summed"):
                    dve.wait_ge(sem("n_std"), at.v("n_std", 1))
                    dve.reciprocal(tmp[:, 2, 0:nt], tmp[:, 2, 0:nt]).then_inc(sem("n_rstd"), 1)
                    dve.wait_ge(sem("n_rstd"), at.v("n_rstd", 1))

                elif kind == "norm":
                    gi = 0 if ph["first"] else 1
                    for t in range(KT + 1):
                        if t < KT:
                            if t >= 2:
                                dve.wait_ge(sem("n_hi"), at.v("n_hi", t - 1))
                                dve.wait_ge(sem("n_full"), at.v("n_full", t - 1))
                            dve.tensor_tensor(tmp[:, t % 2, 0:nt], xz[:, t, 0:nt], tmp[:, 2, 0:nt],
                                              ALU.mult).then_inc(sem("n_t1"), 1)
                        m = t - 1
                        if m >= 0:
                            if m >= 2:
                                dve.wait_ge(sem("n_lo"), at.v("n_lo", m - 1))
                            dve.wait_ge(sem("n_t1"), at.v("n_t1", m + 1))
                            for u, (r0, r1) in enumerate(ranges(nt)):
                                ins = dve.tensor_scalar(prob[:, m % 2, r0:r1], tmp[:, m % 2, r0:r1],
                                                        gm[:, gi, m, u:u + 1],
                                                        mods[:, layer, 3 * gi * KT + m, u:u + 1], ALU.mult, ALU.add)
                            ins.then_inc(sem("n_full"), 1)

                elif kind == "mla_in":
                    for j, nt_j in enumerate((TOK if layer < DEPTH - 1 else LAT, TOK)):
                        for k in range(RKT):
                            split(at, 2 * j + k + 1)
                        rstd(at, j, nt_j)
                        for k in range(RKT):
                            col = g0 + 2 * KT + j * RKT + k
                            dve.scalar_tensor_tensor(out=tmp[:, k, 0:nt_j], in0=tmp[:, k, 0:nt_j],
                                                     scalar=gains[:, col:col + 1], in1=tmp[:, 2, 0:nt_j],
                                                     op0=ALU.mult, op1=ALU.mult).then_inc(sem("v_norm"), 1)
                        for k in range(RKT):
                            dve.wait_ge(sem("v_norm"), at.v("v_norm", 2 * j + k + 1))
                            dve.wait_ge(sem("v_hi"), at.v("v_hi", 2 * j + k + 1))
                            dve.tensor_tensor(ranks[:, j, 1, k, 0:nt_j], tmp[:, k, 0:nt_j],
                                              ranks[:, j, 0, k, 0:nt_j].bitcast(F32), ALU.subtract).then_inc(
                                sem("v_lo"), 1)
                    split(at, 5)
                    split(at, 6)
                    tabs += 1
                    dve.wait_ge(sem("tab_in"), 16 * tabs)
                    roped(at, (4, 0), 0, 0, 3, kh, kl, MLA_QK, MLA_NOPE, TOK)
                    rows = slice(MLA_NOPE, MLA_QK)
                    dve.wait_ge(sem("v_hi"), at.v("v_hi", 6))
                    dve.tensor_tensor(k2l[rows, :], tmp[rows, 0, :], k2h[rows, :].bitcast(F32),
                                      ALU.subtract).then_inc(sem("v_lo"), 1)

                elif kind in ("mla_first", "gqa_first"):
                    head, scale = heads(ph)
                    fill = head(at, 0, 0)
                    for n in range(4):
                        fill(n)
                    attend(at, 0, nt, scale(0), home(kind, 0), head(at, 1, 1), first=True)

                elif kind in ("mla", "gqa"):
                    head, scale = heads(ph)
                    with dve.Fori(0, turns) as i:
                        t = At(ph, i)
                        for k in range(2):
                            attend(t, k, nt, scale(1 - k), home(kind, i, k + 1), head(t, k, k))

                elif kind in ("mla_last", "gqa_last"):
                    attend(at, 0, nt, heads(ph)[1](1), home(kind, MLA_HEADS // 2 - 1, 1), last=True)

                elif kind == "gqa_in":
                    tabs += 1
                    dve.wait_ge(sem("tab_in"), 16 * tabs)
                    for j in range(GQA_KV):
                        split(at, 2 * j + 1)
                        split(at, 2 * j + 2)
                        rstd(at, j, TOK)
                        col = g0 + 2 * KT + 2 * RKT + 1
                        dve.scalar_tensor_tensor(out=tmp[:, 0, :], in0=tmp[:, 0, :], scalar=gains[:, col:col + 1],
                                                 in1=tmp[:, 2, :], op0=ALU.mult, op1=ALU.mult).then_inc(
                            sem("v_norm"), 1)
                        dve.wait_ge(sem("vt_hi"), at.v("vt_hi", j + 1))
                        dve.tensor_tensor(vl[:, j, :], pair(1)[:, :], vh[:, j, :].bitcast(F32),
                                          ALU.subtract).then_inc(sem("vt_lo"), 1)
                        dve.wait_ge(sem("v_norm"), at.v("v_norm", j + 1))
                        roped(at, (j, j), j, 0, j + 1, *keys[j], P, 0, TOK)

                elif kind == "merge":
                    with dve.Fori(0, turns) as i:
                        t = At(ph, i)
                        for k in range(2):
                            c = 2 * k
                            for r in range(2):
                                split(t, c + r + 1)
                            dve.wait_ge(sem("free0"), t.v("free0", k + 1))
                            dve.wait_ge(sem("product"), t.v("chunk", c + 2))
                            z = xz[:, bass.ds(2 * i + k, 1), 0:nt]
                            dve.tensor_tensor(z if ph["first"] else prob[:, k:k + 1, 0:nt],
                                              pair(1)[:, 0:nt].unsqueeze(1), tmp[:, k:k + 1, 0:nt],
                                              ALU.mult).then_inc(sem("free1"), 1)
                            if not ph["first"]:
                                dve.wait_ge(sem("free1"), t.v("free1", k + 1))
                                dve.tensor_tensor(z, z, prob[:, k:k + 1, 0:nt], ALU.add).then_inc(sem("mg_add"), 1)
                                dve.wait_ge(sem("mg_add"), t.v("mg_add", k + 1))
                            if ph["nmod"]:
                                mod_add(t, k, 0, 2 * i + (ph["j0"] + k))

                elif kind == "ret":
                    split(at, 1)

                    def turn(i, last=False):
                        t = At(ph, i)
                        for k in range(2, 4):
                            split(t, k)
                        dve.wait_ge(sem("vt_hi"), t.v("vt_hi", 1))
                        dve.tensor_tensor(vl_f[:, :], ps[:, 5 * BANK:8 * BANK], vh_f[:, :].bitcast(F32),
                                          ALU.subtract).then_inc(sem("vt_lo"), 1)
                        split(t, 4)
                        roped(t, (0, 0), 0, 0, 2, qh, ql, P, 0, nt, 4 * BANK)
                        split(t, 5)
                        roped(t, (1, 1), 1, 1, 2, kh, kl, P, 0, TOK, 4 * BANK)
                        split(t, 6)
                        units = 8 if nt > LAT else 6
                        dve.wait_ge(sem("dec_in"), t.v("dec", 1) * 16)
                        for u in range(units):
                            w = LAT if u < 6 else CTX
                            d0 = (3 * P - P * u if u < 4 else DEC1 + P - P * (u - 4) if u < 6
                                  else 3 * P - P * (u - 6))
                            dve.wait_ge(sem("rs_ready"), t.v("rs_ready", u + 1))
                            if u >= 3:
                                dve.wait_ge(sem("rs_lo"), t.v("rs_lo", u - 2))
                            dve.tensor_tensor(prob[:, u % 3, 0:w], ps[:, (4 + u % 3) * BANK:(4 + u % 3) * BANK + w],
                                              dec[:, d0:d0 + w], ALU.mult).then_inc(sem("rs_sd"), 1)
                        if not last:
                            split(t, 7)
                        for e in range(2):
                            dve.wait_ge(sem("y_sq"), t.v("y_sq", e + 1))
                            dve.tensor_tensor(prob[:, e, 0:nt], pair(e)[:, 0:nt], tmp[:, 1 + e, 0:nt],
                                              ALU.mult).then_inc(sem(f"free{e}"), 1)
                        dve.wait_ge(sem("v_std"), t.v("v_std", 1))
                        dve.reciprocal(prob[:, 2, 0:nt], prob[:, 2, 0:nt]).then_inc(sem("v_rstd"), 1)
                        dve.wait_ge(sem("v_rstd"), t.v("v_rstd", 1))
                        for e in range(2):
                            dve.wait_ge(sem(f"free{e}"), t.v(f"free{e}", 4))
                            dve.tensor_tensor(prob[:, e, 0:nt], prob[:, e, 0:nt], prob[:, 2, 0:nt],
                                              ALU.mult).then_inc(sem("v_full"), 1)
                        for e in range(2):
                            dve.wait_ge(sem("v_full"), t.v("v_full", 3 + e))
                            dve.wait_ge(sem("v_hi"), t.v("v_hi", 3 + e))
                            dve.tensor_tensor(yl[:, bass.ds(2 * i + e, 1), 0:nt], prob[:, e:e + 1, 0:nt],
                                              yh[:, bass.ds(2 * i + e, 1), 0:nt].bitcast(F32),
                                              ALU.subtract).then_inc(sem("v_lo"), 1)

                    with dve.Fori(0, turns - 1) as i:
                        turn(i)
                    turn(turns - 1, last=True)

                elif kind == "z":
                    for t in range(KT):
                        dve.wait_ge(sem("z_hi"), at.v("z_hi", t + 1))
                        dve.tensor_tensor(yl[:, t, 0:nt], xz[:, t, 0:nt], yh[:, t, 0:nt].bitcast(F32),
                                          ALU.subtract).then_inc(sem("z_lo"), 1)
                    x_loads += 1

                elif kind == "out":
                    dve.wait_ge(sem("m_add"), at.v("m_add"))
                    if ph["mod"] == 2:
                        dve.wait_ge(sem("x_in"), 16 * KT * x_loads)
                    for k in range(2):
                        dve.wait_ge(sem(f"free{k}"), at.v(f"free{k}"))

                    def turn(i, last=False):
                        t = At(ph, i)
                        for k in range(2):
                            if not (last and k == 1):
                                split(t, k + 1)
                            if ph["nmod"] == 2:
                                mod_add(t, 2 * k, ph["home"], 4 * i + (ph["j0"] + 2 * k))
                            dve.wait_ge(sem("product"), t.v("chunk", k + 1))
                            for u, (r0, r1) in enumerate(ranges(nt)):
                                m = ph["mod"] * KT + k
                                scalar = mods[:, layer, bass.ds(2 * i + m, 1), u:u + 1].rearrange("p a b -> p (a b)")
                                ins = dve.scalar_tensor_tensor(
                                    out=xz[:, bass.ds(2 * i + k, 1), r0:r1], in0=pair(k)[:, r0:r1].unsqueeze(1),
                                    scalar=scalar, in1=xz[:, bass.ds(2 * i + k, 1), r0:r1], op0=ALU.mult, op1=ALU.add)
                            ins.then_inc(sem(f"free{k}"), 1)
                            if ph["nmod"]:
                                km = (k + 1) * ph["nmod"] - 1
                                mod_add(t, km, ph["home"], 2 * ph["nmod"] * i + (ph["j0"] + km))
                    if at.v("chunk") + 2 * turns < NCHUNK:
                        with dve.Fori(0, turns) as i:
                            turn(i)
                    else:
                        with dve.Fori(0, turns - 1) as i:
                            turn(i)
                        turn(turns - 1, last=True)

                elif kind == "ffn":
                    with dve.Fori(0, turns) as i:
                        t = At(ph, i)
                        for k in range(2):
                            split(t, 2 * k + 1)
                            split(t, 2 * k + 2)
                            dve.wait_ge(sem("free0"), t.v("free0", k + 1))
                            dve.wait_ge(sem("product"), t.v("chunk", 2 * k + 2))
                            dve.wait_ge(sem("f_lo"), t.v("f_lo", k - 1))
                            dve.tensor_tensor(prob[:, k, 0:nt], pair(1)[:, 0:nt], tmp[:, k, 0:nt],
                                              ALU.mult).then_inc(sem("free1"), 1)

                elif kind == "final":
                    for t in range(KT):
                        dve.scalar_tensor_tensor(out=xz[:, t, 0:nt], in0=xz[:, t, 0:nt],
                                                 scalar=gains[:, G_FINAL + t:G_FINAL + t + 1],
                                                 in1=tmp[:, 2, 0:nt], op0=ALU.mult, op1=ALU.mult).then_inc(
                            sem("o_ready"), 1)

        @block.gpsimd
        def _(pool):
            def attend(at, ka, nt, first=False, last=False):
                c = Tiles(at, ka, nt // P, first)
                for n in range(c.nq + last):
                    m = n - 1
                    if c.has(m):
                        w = TOK if m % c.nq < 4 else CTX
                        col = m % c.nq
                        pool.wait_ge(sem("s_rinv"), c.v("s_rinv", m))
                        pool.tensor_tensor(prob[:, c.prob(m), 0:w], prob[:, c.prob(m), 0:w],
                                           ri[:, col:col + 1].to_broadcast([P, w]), ALU.mult).then_inc(
                            sem("s_pn"), 1)

            for k in range(2):
                pool.memset(mark[:, k:k + 1], 0.0).then_inc(sem("f_lo"), 1)
            pool.memset(mark[:, 2:3], 0.0).then_inc(sem("y_lo"), 1)
            pool.memset(mark[:, 3:4], 0.0).then_inc(sem("m_add"), 1)
            for ph in PHASES:
                kind, layer, at = ph["kind"], ph["layer"], At(ph)
                nt, turns = ph.get("nt"), ph["turns"]
                if kind == "zero":
                    pool.wait_ge(sem("product"), at.v("chunk"))
                    for h in range(2):
                        pool.memset(prob[:, 3, h * TOK // 2:(h + 1) * TOK // 2], 0.0).then_inc(sem("o_acc"), 1)
                elif kind == "out" and ph["sums"]:
                    with pool.Fori(0, turns) as i:
                        t = At(ph, i)
                        for k in range(2):
                            pool.wait_ge(sem("o_sq"), t.v("o_sq", k + 1))
                            pool.wait_ge(sem("o_acc"), t.v("o_acc", k))
                            pool.tensor_tensor(prob[:, 3, 0:nt], prob[:, 3, 0:nt], tmp[:, k, 0:nt],
                                               ALU.add).then_inc(sem("o_acc"), 1)
                elif kind == "norm":
                    for t in range(KT):
                        pool.wait_ge(sem("n_hi"), at.v("n_hi", t + 1))
                        pool.wait_ge(sem("n_full"), at.v("n_full", t + 1))
                        pool.tensor_tensor(hl[:, t, 0:nt], prob[:, t % 2, 0:nt], hh[:, t, 0:nt].bitcast(F32),
                                           ALU.subtract).then_inc(sem("n_lo"), 1)
                elif kind in ("mla_first", "gqa_first"):
                    attend(at, 0, nt, first=True)
                elif kind in ("mla", "gqa"):
                    with pool.Fori(0, turns) as i:
                        for k in range(2):
                            attend(At(ph, i), k, nt)
                elif kind in ("mla_last", "gqa_last"):
                    attend(at, 0, nt, last=True)
                elif kind == "ret":
                    units = 8 if nt > LAT else 6
                    with pool.Fori(0, turns) as i:
                        t = At(ph, i)
                        for u in range(units):
                            w = LAT if u < 6 else CTX
                            pool.wait_ge(sem("rs_hi"), t.v("rs_hi", u + 1))
                            cols = slice((u % 3) * LAT, (u % 3) * LAT + w)
                            pool.tensor_tensor(ptl_f[:, cols], prob[:, u % 3, 0:w], pth_f[:, cols].bitcast(F32),
                                               ALU.subtract).then_inc(sem("rs_lo"), 1)
                elif kind == "ffn":
                    with pool.Fori(0, turns) as i:
                        t = At(ph, i)
                        for k in range(2):
                            pool.wait_ge(sem("f_hi"), t.v("f_hi", k + 1))
                            pool.tensor_tensor(yl[:, bass.ds(2 * i + k, 1), 0:nt], prob[:, k:k + 1, 0:nt],
                                               yh[:, bass.ds(2 * i + k, 1), 0:nt].bitcast(F32), ALU.subtract).then_inc(
                                sem("f_lo"), 1)

        @block.tensor
        def _(pe):
            def three(outs, lhs, rhs, start, stop):
                for n, (w, x) in enumerate(((0, 0), (0, 1), (1, 0))):
                    for out, cols in outs:
                        ins = pe.matmul(out, lhs[w], rhs[x](cols), start=start and n == 0, stop=stop and n == 2)
                return ins

            def project(at, kc, slot, kfree, mov, kts, nt, cut, rows=P, kt0=0, ktn=None, done=True, piece=False, late={}):
                s = at.slot(kc)
                if kfree is not None and (at.base.get(f"free{slot}", 0) + kfree > 0 or not isinstance(at.i, int)):
                    pe.wait_ge(sem(f"free{slot}"), at.v(f"free{slot}", kfree))
                pe.wait_ge(sem("w_lo"), at.v("chunk", kc + 1))
                for kt in range(kts):
                    g = kt0 + kt
                    if g in late:
                        pe.wait_ge(sem(late[g][0]), late[g][1])
                    outs = [(pair(slot)[0:rows, r0:r1], (r0, r1)) for r0, r1 in ranges(nt)]
                    ins = three(outs, [w[:, s, cut(kt if piece else g)] for w in (wh, wl)],
                                [lambda c, x=x: x(g, c) for x in mov], g == 0, g == (ktn or kts) - 1)
                if done:
                    ins.then_inc(sem("product"), 1)
                return ins

            H = [lambda k, c, x=x: x[:, k, c[0]:c[1]] for x in (hh, hl)]
            Y = [lambda k, c, x=x: x[:, k, c[0]:c[1]] for x in (yh, yl)]
            R = [[lambda k, c, j=j, x=x: ranks[:, j, x, k, c[0]:c[1]] for x in range(2)] for j in range(2)]
            whole = lambda kt: slice(kt * P, (kt + 1) * P)

            def normed(at):
                return {kt: ("n_lo", at.v("n_lo", kt + 1 - KT)) for kt in range(KT)}

            def stats(at, src, slots, nt, k):
                for n, x in enumerate(slots):
                    for r0, r1 in ranges(nt):
                        ins = pe.matmul(pair(AUX)[:, r0:r1], ones[:, :], src[:, x, r0:r1], start=n == 0,
                                        stop=n == len(slots) - 1)
                ins.then_inc(sem("v_stat"), 1)

            def rotate(which, rows, bank=6 * BANK):
                pe.matmul(ps[0:rows, bank:bank + LAT], perm[0:rows, which, 0:rows], tmp[0:rows, 0, 0:LAT],
                          start=True, stop=True).then_inc(sem("v_perm"), 1)

            def attend(at, ka, par, nt, rows, fill=lambda n: None, first=False, last=False):
                c = Tiles(at, ka, nt // P, first)
                for n in range(c.steps(last)):
                    if n < c.nq:
                        if c.has(n - 2):
                            pe.wait_ge(sem("s_exp"), c.v("s_exp", n - 2))
                        s0 = SCORES[n % 2]
                        spans = [(s0, (0, LAT)), (s0 + LAT, (LAT, TOK))] if n < 4 else [(s0, (LAT, TOK))]
                        outs = [(ps[:, o:o + x[1] - x[0]], x) for o, x in spans]
                        three(outs, [q[0:rows, n * P:(n + 1) * P] for q in queries[par]],
                              [lambda x, k=k: k[0:rows, x[0]:x[1]] for k in keys[par]], True, True).then_inc(
                            sem("s_ready"), 1)
                    if n % 2 == 0:
                        if c.has(n - 3):
                            values(c, n - 3, par if n >= 3 else 1 - par)
                        fill(n)
                    m = n - 2
                    if c.has(m):
                        pe.wait_ge(sem("s_pn"), c.v("s_pn", m))
                        if c.has(m - 1):
                            pe.wait_ge(sem("t_lo"), c.v("t_lo", m - 1))
                        if m % 2 == 0:
                            pe.wait_ge(sem("y_lo"), c.v("y_lo", m // 2 - 1))
                        for s in range(c.span(m)):
                            ins = pe.transpose(ps[:, TRANS + s * P:TRANS + (s + 1) * P],
                                               prob[:, c.prob(m), s * P:(s + 1) * P], ident[:, :])
                        ins.then_inc(sem("t_ready"), 1)
                    if n % 2:
                        fill(n)

            def values(c, m, vpar):
                st = c.span(m)
                v0 = 6 - st
                pe.wait_ge(sem("t_lo"), c.v("t_lo", m))
                for s in range(st):
                    ins = three([(ps[:, OUTS:OUTS + 2 * P], None)],
                                [v[:, vpar, (v0 + s) * P:(v0 + s + 1) * P] for v in (vh, vl)],
                                [lambda c, x=x: x[:, s, :] for x in (pth, ptl)], s == 0, s == st - 1)
                ins.then_inc(sem("y_ready"), 1)

            def mod_row(at, km):
                pe.wait_ge(sem("m_in"), at.v("m_in", km + 1) * 16)
                for kt in range(KT):
                    ins = pe.matmul(ps[0:2, ROW:ROW + P], csil[:, kt, :], mraw[:, whole(kt)], start=kt == 0,
                                    stop=kt == KT - 1)
                ins.then_inc(sem("m_prod"), 1)

            def mod_fold(at, km):
                pe.wait_ge(sem("m_row"), at.v("m_row", km + 1))
                pe.wait_ge(sem("m_add"), at.v("m_add", km - 1))
                pe.matmul(ps[:, FOLD[km % 2]:FOLD[km % 2] + 2], tmp[0:2, 2, (km % 2) * P:(km % 2 + 1) * P],
                          ident[0:2, 0:2], start=True, stop=True).then_inc(sem("m_fold"), 1)

            def mla_head(at, kp, nt):
                c0 = 2 * kp

                def fill(n):
                    s = at.slot(c0 + 1)
                    if n == 0:
                        project(at, c0, 0, 3 * kp, R[0], RKT, nt,
                                lambda kt: slice(kt * P, kt * P + MLA_QK), rows=MLA_QK)
                    if n == 1:
                        pe.wait_ge(sem("free0"), at.v("free0", 3 * kp + 1))
                        rotate(1, MLA_QK, TURN)
                    if n == 2:
                        pe.wait_ge(sem("v_s"), at.v("v_s", kp + 1))
                        pe.wait_ge(sem("w_lo"), at.v("chunk", c0 + 2))
                        for kt in range(RKT):
                            ins = three([(pair(0)[0:MLA_NOPE, r0:r1], (r0, r1)) for r0, r1 in ranges(TOK)],
                                        [w[:, s, kt * 256:kt * 256 + MLA_NOPE] for w in (wh, wl)],
                                        [lambda c, x=x: x(kt, c) for x in R[1]], kt == 0, kt == RKT - 1)
                        ins.then_inc(sem("k_ready"), 1)
                    if n == 3:
                        pe.wait_ge(sem("free0"), at.v("free0", 3 * kp + 2))
                        for tt in range(TOK // P):
                            for kt in range(RKT):
                                ins = three([(pair(0)[:, tt * P:(tt + 1) * P], None)],
                                            [x(kt, (tt * P, (tt + 1) * P)) for x in R[1]],
                                            [lambda c, w=w: w[:, s, kt * 256 + 64:kt * 256 + 192] for w in (wh, wl)],
                                            kt == 0, kt == RKT - 1)
                        ins.then_inc(sem("product"), 1)
                return fill

            def gqa_query(at, kq, nt):
                def fill(n):
                    if n < 2:
                        project(at, kq, 0, kq if n == 0 else None, H, KT // 2, nt, whole, kt0=n * KT // 2,
                                ktn=KT, done=n == 1)
                    if n == 2:
                        pe.wait_ge(sem("free0"), at.v("free0", kq + 1))
                        for j in range(nt // P):
                            ins = pe.matmul(ps[:, QSUM + j:QSUM + j + 1], tmp[:, 2, j * P:(j + 1) * P],
                                            ones[:, 0:1], start=True, stop=True)
                        ins.then_inc(sem("v_stat"), 1)
                        rotate(0, P, TURN)
                    if n == 3:
                        pe.wait_ge(sem("v_s"), at.v("v_s", kq + 1))
                return fill

            def heads(ph):
                if ph["kind"].startswith("mla"):
                    return (lambda at, kp: mla_head(at, kp, ph["nt"])), MLA_QK
                return (lambda at, kq: gqa_query(at, kq, ph["nt"])), P

            pe.wait_ge(sem("c_silu"), 1)
            pe.wait_ge(sem("const_in"), 64)
            pe.wait_ge(sem("ones_set"), 1)

            for ph in PHASES:
                kind, layer, at = ph["kind"], ph["layer"], At(ph)
                nt, turns = ph.get("nt"), ph["turns"]
                if kind == "mod":
                    for g in range(EARLY // 4):
                        pe.wait_ge(sem(f"early{g}"), 64)
                        for j in range(4 * g, 4 * g + 4):
                            for kt in range(KT):
                                ins = pe.matmul(ps[0:2, 4 * BANK + j * P:4 * BANK + (j + 1) * P], csil[:, kt, :],
                                                early[:, j, whole(kt)], start=kt == 0, stop=kt == KT - 1)
                        ins.then_inc(sem("m_prod"), 1)
                    pe.wait_ge(sem("m_row"), EARLY // 4)
                    for j in range(EARLY):
                        ins = pe.matmul(ps[:, 2 * j:2 * j + 2], prob_f[0:2, j * P:(j + 1) * P], ident[0:2, 0:2],
                                        start=True, stop=True)
                    ins.then_inc(sem("m_fold"), 1)

                elif kind == "squares":
                    for t in range(KT):
                        pe.wait_ge(sem("sq"), at.v("sq", t + 1))
                        for r0, r1 in ranges(nt):
                            ins = pe.matmul(pair(AUX)[:, r0:r1], ones[:, :], tmp[:, t % 2, r0:r1], start=t == 0,
                                            stop=t == KT - 1)
                        ins.then_inc(sem("sq_used"), 1)
                    pe.wait_ge(sem("n_std"), at.v("n_std", 1))

                elif kind == "summed":
                    pe.wait_ge(sem("o_acc"), at.v("o_acc"))
                    for r0, r1 in ranges(nt):
                        ins = pe.matmul(pair(AUX)[:, r0:r1], ones[:, :], prob[:, 3, r0:r1], start=True, stop=True)
                    ins.then_inc(sem("sq_used"), 1)

                elif kind == "mla_in":
                    for j, nt_j in enumerate((TOK if layer < DEPTH - 1 else LAT, TOK)):
                        for k in range(RKT):
                            project(at, 2 * j + k, k, j, H, KT, nt_j, whole, late=normed(at))
                        for k in range(RKT):
                            pe.wait_ge(sem(f"free{k}"), at.v(f"free{k}", j + 1))
                        stats(at, prob, (0, 1), nt_j, j)
                    cut = lambda kt: slice(kt * P, kt * P + MLA_QK)
                    project(at, 4, 0, 2, H, KT // 2, TOK, cut, rows=MLA_QK, ktn=KT, piece=True)
                    project(at, 5, 0, None, H, KT // 2, TOK, cut, rows=MLA_QK, kt0=KT // 2, ktn=KT, piece=True)
                    pe.wait_ge(sem("free0"), at.v("free0", 3))
                    rotate(1, MLA_QK)

                elif kind in ("mla_first", "gqa_first"):
                    head, rows = heads(ph)
                    pe.wait_ge(sem("v_lo"), at.v("v_lo"))
                    fill = head(at, 0)
                    for n in range(4):
                        fill(n)
                    pe.wait_ge(sem("v_lo"), at.v("v_lo", 1))
                    attend(at, 0, 0, nt, rows, head(at, 1), first=True)

                elif kind in ("mla", "gqa"):
                    head, rows = heads(ph)
                    with pe.Fori(0, turns) as i:
                        t = At(ph, i)
                        for k in range(2):
                            pe.wait_ge(sem("v_lo"), t.v("v_lo", k))
                            attend(t, k, 1 - k, nt, rows, head(t, k))

                elif kind in ("mla_last", "gqa_last"):
                    pe.wait_ge(sem("v_lo"), at.v("v_lo"))
                    pe.wait_ge(sem("free0"), at.v("free0"))
                    attend(at, 0, 1, nt, heads(ph)[1], last=True)

                elif kind == "gqa_in":
                    pe.wait_ge(sem("m_add"), at.v("m_add"))
                    for j in range(GQA_KV):
                        project(at, 2 * j, 0, j, H, KT, TOK, whole)
                        if j:
                            pe.wait_ge(sem("v_norm"), at.v("v_norm", j))
                            rotate(0, P)
                            pe.wait_ge(sem("vt_lo"), at.v("vt_lo", j))
                        project(at, 2 * j + 1, 1, j, H, KT, TOK, whole)
                        pe.wait_ge(sem("free0"), at.v("free0", j + 1))
                        stats(at, tmp, (1,), TOK, j)
                        pe.wait_ge(sem("free1"), at.v("free1", j + 1))
                        for tt in range(TOK // P):
                            ins = pe.transpose(pair(1)[:, tt * P:(tt + 1) * P], prob[:, 0, tt * P:(tt + 1) * P],
                                               ident[:, :])
                        ins.then_inc(sem("vt"), 1)
                    pe.wait_ge(sem("v_norm"), at.v("v_norm", GQA_KV))
                    rotate(0, P)

                elif kind == "merge":
                    with pe.Fori(0, turns) as i:
                        t = At(ph, i)
                        for k in range(2):
                            project(t, 2 * k, 0, k, H, KT, nt, whole)
                            if ph["nmod"]:
                                mod_row(t, k)
                            pe.wait_ge(sem("v_lo"), at.v("v_lo"))
                            pe.wait_ge(sem("y_lo"), at.v("y_lo"))
                            project(t, 2 * k + 1, 1, k, Y, KT, nt, whole)
                            if ph["nmod"]:
                                mod_fold(t, k)

                elif kind == "ret":
                    units = 8 if nt > LAT else 6
                    with pe.Fori(0, turns) as i:
                        t = At(ph, i)
                        for e in range(2):
                            project(t, e, e, 0, H, KT, TOK, whole)
                        project(t, 2, 0, 1, H, KT, nt, whole)
                        pe.wait_ge(sem("v_std"), t.v("v_std"))
                        pe.wait_ge(sem("v_lo"), t.v("v_lo"))
                        pe.wait_ge(sem("free1"), t.v("free1", 1))
                        for tt in range(TOK // P):
                            for e in range(2):
                                c0 = 5 * BANK + (2 * tt + e) * P
                                ins = pe.transpose(ps[:, c0:c0 + P], prob[:, e, tt * P:(tt + 1) * P], ident[:, :])
                        ins.then_inc(sem("vt"), 1)
                        project(t, 3, 1, 1, H, KT, TOK, whole)
                        pe.wait_ge(sem("free0"), t.v("free0", 2))
                        rotate(0, P, 4 * BANK)
                        project(t, 4, 0, 2, H, KT, nt, whole)
                        pe.wait_ge(sem("free1"), t.v("free1", 2))
                        pe.wait_ge(sem("v_s"), t.v("v_s", 1))
                        rotate(0, P, 4 * BANK)
                        project(t, 5, 1, 2, H, KT, nt, whole)
                        pe.wait_ge(sem("v_lo"), t.v("v_lo", 2))
                        for e in range(2):
                            pe.wait_ge(sem(f"free{e}"), t.v(f"free{e}", 3))

                        def span(u):
                            return (0, LAT) if u < 6 else (LAT, TOK)

                        def score(u):
                            if u >= 3:
                                pe.wait_ge(sem("rs_sd"), t.v("rs_sd", u - 2))
                            tile = u if u < 6 else u - 2
                            r0, r1 = span(u)
                            three([(ps[:, (4 + u % 3) * BANK:(4 + u % 3) * BANK + r1 - r0], (r0, r1))],
                                  [x[:, tile * P:(tile + 1) * P] for x in (kh, kl)],
                                  [lambda c, x=x: x[:, c[0]:c[1]] for x in (qh, ql)], True, True).then_inc(
                                sem("rs_ready"), 1)

                        score(0)
                        score(1)
                        for u in range(units):
                            if u + 2 < units:
                                score(u + 2)
                            pe.wait_ge(sem("rs_lo"), t.v("rs_lo", u + 1))
                            tile = u if u < 6 else u - 2
                            r0, r1 = span(u)
                            for e in range(2):
                                ins = three([(pair(e)[:, r0:r1], None)],
                                            [v[:, tile * 2 * P + e * P:tile * 2 * P + (e + 1) * P] for v in (vh_f, vl_f)],
                                            [lambda c, x=x: x[:, (u % 3) * LAT:(u % 3) * LAT + r1 - r0]
                                             for x in (pth_f, ptl_f)], u in (0, 6), u in (5, 7))
                            ins.then_inc(sem("rs_used"), 1)
                        pe.wait_ge(sem("y_sq"), t.v("y_sq", 2))
                        for r0, r1 in ranges(nt):
                            for e, x in enumerate((tmp[:, 0, r0:r1], prob[:, 2, r0:r1])):
                                ins = pe.matmul(pair(AUX)[:, r0:r1], ones[:, :], x, start=e == 0, stop=e == 1)
                        ins.then_inc(sem("v_stat"), 1)

                elif kind == "out":
                    name, kts = ("z_lo" if ph["mod"] == 2 else "f_lo"), ph["kt"]
                    pe.wait_ge(sem(name), at.v(name, 1 - kts))
                    late = {kt: (name, at.v(name, kt + 1 - kts)) for kt in range(1, kts)}
                    with pe.Fori(0, turns) as i:
                        t = At(ph, i)
                        for k in range(2):
                            for r in range(2):
                                project(t, k, k, None if r else 0, Y, kts // 2, nt, whole, kt0=r * kts // 2, ktn=kts,
                                        done=r == 1, late=late)
                                if ph["nmod"] == 2:
                                    if k + r:
                                        mod_fold(t, 2 * k + r - 1)
                                    mod_row(t, 2 * k + r)
                                elif ph["nmod"] and r == 0:
                                    mod_row(t, k)
                            if ph["nmod"] == 1:
                                mod_fold(t, k)
                        if ph["nmod"] == 2:
                            mod_fold(t, 3)

                elif kind == "ffn":
                    with pe.Fori(0, turns) as i:
                        t = At(ph, i)
                        for k in range(2):
                            for j in range(2):
                                project(t, 2 * k + j, j, k, H, KT, nt, whole, late=normed(at))


def rope_table(dim, lead):
    half = dim // 4
    inv = (ROPE_BASE ** (-np.arange(half) / half)).astype(np.float32)
    tok = np.arange(LAT)
    c, s = np.ones((P, LAT)), np.zeros((P, LAT))
    for part, pos in enumerate((tok // GRID_W, tok % GRID_W)):
        ang = (inv[:, None] * pos[None, :].astype(np.float32)).astype(np.float64)
        for h in range(2):
            rows = slice(lead + (2 * part + h) * half, lead + (2 * part + h + 1) * half)
            c[rows], s[rows] = np.cos(ang), np.sin(ang)
    return np.stack([c, s], 1).astype(np.float32)


def perm_table(dim, lead):
    half = dim // 4
    m = np.zeros((P, P), np.float32)
    for part in range(2):
        for r in range(half):
            lo, hi = lead + 2 * part * half + r, lead + (2 * part + 1) * half + r
            m[hi, lo], m[lo, hi] = -1.0, 1.0
    return m


def decay_table():
    out = np.zeros((RET_HEADS, P, DEC), np.float64)
    p = np.arange(P)[:, None]
    for h in range(RET_HEADS):
        f, b = (np.log1p(-np.exp2(-(5.0 + off) - h)) for off in (0.0, 0.5))
        d = np.arange(DEC1)[None, :] - 3 * P - p
        out[h, :, :DEC1] = np.exp(f * np.maximum(d, 0)) * (d >= 0) + np.exp(b * np.maximum(-d, 0)) * (d <= 0)
        d = np.arange(DEC2)[None, :] - P - p
        out[h, :, DEC1:] = np.exp(f * (CTX + d)) + np.exp(b * (LAT - d))
    return out.astype(np.float32)


def stream_of(w):
    out = np.zeros((NCHUNK, P, CH), np.float32)
    n = 0

    def put(m, at=0, step=P):
        nonlocal n
        kt, cols = m.shape[0] // P, m.shape[1]
        out[n].reshape(P, CH // step, step)[:, :kt, at:at + cols] = m.reshape(kt, P, cols).transpose(1, 0, 2)
        n += 1

    for layer in range(DEPTH):
        win = w["w_in"][layer]
        col = lambda o, k=0, c=P: win[:, o + k * P:o + k * P + c]
        for o in (O_CQ, O_CKV):
            for k in range(RKT):
                put(col(o, k))
        for k in range(2):
            put(col(O_KR, 0, MLA_ROPE)[k * D // 2:(k + 1) * D // 2], at=MLA_NOPE)
        for h in range(MLA_HEADS):
            step = MLA_NOPE + MLA_V
            put(w["w_mla_qb"][layer][:, h * MLA_QK:(h + 1) * MLA_QK])
            put(w["w_mla_kvb"][layer][:, h * step:(h + 1) * step], step=256)

        def merge(branch, name):
            for m in range(KT):
                put(col(O_GATE + branch * D, m))
                put(w[name][layer][:, m * P:(m + 1) * P])

        merge(1, "w_mla_o")
        for kv in range(GQA_KV):
            put(col(O_GK, kv))
            put(col(O_GV, kv))
        for h in range(GQA_HEADS // GQA_KV):
            for kv in range(GQA_KV):
                put(col(O_GQ, kv * (GQA_HEADS // GQA_KV) + h))
        merge(2, "w_gqa_o")
        for h in range(RET_HEADS):
            for e in range(2):
                put(col(O_RV, 2 * h + e))
            put(col(O_RQ, h))
            put(col(O_RK, h))
            for e in range(2):
                put(col(O_RG, 2 * h + e))
        merge(0, "w_ret_o")
        for m in range(KT):
            put(w["w_out"][layer][:, m * P:(m + 1) * P])
        for g, (t0, tiles) in enumerate(GROUPS):
            for t in range(t0, t0 + tiles):
                for half in range(2):
                    put(w["w_ffn_in"][layer][:, half * FFN + t * P:half * FFN + (t + 1) * P])
            for m in range(KT):
                put(w["w_ffn_out"][layer][t0 * P:(t0 + tiles) * P, m * P:(m + 1) * P])
    assert n == NCHUNK
    return out


def kernel(**inputs):
    import concourse.bacc as bacc
    from concourse.bass_utils import run_bass_kernel_spmd as run

    w = {name: np.asarray(x) for name, x in inputs.items()}

    def tiles(v):
        return v.reshape(-1, P).T

    gains = [tiles(w[name][layer]) for layer in range(DEPTH)
             for name in ("g_mix", "g_ffn", "g_mla_q", "g_mla_kv", "g_gqa_q", "g_gqa_k")] + [tiles(w["g_final"])]
    arrays = {
        "xT": np.ascontiguousarray(np.concatenate([w["x"][0], w["ctx"][0]], 0).T),
        "cvec": np.ascontiguousarray(np.stack([tiles(w["c"][0]), tiles(w["c_ctx"])], 2)),
        "bmod": np.ascontiguousarray(np.stack([tiles(b) for b in w["b_mod"]], 1)),
        "gains": np.ascontiguousarray(np.concatenate(gains, 1)),
        "stream": stream_of(w),
        "rope": np.stack([rope_table(RET_DK, 0), rope_table(MLA_ROPE, MLA_NOPE)]),
        "perm": np.ascontiguousarray(np.stack([perm_table(RET_DK, 0), perm_table(MLA_ROPE, MLA_NOPE)], 1)),
        "ident": np.eye(P, dtype=np.float32),
        "dec": decay_table(),
        "wmod": np.ascontiguousarray(w["w_mod"].reshape(DEPTH, KT, P, N_MOD * KT, P).transpose(
            0, 3, 2, 1, 4).reshape(DEPTH * N_MOD * KT, P, CH)),
    }
    nc = bacc.Bacc("TRN2", target_bir_lowering=False, num_devices=1, dynamic_dma_scratch_size=1024)
    a = {name: nc.dram_tensor(f"in_{name}", x.shape, mybir.dt.from_np(x.dtype), kind="ExternalInput").ap()
         for name, x in arrays.items()}
    a["out"] = nc.dram_tensor("out", (D, LAT), F32, kind="ExternalOutput").ap()
    build(nc, a)
    r = run(nc, [{f"in_{name}": x for name, x in arrays.items()}], core_ids=[0])
    return np.ascontiguousarray(r.results[0]["out"].T)[None]
```
